# Optimizing a Trainium2 kernel written in Bass

```python
import jax, jax.numpy as jnp
from jax import lax
import numpy as np

D_MODEL = 2048
BATCH = 1
SEQ = 1024
DEPTH = 1

CHUNK = 64
N_MEM = 256
EPS = 1e-6
ROPE_THETA = 10000.0

A_HEADS = 16
A_KV_HEADS = 2
A_GROUP = A_HEADS // A_KV_HEADS
A_HEAD_DIM = 64
A_WINDOW = 128
A_WIN_CHUNKS = A_WINDOW // CHUNK
A_WIDTH = A_HEADS * A_HEAD_DIM

B_HEADS = 4
B_NOPE = 128
B_ROPE = 64
B_V = 128
B_Q_RANK = 512
B_KV_RANK = 256
B_WIDTH = B_HEADS * B_V
Q_BLOCK = 128

M_HEADS = 4
M_HEAD_DIM = 128
M_WIDTH = M_HEADS * M_HEAD_DIM

MIX_WIDTH = A_WIDTH + B_WIDTH + M_WIDTH

IN_SPLITS = (A_WIDTH, A_KV_HEADS * A_HEAD_DIM, A_KV_HEADS * A_HEAD_DIM, A_WIDTH,
             B_Q_RANK, B_KV_RANK, B_ROPE, B_WIDTH,
             M_WIDTH, M_WIDTH)
IN_WIDTH = sum(IN_SPLITS)

kernel_name = 'hybrid_swa_mla_memxattn_gated_layer'

def rms_norm(x, g):
    xf = x.astype(jnp.float32)
    y = xf * lax.rsqrt(jnp.mean(xf * xf, axis=-1, keepdims=True) + EPS)
    return (y * g.astype(jnp.float32)).astype(x.dtype)

def rope(x, positions):
    d = x.shape[-1]
    inv_freq = ROPE_THETA ** (-jnp.arange(0, d, 2, dtype=jnp.float32) / d)
    ang = positions.astype(jnp.float32)[..., None] * inv_freq
    cos = jnp.cos(ang)[:, :, None, :]
    sin = jnp.sin(ang)[:, :, None, :]
    xf = x.astype(jnp.float32)
    x1, x2 = xf[..., :d // 2], xf[..., d // 2:]
    return jnp.concatenate([x1 * cos - x2 * sin, x2 * cos + x1 * sin], axis=-1).astype(x.dtype)

def swa_sink_attention(q, k, v, sinks):
    b, s = q.shape[0], q.shape[1]
    nc = s // CHUNK
    w = A_WIN_CHUNKS
    qc = q.reshape(b, nc, CHUNK, A_KV_HEADS, A_GROUP, A_HEAD_DIM)
    pad = ((0, 0), ((w - 1) * CHUNK, 0), (0, 0), (0, 0))
    kc = jnp.pad(k, pad).reshape(b, nc + w - 1, CHUNK, A_KV_HEADS, A_HEAD_DIM)
    vc = jnp.pad(v, pad).reshape(b, nc + w - 1, CHUNK, A_KV_HEADS, A_HEAD_DIM)
    kb = jnp.concatenate([kc[:, j:j + nc] for j in range(w)], axis=2)
    vb = jnp.concatenate([vc[:, j:j + nc] for j in range(w)], axis=2)
    scores = jnp.einsum('bcqkgd,bcjkd->bckgqj', qc, kb).astype(jnp.float32) * (A_HEAD_DIM ** -0.5)
    key_chunk = jnp.arange(nc)[:, None] - (w - 1) + jnp.arange(w * CHUNK)[None, :] // CHUNK
    valid = (key_chunk >= 0)[None, :, None, None, None, :]
    scores = jnp.where(valid, scores, -jnp.inf)
    sink = sinks.astype(jnp.float32).reshape(1, 1, A_KV_HEADS, A_GROUP, 1, 1)
    m = jnp.maximum(jnp.max(scores, axis=-1, keepdims=True), sink)
    p = jnp.exp(scores - m)
    p = p / (jnp.sum(p, axis=-1, keepdims=True) + jnp.exp(sink - m))
    o = jnp.einsum('bckgqj,bcjkd->bcqkgd', p.astype(v.dtype), vb)
    return o.reshape(b, s, A_WIDTH)

def mla_attention(q_nope, q_rope, k_nope, k_rope, v):
    b, s = q_nope.shape[0], q_nope.shape[1]
    nb = s // Q_BLOCK
    scale = (B_NOPE + B_ROPE) ** -0.5
    k_chunk = jnp.arange(s) // CHUNK

    def to_blocks(t):
        return jnp.moveaxis(t.reshape((b, nb, Q_BLOCK) + t.shape[2:]), 1, 0)

    def block(args):
        qn, qr, i = args
        sc = (jnp.einsum('bqhd,bkhd->bhqk', qn, k_nope)
              + jnp.einsum('bqhd,bkd->bhqk', qr, k_rope)).astype(jnp.float32) * scale
        q_chunk = (i * Q_BLOCK + jnp.arange(Q_BLOCK)) // CHUNK
        mask = k_chunk[None, :] <= q_chunk[:, None]
        p = jax.nn.softmax(jnp.where(mask, sc, -jnp.inf), axis=-1)
        return jnp.einsum('bhqk,bkhd->bqhd', p.astype(v.dtype), v)

    o = lax.map(block, (to_blocks(q_nope), to_blocks(q_rope), jnp.arange(nb)))
    return jnp.moveaxis(o, 0, 1).reshape(b, s, B_WIDTH)

def memory_cross_attention(q, k, v):
    b, s = q.shape[0], q.shape[1]
    sc = jnp.einsum('bshd,bnhd->bhsn', q, k).astype(jnp.float32) * (M_HEAD_DIM ** -0.5)
    p = jax.nn.softmax(sc, axis=-1)
    o = jnp.einsum('bhsn,bnhd->bshd', p.astype(v.dtype), v)
    return o.reshape(b, s, M_WIDTH)

def hybrid_layer(x, mem, positions, g_in, w_in, a_g_q, a_g_k, a_sinks,
                 b_g_cq, b_w_q_up, b_g_ckv, b_w_kv_up, b_g_q_nope, b_g_q_rope,
                 b_g_k_nope, b_g_k_rope, m_g_mem, m_w_kv, m_g_q, m_g_k, w_o):
    b, s, _ = x.shape
    h = rms_norm(x, g_in)
    proj = h @ w_in
    points = [int(p) for p in np.cumsum(IN_SPLITS)[:-1]]
    (a_q, a_k, a_v, a_gate, b_cq, b_ckv, b_kr, b_gate, m_q, m_gate) = jnp.split(proj, points, axis=-1)

    qa = rope(rms_norm(a_q.reshape(b, s, A_HEADS, A_HEAD_DIM), a_g_q), positions)
    ka = rope(rms_norm(a_k.reshape(b, s, A_KV_HEADS, A_HEAD_DIM), a_g_k), positions)
    va = a_v.reshape(b, s, A_KV_HEADS, A_HEAD_DIM)
    out_a = swa_sink_attention(qa, ka, va, a_sinks) * jax.nn.silu(a_gate)

    qb = (rms_norm(b_cq, b_g_cq) @ b_w_q_up).reshape(b, s, B_HEADS, B_NOPE + B_ROPE)
    qb_nope = rms_norm(qb[..., :B_NOPE], b_g_q_nope)
    qb_rope = rope(rms_norm(qb[..., B_NOPE:], b_g_q_rope), positions)
    kvb = (rms_norm(b_ckv, b_g_ckv) @ b_w_kv_up).reshape(b, s, B_HEADS, B_NOPE + B_V)
    kb_nope = rms_norm(kvb[..., :B_NOPE], b_g_k_nope)
    vb = kvb[..., B_NOPE:]
    kb_rope = rope(rms_norm(b_kr, b_g_k_rope)[:, :, None, :], positions)[:, :, 0, :]
    out_b = mla_attention(qb_nope, qb_rope, kb_nope, kb_rope, vb) * jax.nn.silu(b_gate)

    n_mem = mem.shape[1]
    kvm = (rms_norm(mem, m_g_mem) @ m_w_kv).reshape(b, n_mem, 2, M_HEADS, M_HEAD_DIM)
    km = rms_norm(kvm[:, :, 0], m_g_k)
    vm = kvm[:, :, 1]
    qm = rms_norm(m_q.reshape(b, s, M_HEADS, M_HEAD_DIM), m_g_q)
    out_m = memory_cross_attention(qm, km, vm) * jax.nn.silu(m_gate)

    mixed = jnp.concatenate([out_a, out_b, out_m], axis=-1)
    return x + mixed @ w_o

def setup_inputs(seed: int = 0) -> dict:
    key = jax.random.key(seed)
    ks = jax.random.split(key, 24)

    def nrm(k, shape, scale):
        return jax.random.normal(k, shape, dtype=jnp.float32) * scale

    def gain(k, shape):
        return 1.0 + 0.02 * jax.random.normal(k, shape, dtype=jnp.float32)

    x = nrm(ks[0], (BATCH, SEQ, D_MODEL), 1.0)
    mem = nrm(ks[1], (BATCH, N_MEM, D_MODEL), 1.0)
    offset = jax.random.randint(ks[2], (BATCH, 1), 0, 16, dtype=jnp.int32) * CHUNK
    positions = (offset + jnp.arange(SEQ, dtype=jnp.int32)[None, :]).astype(jnp.int32)
    return {
        'x': x,
        'mem': mem,
        'positions': positions,
        'g_in': gain(ks[3], (DEPTH, D_MODEL)),
        'w_in': nrm(ks[4], (DEPTH, D_MODEL, IN_WIDTH), D_MODEL ** -0.5),
        'a_g_q': gain(ks[5], (DEPTH, A_HEAD_DIM)),
        'a_g_k': gain(ks[6], (DEPTH, A_HEAD_DIM)),
        'a_sinks': nrm(ks[7], (DEPTH, A_HEADS), 0.5),
        'b_g_cq': gain(ks[8], (DEPTH, B_Q_RANK)),
        'b_w_q_up': nrm(ks[9], (DEPTH, B_Q_RANK, B_HEADS * (B_NOPE + B_ROPE)), B_Q_RANK ** -0.5),
        'b_g_ckv': gain(ks[10], (DEPTH, B_KV_RANK)),
        'b_w_kv_up': nrm(ks[11], (DEPTH, B_KV_RANK, B_HEADS * (B_NOPE + B_V)), B_KV_RANK ** -0.5),
        'b_g_q_nope': gain(ks[12], (DEPTH, B_NOPE)),
        'b_g_q_rope': gain(ks[13], (DEPTH, B_ROPE)),
        'b_g_k_nope': gain(ks[14], (DEPTH, B_NOPE)),
        'b_g_k_rope': gain(ks[15], (DEPTH, B_ROPE)),
        'm_g_mem': gain(ks[16], (DEPTH, D_MODEL)),
        'm_w_kv': nrm(ks[17], (DEPTH, D_MODEL, 2 * M_WIDTH), D_MODEL ** -0.5),
        'm_g_q': gain(ks[18], (DEPTH, M_HEAD_DIM)),
        'm_g_k': gain(ks[19], (DEPTH, M_HEAD_DIM)),
        'w_o': nrm(ks[20], (DEPTH, MIX_WIDTH, D_MODEL), MIX_WIDTH ** -0.5),
    }

def reference(x, mem, positions, g_in, w_in, a_g_q, a_g_k, a_sinks,
              b_g_cq, b_w_q_up, b_g_ckv, b_w_kv_up, b_g_q_nope, b_g_q_rope,
              b_g_k_nope, b_g_k_rope, m_g_mem, m_w_kv, m_g_q, m_g_k, w_o):
    y = x
    for l in range(DEPTH):
        y = hybrid_layer(y, mem, positions, g_in[l], w_in[l], a_g_q[l], a_g_k[l], a_sinks[l],
                         b_g_cq[l], b_w_q_up[l], b_g_ckv[l], b_w_kv_up[l], b_g_q_nope[l],
                         b_g_q_rope[l], b_g_k_nope[l], b_g_k_rope[l], m_g_mem[l], m_w_kv[l],
                         m_g_q[l], m_g_k[l], w_o[l])
    return y


_drawn_inputs = setup_inputs


def setup_inputs(seed=0):
    import zlib

    import numpy as np

    out = dict(_drawn_inputs(seed))
    spreads = {}
    factors = {'g_in': 8.0,
     'a_g_q': 8.0,
     'a_g_k': 8.0,
     'a_sinks': 8.0,
     'b_g_cq': 8.0,
     'b_g_ckv': 8.0,
     'b_g_q_nope': 8.0,
     'b_g_q_rope': 8.0,
     'b_g_k_nope': 8.0,
     'b_g_k_rope': 8.0,
     'm_g_mem': 8.0,
     'm_g_q': 8.0,
     'm_g_k': 8.0}
    for name, (base, spread) in spreads.items():
        noise = np.random.default_rng([zlib.crc32(name.encode()), seed]).standard_normal(out[name].shape)
        drawn = base * np.exp(spread * noise) if base else spread * noise
        out[name] = __import__('jax').numpy.asarray(drawn.astype(out[name].dtype))
    for name, factor in factors.items():
        out[name] = (out[name] * factor).astype(out[name].dtype)
    return out
```

```python
from contextlib import ExitStack

import concourse.bass as bass
import numpy as np
from concourse import mybir

F32 = mybir.dt.float32
F32R = mybir.dt.float32r
I32 = mybir.dt.int32
ALU = mybir.AluOpType
ACT = mybir.ActivationFunctionType
X = mybir.AxisListType.X

P = 128
D = 2048
SEQ = 1024
KT = D // P
TT = SEQ // P
HALF = 512
NMEM = 256
CHUNK = 64
NCHUNK = SEQ // CHUNK
AH, AKV, AD = 16, 2, 64
AJ = AH // AKV
BH, BN, BR, BV = 4, 128, 64, 128
BQR, BKVR = 512, 256
MH, MD = 4, 128
EPS = 1e-6
SCALE_A = AD ** -0.5
SCALE_B = (BN + BR) ** -0.5
SCALE_M = MD ** -0.5
BIG = 3.0e38
TWO_PI = 2 * float(np.pi)
PI_BELOW = 3.1415925
ROUND = 1.5 * 2.0 ** 23
_C1 = 6.28125
_C2 = float(np.round((TWO_PI - _C1) * 2.0 ** 20) / 2.0 ** 20)
TWO_PI_PARTS = (_C1, _C2, TWO_PI - _C1 - _C2)

G_KV, G_CQ, G_AQ0, G_AQ1, G_MQ, G_GATE0 = 0, 1, 2, 3, 4, 5
NGATE = 4
G_MEM0 = G_GATE0 + NGATE
CPG = KT // 2
CH_KR = G_MEM0 * CPG
CH_MEM = CH_KR + 1
CH_OUT = CH_MEM + 2 * CPG
NCH = CH_OUT + (D // HALF) * CPG
RAW = 3
SPLIT = 2
PAD = CHUNK


def wait(e, sem, value):
    if isinstance(value, int) and value <= 0:
        return
    e.wait_ge(sem, value)


class Steps:

    def __init__(self, engine, sem):
        self.engine, self.sem, self.n = engine, sem, 0

    def did(self, ins):
        ins.then_inc(self.sem, 1)
        self.n = self.n + 1

    def settle(self):
        self.engine.wait_ge(self.sem, self.n)


def pipelined(engine, n, body, steps=()):
    before = [s.n for s in steps]
    body(0, True, False)
    per = [s.n - b for s, b in zip(steps, before)]
    with engine.Fori(1, n - 1) as i:
        for s, b, k in zip(steps, before, per):
            s.n = i * k + b
        body(i, False, False)
    for s, b, k in zip(steps, before, per):
        s.n = b + (n - 1) * k
    body(n - 1, False, True)


def layer(nc, io):
    with ExitStack() as ctx:
        def sem(name):
            return ctx.enter_context(nc.semaphore(name))

        top = [(nc.sbuf_base + 31) // 32 * 32]

        def region(size):
            at = top[0]
            top[0] += size
            assert top[0] <= nc.sbuf_usable_end, top[0] - nc.sbuf_usable_end
            return at

        def at(name, shape, dt, offset):
            return nc.alloc_sbuf_tensor_at(name, shape, dt, offset=offset)

        R0, R1 = region(KT * SEQ * 4), region(KT * SEQ * 4)
        WRAW = region(RAW * 4096)
        WHI, WLO = region(SPLIT * 4096), region(SPLIT * 4096)
        RS, RT = region(16384), region(16384)

        def small(name, shape, dt=F32):
            size = int(np.prod(shape[1:])) * 4
            return at(name, shape, dt, region((size + 31) // 32 * 32))

        def inside(start, size):
            where = [start]

            def place(name, shape, dt=F32):
                t = at(name, shape, dt, where[0])
                where[0] += int(np.prod(shape[1:])) * 4
                assert where[0] <= start + size, name
                return t
            return place

        h_hi = at("h_hi", [P, KT, SEQ], F32R, R0)
        h_lo = at("h_lo", [P, KT, SEQ], F32R, R1)
        x_raw = at("x_raw", [P, KT, SEQ], F32, R1)
        m_hi = at("m_hi", [P, KT, NMEM], F32R, R0)
        m_lo = at("m_lo", [P, KT, NMEM], F32R, R1)
        mem_raw = at("mem_raw", [P, KT, NMEM], F32, R1)
        mixed = at("mixed", [P, KT, SEQ], F32, R1)
        w_raw = at("w_raw", [P, RAW, 1024], F32, WRAW)
        w_hi = at("w_hi", [P, SPLIT, 1024], F32R, WHI)
        w_lo = at("w_lo", [P, SPLIT, 1024], F32R, WLO)
        S = at("S", [P, 8, HALF], F32, RS)
        T = at("T", [P, 8, HALF], F32, RT)

        qnT = at("qnT", [P, BH, SEQ], F32, R0)
        knT = at("knT", [P, BH, SEQ], F32, R0 + 16384)
        vB = at("vB", [P, TT, BH * BV], F32, R0 + 32768)
        qrT = at("qrT", [P, BH // 2, SEQ], F32, R0 + 49152)
        krT = at("krT", [P, SEQ], F32, R0 + 57344)

        ident = small("ident", [P, P])
        cos = small("cos", [P, TT, 32])
        sin = small("sin", [P, TT, 32])
        tab_at = top[0]
        tab = small("tab", [P, 4, TT, 32])
        sumsq = at("sumsq", [P, SEQ], F32, RS)
        rs_row_at = top[0]
        rs_row = small("rs_row", [P, SEQ])
        rs_col = small("rs_col", [P, TT])
        ms_col = small("ms_col", [P, 2])
        g_x = small("g_x", [P, KT])
        g_mem = small("g_mem", [P, KT])
        sinks = small("sinks", [P, AJ])
        g_aq = small("g_aq", [P, AD])
        g_ak = small("g_ak", [P, AD])
        g_cq = small("g_cq", [P, BQR])
        g_ckv = small("g_ckv", [P, BKVR])
        g_qn = small("g_qn", [P, BN])
        g_kn = small("g_kn", [P, BN])
        g_qr = small("g_qr", [P, BR])
        g_kr = small("g_kr", [P, BR])
        g_mq = small("g_mq", [P, MD])
        g_mk = small("g_mk", [P, MD])
        invf = small("invf", [P, 32])
        b_pad = small("b_pad", [PAD, 256])
        posi = small("posi", [P, TT], I32)
        pos = small("pos", [P, TT])
        mhalf = small("mhalf", [P, 1])
        kmT = at("kmT", [P, MH, NMEM], F32, rs_row_at)
        vM = at("vM", [P, 2, MH * MD], F32, tab_at)
        ss = small("ss", [P, 64])
        rr = small("rr", [P, 64])
        st = small("st", [P, 2, 4, 8])

        up_at = inside(R1 + 16384, 40960)
        uq_hi = up_at("uq_hi", [P, 4, 768], F32R)
        uq_raw_at = R1 + 16384 + 12288
        uq_lo = up_at("uq_lo", [P, 4, 768], F32R)
        ukv_hi = up_at("ukv_hi", [P, 2, 1024], F32R)
        ukv_raw_at = R1 + 16384 + 24576 + 8192
        ukv_lo = up_at("ukv_lo", [P, 2, 1024], F32R)
        uq_raw = at("uq_raw", [P, 4, 768], F32, uq_raw_at)
        ukv_raw = at("ukv_raw", [P, 2, 1024], F32, ukv_raw_at)
        put = inside(RS, 32768)
        u_in = put("u_in", [P, 2, 768])
        c_hi = put("c_hi", [P, 6, P], F32R)
        c_lo = put("c_lo", [P, 6, P], F32R)
        u_out = put("u_out", [P, 1280])
        u_fin = put("u_fin", [P, 1280])
        u_tmp = put("u_tmp", [P, 2, 4, 32])
        put = inside(RS, 32768)
        a_q = put("a_q", [CHUNK, 2, AJ * P])
        a_kv = put("a_kv", [P, 2, 256])
        a_gate = put("a_gate", [P, 2, AJ, CHUNK])
        a_qT = put("a_qT", [P, 2, AJ, CHUNK])
        a_kT = put("a_kT", [P, 2, P])
        a_p = put("a_p", [P, 2, 8, P])
        a_pT = put("a_pT", [P, 2, HALF])
        put = inside(RS, 32768)
        c_q = put("c_q", [P, 2, MH * MD])
        c_gate = put("c_gate", [P, 2, MH, P])
        c_qT = put("c_qT", [P, 2, MH, P])
        c_p = put("c_p", [P, 2, MH, NMEM])
        c_pT = put("c_pT", [P, 2, HALF])
        c_km = put("c_km", [P, 2, HALF])
        put = inside(RS, 32768)
        b_p = put("b_p", [P, 2, SEQ])
        b_pT = put("b_pT", [P, SEQ])
        b_gate = put("b_gate", [P, 2, SEQ])

        ps = ctx.enter_context(nc.psum_tensor("ps", [P, 8, HALF], F32))

        def scratch(name, shape):
            return nc.dram_tensor(name, shape, F32, kind="Internal").ap()

        kv_s = scratch("kv_s", [PAD + SEQ, HALF])
        cq_s = scratch("cq_s", [SEQ, BQR])
        aq_s = scratch("aq_s", [SEQ, 2, HALF])
        mq_s = scratch("mq_s", [SEQ, HALF])
        gate_s = scratch("gate_s", [KT, P, SEQ])
        km_s = scratch("km_s", [NMEM, HALF])
        vm_s = scratch("vm_s", [NMEM, HALF])
        row_s = scratch("row_s", [2, SEQ])

        w_loaded = [sem(f"w_loaded{i}") for i in range(RAW)]
        hi_ready, lo_ready, w_used = sem("hi_ready"), sem("lo_ready"), sem("w_used")
        x_loaded = [sem(f"x_loaded{i}") for i in range(KT // 2)]
        h_hi_ready, h_lo_ready = sem("h_hi_ready"), sem("h_lo_ready")
        sq_ready, sq_used, sum_ready = sem("sq_ready"), sem("sq_used"), sem("sum_ready")
        row_ready, row_stored, col_loaded = sem("row_ready"), sem("row_stored"), sem("col_loaded")
        consts_loaded, pool_consts = sem("consts_loaded"), sem("pool_consts")
        angles_ready, trig_ready = sem("angles_ready"), sem("trig_ready")
        acc_done, acc_free, mem_done, mem_free = sem("acc_done"), sem("acc_free"), sem("mem_done"), sem("mem_free")
        t_square, t_ready = sem("t_square"), sem("t_ready")
        t_stored, ms_ready, rr_ready = sem("t_stored"), sem("ms_ready"), sem("rr_ready")
        dve_sem, act_sem, pool_sem = sem("dve_steps"), sem("act_steps"), sem("pool_steps")
        mem_loaded, mem_scaled, m_hi_ready, m_lo_ready = (
            sem("mem_loaded"), sem("mem_scaled"), sem("m_hi_ready"), sem("m_lo_ready"))
        kr_raw, kr_back, kr_nat, kr_sq, kr_norm, kr_turned, kr_kept = (
            sem("kr_raw"), sem("kr_back"), sem("kr_nat"), sem("kr_sq"), sem("kr_norm"), sem("kr_turned"), sem("kr_kept"))
        up_w_loaded, up_hi, up_lo = sem("up_w_loaded"), sem("up_hi"), sem("up_lo")
        u_loaded = [sem(f"u_loaded{i}") for i in range(2)]
        u_turned, u_chi, u_clo, u_up, u_ev, u_sq = (
            sem("u_turned"), sem("u_chi"), sem("u_clo"), sem("u_up"), sem("u_ev"), sem("u_sq"))
        u_ms, u_rr, u_done, u_qn, u_kn, u_qr = (
            sem("u_ms"), sem("u_rr"), sem("u_done"), sem("u_qn"), sem("u_kn"), sem("u_qr"))
        u_qn_kept, u_kn_kept, u_qr_kept = sem("u_qn_kept"), sem("u_kn_kept"), sem("u_qr_kept")

        class Attention:

            def __init__(self, b):
                self.loaded = [sem(f"{b}_loaded{i}") for i in range(2)]
                self.q_turned, self.k_turned = sem(f"{b}_q_turned"), sem(f"{b}_k_turned")
                self.qT, self.kT = sem(f"{b}_qT"), sem(f"{b}_kT")
                self.scored, self.shifted, self.exp = sem(f"{b}_scored"), sem(f"{b}_shifted"), sem(f"{b}_exp")
                self.p, self.p_turned, self.pT = sem(f"{b}_p"), sem(f"{b}_p_turned"), sem(f"{b}_pT")
                self.pv, self.gated = sem(f"{b}_pv"), sem(f"{b}_gated")

        A, B, M = Attention("a"), Attention("b"), Attention("m")
        pad_stored = sem("pad_stored")
        km_loaded, vm_loaded, km_turned, km_kept = sem("km_loaded"), sem("vm_loaded"), sem("km_turned"), sem("km_kept")
        res_loaded = [sem(f"res_loaded{i}") for i in range(2)]
        out_stored = sem("out_stored")

        CONSTS = [(g_x, "g_in"), (g_mem, "m_g_mem"), (g_aq, "a_g_q"), (g_ak, "a_g_k"), (g_cq, "b_g_cq"),
                  (g_ckv, "b_g_ckv"), (g_qn, "b_g_q_nope"), (g_kn, "b_g_k_nope"), (g_qr, "b_g_q_rope"),
                  (g_kr, "b_g_k_rope"), (g_mq, "m_g_q"), (g_mk, "m_g_k"), (invf, "invf"), (posi, "positions")]
        N_CONSTS = len(CONSTS) + 2

        block = ctx.enter_context(nc.Block())

        NTOK = G_MEM0
        POST_MEM = NTOK
        NPOST = NTOK + 2
        ROOTS = {G_KV: 24, G_CQ: 8, G_AQ0: 64, G_AQ1: 64, G_MQ: 32}
        OUT_GROUPS = D // HALF

        BSTEPS = [(h, t) for h in range(BH) for t in range(TT)]

        @block.sync
        def _(sp):
            def load_w(n, slot, first=False):
                if not first:
                    sp.wait_ge(hi_ready, n - (RAW - 1))
                    sp.wait_ge(lo_ready, n - (RAW - 1))
                sp.dma_start(w_raw[:, slot, :], io["w"][n]).then_inc(w_loaded[slot], 16)

            def load_x(k2):
                sp.dma_start(x_raw[:, 2 * k2:2 * k2 + 2, :],
                             io["xT"][2 * k2:2 * k2 + 2].rearrange("k p s -> p k s")).then_inc(x_loaded[k2], 16)

            load_w(0, 0, first=True)
            load_x(0)
            load_w(1, 1, first=True)
            load_x(1)
            load_w(2, 2, first=True)
            for k2 in range(2, KT // 2):
                load_x(k2)
            mid = (CH_OUT + RAW) // RAW * RAW - RAW
            with sp.Fori(1, mid // RAW) as i:
                for s in range(RAW):
                    load_w(i * RAW + s, s)
            n = mid
            while n < CH_OUT + RAW:
                load_w(n, n % RAW)
                n += 1

            sp.wait_ge(t_stored, 16 * NPOST)
            for t in range(TT):
                if t >= 2:
                    sp.wait_ge(u_turned, t - 1)
                sp.dma_start(u_in[:, t % 2, 0:BQR], cq_s[t * P:(t + 1) * P, :]).then_inc(u_loaded[t % 2], 16)
                sp.dma_start(u_in[:, t % 2, BQR:], kv_s[PAD + t * P:PAD + (t + 1) * P, 256:]
                             ).then_inc(u_loaded[t % 2], 16)

            sp.wait_ge(u_qr_kept, TT)
            sp.wait_ge(u_kn_kept, TT)
            sp.wait_ge(pad_stored, 16)

            def load_a(i, first, last):
                for par in range(2):
                    c = 2 * i + par
                    if not first:
                        sp.wait_ge(A.gated, c - 1)
                    aq = aq_s.rearrange("s a n -> s (a n)")
                    sp.dma_start(a_q[:, par, :], aq[bass.ds(c * CHUNK, CHUNK), :]).then_inc(A.loaded[par], 16)
                    sp.dma_start(a_kv[:, par, :], kv_s[bass.ds(c * CHUNK, P), 0:256]).then_inc(A.loaded[par], 16)
                    sp.dma_start(a_gate[:, par], gate_s[0:AJ, :, bass.ds(c * CHUNK, CHUNK)].rearrange("j p s -> p j s")
                                 ).then_inc(A.loaded[par], 16)

            pipelined(sp, NCHUNK // 2, load_a)

            sp.wait_ge(A.gated, NCHUNK)
            for h in range(BH):
                if h >= 2:
                    sp.wait_ge(B.gated, TT * (h - 1))
                sp.dma_start(b_gate[:, h % 2, :], gate_s[AJ + h]).then_inc(B.loaded[h % 2], 16)

            sp.wait_ge(B.gated, len(BSTEPS))
            sp.dma_start(c_km[:], km_s.rearrange("(t p) n -> p t n", p=P)).then_inc(km_loaded, 16)
            sp.dma_start(vM[:], vm_s.rearrange("(t p) n -> p t n", p=P)).then_inc(vm_loaded, 16)

            def load_m(i, first, last):
                for par in range(2):
                    t = 2 * i + par
                    if not first:
                        sp.wait_ge(M.gated, t - 1)
                    sp.dma_start(c_q[:, par, :], mq_s[bass.ds(t * P, P), :]).then_inc(M.loaded[par], 16)
                    sp.dma_start(c_gate[:, par], gate_s[AJ + BH:KT, :, bass.ds(t * P, P)].rearrange("j p s -> p j s")
                                 ).then_inc(M.loaded[par], 16)

            pipelined(sp, TT // 2, load_m)

            while n % RAW:
                load_w(n, n % RAW)
                n += 1
            with sp.Fori(n // RAW, NCH // RAW) as i:
                for s in range(RAW):
                    load_w(i * RAW + s, s)
            for n in range(NCH // RAW * RAW, NCH):
                load_w(n, n % RAW)

        @block.gpsimd
        def _(pool):
            steps = Steps(pool, pool_sem)
            g = nc.gpsimd
            steps.did(g.memset(ident[:], 0.0))
            steps.settle()
            g.affine_select(out=ident[:], in_=ident[:], compare_op=ALU.not_equal, fill=1.0, base=0,
                            pattern=[[-1, P]], channel_multiplier=1).then_inc(pool_consts, 1)
            g.memset(mhalf[:], -0.5).then_inc(pool_consts, 1)
            pool.wait_ge(pool_consts, 2)
            steps.did(g.memset(b_pad[:], 0.0))
            steps.settle()
            pool.dma_start(kv_s[0:PAD, 0:256], b_pad[:]).then_inc(pad_stored, 16)

            def rms_row(wave, sums, width, col):
                row = rs_row[:, 0:width]
                steps.did(g.partition_all_reduce(row, sums, P, bass.bass_isa.ReduceOp.add))
                steps.settle()
                steps.did(g.tensor_scalar(row, row, 1.0 / D, EPS, ALU.mult, ALU.add))
                steps.settle()
                g.tensor_tensor(row, row, mhalf[:].to_broadcast([P, width]), ALU.pow).then_inc(row_ready, 1)
                pool.wait_ge(row_ready, wave + 1)
                pool.dma_start(row_s[wave:wave + 1, 0:width], rs_row[0:1, 0:width]).then_inc(row_stored, 16)
                pool.wait_ge(row_stored, 16 * (wave + 1))
                pool.dma_start(col[:], row_s[wave, 0:width].rearrange("(t p) -> p t", p=P),
                               allow_slow_non_contiguous=True).then_inc(col_loaded, 16)

            roots = [0]

            def root(width):
                pool.wait_ge(ms_ready, roots[0] + 1)
                g.tensor_tensor(rr[:, 0:width], ss[:, 0:width], mhalf[:].to_broadcast([P, width]),
                                ALU.pow).then_inc(rr_ready, 1)
                roots[0] += 1

            pool.wait_ge(sq_used, KT)
            rms_row(0, sumsq[:], SEQ, rs_col)
            rows = lambda a: a.rearrange("(t p) n -> p t n", p=P)
            for post in range(NTOK):
                if post in ROOTS:
                    root(ROOTS[post])
                if post < G_GATE0:
                    dst = {G_KV: kv_s[PAD:PAD + SEQ, :], G_CQ: cq_s, G_AQ0: aq_s[:, 0, :], G_AQ1: aq_s[:, 1, :],
                           G_MQ: mq_s}[post]
                    dst, src = rows(dst), T[:]
                else:
                    j = 4 * (post - G_GATE0)
                    dst = gate_s[j:j + 4].rearrange("c p s -> p c s")
                    src = T[:].rearrange("p (c h) n -> p c (h n)", h=2)
                pool.wait_ge(t_ready, post + 1)
                pool.dma_start(dst, src).then_inc(t_stored, 16)
            pool.wait_ge(w_used, CH_KR + 1)
            pool.dma_start(mem_raw[:], io["memT"].rearrange("k p s -> p k s")).then_inc(mem_loaded, 16)
            pool.dma_start(uq_raw[:], io["w_q_up"].rearrange("k p n -> p k n")).then_inc(up_w_loaded, 16)
            pool.dma_start(ukv_raw[:], io["w_kv_up"].rearrange("k p n -> p k n")).then_inc(up_w_loaded, 16)
            root(8)
            pool.wait_ge(sum_ready, 1)
            rms_row(1, S[:, 7, 0:NMEM], NMEM, ms_col)
            root(8)
            for m in range(2):
                pool.wait_ge(t_ready, POST_MEM + m + 1)
                pool.dma_start(rows(km_s if m == 0 else vm_s), T[:, 0:2, :]).then_inc(t_stored, 16)
            for t in range(TT):
                pool.wait_ge(u_ms, t + 1)
                g.tensor_tensor(rr[:, 0:12], ss[:, 0:12], mhalf[:].to_broadcast([P, 12]), ALU.pow).then_inc(u_rr, 1)
            xr = io["x"].rearrange("(t p) n -> p t n", p=P)
            yr = io["y"].rearrange("(t p) n -> p t n", p=P)
            pool.wait_ge(M.gated, TT)
            for og in range(OUT_GROUPS + 2):
                if og >= 2:
                    pool.wait_ge(acc_free, TT * (NTOK + og - 1))
                    buf = (S, T)[og % 2]
                    pool.dma_start(yr[:, :, (og - 2) * HALF:(og - 1) * HALF], buf[:]).then_inc(out_stored, 16)
                if og < OUT_GROUPS:
                    if og >= 2:
                        pool.wait_ge(out_stored, 16 * (og - 1))
                    buf = (S, T)[og % 2]
                    pool.dma_start(buf[:], xr[:, :, og * HALF:(og + 1) * HALF]).then_inc(res_loaded[og % 2], 16)
            pool.wait_ge(out_stored, 16 * OUT_GROUPS)

        def gate_exp(act, a, group):
            act.wait_ge(acc_free, TT * (group + 1))
            act.wait_ge(t_stored, 16 * group)
            a.activation(T[:], S[:], ACT.Exp, scale=-1.0).then_inc(t_square, 1)

        @block.scalar
        def _(act):
            a = nc.scalar
            steps = Steps(act, act_sem)
            for tile, name in CONSTS:
                src = io[name]
                if src.shape[0] == 1:
                    src = src.to_broadcast([P, src.shape[-1]])
                act.dma_start(tile[:], src).then_inc(consts_loaded, 16)
            for o in range(2):
                act.dma_start(sinks[64 * o:64 * o + 64, :], io["sinks"][o:o + 1, :].to_broadcast([64, AJ])
                              ).then_inc(consts_loaded, 16)

            def high(n):
                act.wait_ge(w_loaded[n % RAW], 16 * (n // RAW + 1))
                wait(act, w_used, n - SPLIT + 1)
                a.activation(w_hi[:, n % SPLIT, :], w_raw[:, n % RAW, :], ACT.Copy).then_inc(hi_ready, 1)

            act.wait_ge(consts_loaded, 16 * N_CONSTS)
            for c in range(CPG):
                high(c)
                act.wait_ge(x_loaded[c], 16)
                for k in (2 * c, 2 * c + 1):
                    a.activation(h_hi[:, k, :], x_raw[:, k, :], ACT.Copy, scale=g_x[:, k:k + 1]).then_inc(h_hi_ready, 1)
                    if k >= 4:
                        act.wait_ge(sq_used, k - 3)
                    sq = T[:, 2 * (k % 4):2 * (k % 4) + 2, :].rearrange("p a n -> p (a n)")
                    a.activation(sq, x_raw[:, k, :], ACT.Square).then_inc(sq_ready, 1)

            def evacuate(group):
                if group == 0:
                    act.wait_ge(col_loaded, 16)
                wait(act, t_ready, group)
                for t in range(TT):
                    if t < TT - 1:
                        act.wait_ge(acc_done, (TT - 1) * group + t + 1)
                    else:
                        act.wait_ge(w_used, CPG * (group + 1))
                    a.activation(S[:, t, :], ps[:, t, :], ACT.Copy, scale=rs_col[:, t:t + 1]).then_inc(acc_free, 1)
                if group == 0:
                    act.wait_ge(sq_used, KT)
                else:
                    act.wait_ge(t_stored, 16 * group)
                act.wait_ge(acc_free, TT * (group + 1))
                a.activation(T[:], S[:], ACT.Square).then_inc(t_square, 1)

            for group in range(1, NTOK + 1):
                for c in range(CPG if group < NTOK else 1):
                    high(CPG * group + c)
                    if c == 0 and group - 1 < G_GATE0:
                        evacuate(group - 1)
                    if c == 1 and group == 1:
                        act.wait_ge(angles_ready, 1)
                        for tile in (sin, cos):
                            a.activation(tile[:], tile[:], ACT.Sin).then_inc(trig_ready, 1)
                    if c == (1 if group < NTOK else 0) and group - 1 >= G_GATE0:
                        gate_exp(act, a, group - 1)

            act.wait_ge(w_used, CH_KR + 1)
            act.wait_ge(t_ready, NTOK)
            a.activation(S[0:BR, 0:2, :], ps[0:BR, 0:2, :], ACT.Copy).then_inc(kr_raw, 1)
            act.wait_ge(kr_nat, 1)
            a.activation(S[:, 5, :], S[:, 4, :], ACT.Square).then_inc(kr_sq, 1)
            act.wait_ge(mem_loaded, 16)
            act.wait_ge(t_stored, 16 * NTOK)
            a.activation(T[:].rearrange("p a n -> p (a n)"), mem_raw[:].rearrange("p k s -> p (k s)"), ACT.Square
                         ).then_inc(t_square, 1)
            act.wait_ge(mem_scaled, 1)
            a.activation(m_hi[:].rearrange("p k s -> p (k s)"), mem_raw[:].rearrange("p k s -> p (k s)"), ACT.Copy
                         ).then_inc(m_hi_ready, 1)
            high(CH_MEM)
            high(CH_MEM + 1)
            act.wait_ge(kr_turned, 1)
            act.wait_ge(w_used, CH_KR + 1)
            a.activation(krT[:], ps[:, 3:5, :].rearrange("p a n -> p (a n)"), ACT.Copy).then_inc(kr_kept, 1)
            act.wait_ge(up_w_loaded, 32)
            a.activation(uq_hi[:], uq_raw[:], ACT.Copy).then_inc(up_hi, 1)
            a.activation(ukv_hi[:], ukv_raw[:], ACT.Copy).then_inc(up_hi, 1)
            for n in range(CH_MEM + 2, CH_MEM + CPG + 2):
                high(n)
            for m in range(2):
                if m == 0:
                    act.wait_ge(col_loaded, 32)
                    act.wait_ge(kr_turned, 1)
                else:
                    act.wait_ge(t_ready, NTOK + 1)
                for t in range(2):
                    act.wait_ge(mem_done, m + 1) if t == 0 else act.wait_ge(w_used, CH_MEM + CPG * (m + 1))
                    a.activation(S[:, t, :], ps[:, 5 + t, :], ACT.Copy, scale=ms_col[:, t:t + 1]).then_inc(mem_free, 1)
                if m == 0:
                    act.wait_ge(mem_free, 2)
                    act.wait_ge(sum_ready, 1)
                    a.activation(T[:, 0:2, :], S[:, 0:2, :], ACT.Square).then_inc(t_square, 1)
                    for n in range(CH_MEM + CPG + 2, CH_OUT):
                        high(n)

            def up_in(t):
                act.wait_ge(u_turned, t + 1)
                wait(act, u_up, t)
                a.activation(c_hi[:].rearrange("p k s -> p (k s)"),
                             ps[:, 0:2, :].rearrange("p a n -> p (a n)")[:, 0:768], ACT.Copy).then_inc(u_chi, 1)

            def up_out(t):
                act.wait_ge(u_up, t + 1)
                wait(act, u_done, t)
                a.activation(vB[:, t, :], ps[:, 5, :], ACT.Copy).then_inc(u_ev, 1)
                a.activation(u_out[:], ps[:, 2:5, :].rearrange("p a n -> p (a n)")[:, 0:1280], ACT.Copy
                             ).then_inc(u_ev, 1)
                wait(act, u_qr, t)
                act.wait_ge(u_ev, 2 * (t + 1))
                a.activation(u_fin[:], u_out[:], ACT.Square).then_inc(u_sq, 1)

            up_in(0)
            up_out(0)
            for t in range(TT):
                if t + 1 < TT:
                    up_in(t + 1)
                act.wait_ge(u_qn, t + 1)
                a.activation(qnT[:, :, t * P:(t + 1) * P], ps[:, 6, :].rearrange("p (h s) -> p h s", h=BH), ACT.Copy
                             ).then_inc(u_qn_kept, 1)
                act.wait_ge(u_qr, t + 1)
                a.activation(qrT[:, :, t * P:(t + 1) * P], ps[:, 6, 0:256].rearrange("p (h s) -> p h s", h=2), ACT.Copy
                             ).then_inc(u_qr_kept, 1)
                if t + 1 < TT:
                    up_out(t + 1)

            def a_first(c, par, first):
                act.wait_ge(A.q_turned, c + 1)
                if not first:
                    act.wait_ge(A.scored, c - 1)
                a.activation(a_qT[:, par], ps[:, 0, :].rearrange("p (j s) -> p j s", j=AJ), ACT.Copy).then_inc(A.qT, 1)
                act.wait_ge(A.shifted, c + 1)
                a.activation(st[:, par, 1, :], st[:, par, 1, :], ACT.Exp, scale=SCALE_A).then_inc(A.exp, 1)
                a.activation(a_p[:, par], a_p[:, par], ACT.Exp, scale=SCALE_A).then_inc(A.exp, 1)

            def a_second(c, first):
                act.wait_ge(A.p_turned, c + 1)
                if not first:
                    act.wait_ge(A.pv, c)
                for g in range(2):
                    a.activation(a_pT[:, g, :], ps[:, 6 + g, :], ACT.Copy).then_inc(A.pT, 1)

            def a_pair(i, first, last):
                c = 2 * i
                a_first(c + 1, 1, first)
                a_second(c, first)
                if not last:
                    a_first(c + 2, 0, False)
                a_second(c + 1, False)

            a_first(0, 0, True)
            pipelined(act, NCHUNK // 2, a_pair)

            def b_first(s):
                h, t = BSTEPS[s]
                width, par = (t + 1) * P, s % 2
                act.wait_ge(B.shifted, s + 1)
                if s >= 2:
                    act.wait_ge(B.p_turned, s - 1)
                a.activation(b_p[:, par, 0:width], ps[:, 2 + 2 * par:4 + 2 * par, :].rearrange("p a n -> p (a n)")[:, 0:width],
                             ACT.Exp, bias=st[:, par, 1, 0:1], scale=SCALE_B, accum_out=st[:, par, 2, 0:1]
                             ).then_inc(B.exp, 1)

            def b_second(s):
                h, t = BSTEPS[s]
                width = (t + 1) * P
                act.wait_ge(B.p_turned, s + 1)
                wait(act, B.pv, s)
                a.activation(b_pT[:, 0:width], ps[:, 6:8, :].rearrange("p a n -> p (a n)")[:, 0:width], ACT.Copy
                             ).then_inc(B.pT, 1)

            b_first(0)
            for s in range(len(BSTEPS)):
                if s + 1 < len(BSTEPS):
                    b_first(s + 1)
                b_second(s)

            act.wait_ge(km_turned, 1)
            a.activation(kmT[:].rearrange("p h s -> p (h s)"), ps[:, 6:8, :].rearrange("p a n -> p (a n)"), ACT.Copy
                         ).then_inc(km_kept, 1)

            def m_first(t, par, first):
                act.wait_ge(M.q_turned, t + 1)
                if not first:
                    act.wait_ge(M.scored, t - 1)
                a.activation(c_qT[:, par], ps[:, 0, :].rearrange("p (j s) -> p j s", j=MH), ACT.Copy).then_inc(M.qT, 1)
                act.wait_ge(M.shifted, t + 1)
                a.activation(c_p[:, par], c_p[:, par], ACT.Exp, scale=SCALE_M).then_inc(M.exp, 1)

            def m_second(t, first):
                act.wait_ge(M.p_turned, t + 1)
                if not first:
                    act.wait_ge(M.pv, t)
                for kb in range(2):
                    a.activation(c_pT[:, kb, :], ps[:, 6 + kb, :], ACT.Copy).then_inc(M.pT, 1)

            def m_pair(i, first, last):
                t = 2 * i
                m_first(t + 1, 1, first)
                m_second(t, first)
                if not last:
                    m_first(t + 2, 0, False)
                m_second(t + 1, False)

            m_first(0, 0, True)
            pipelined(act, TT // 2, m_pair)

            act.wait_ge(M.gated, TT)
            for c in range(CPG):
                for k in (2 * c, 2 * c + 1):
                    a.activation(h_hi[:, k, :], mixed[:, k, :], ACT.Copy).then_inc(h_hi_ready, 1)
                high(CH_OUT + c)
            for n in range(CH_OUT + CPG, NCH):
                high(n)

        @block.vector
        def _(dve):
            v = nc.vector
            steps = Steps(dve, dve_sem)

            def do(ins):
                steps.did(ins)
                steps.settle()

            def low(n):
                dve.wait_ge(hi_ready, n + 1)
                wait(dve, w_used, n - SPLIT + 1)
                v.tensor_tensor(w_lo[:, n % SPLIT, :], w_raw[:, n % RAW, :], w_hi[:, n % SPLIT, :].bitcast(F32),
                                ALU.subtract).then_inc(lo_ready, 1)

            dve.wait_ge(consts_loaded, 16 * N_CONSTS)
            do(v.memset(sumsq[:], 0.0))
            for c in range(CPG):
                low(c)
                for k in (2 * c, 2 * c + 1):
                    dve.wait_ge(sq_ready, k + 1)
                    dve.wait_ge(h_hi_ready, k + 1)
                    v.scalar_tensor_tensor(out=h_lo[:, k, :], in0=x_raw[:, k, :], scalar=g_x[:, k:k + 1],
                                           in1=h_hi[:, k, :].bitcast(F32), op0=ALU.mult, op1=ALU.subtract
                                           ).then_inc(h_lo_ready, 1)
                    sq = T[:, 2 * (k % 4):2 * (k % 4) + 2, :].rearrange("p a n -> p (a n)")
                    wait(dve, sq_used, k)
                    v.tensor_tensor(sumsq[:], sumsq[:], sq, ALU.add).then_inc(sq_used, 1)

            def angles():
                do(v.tensor_copy(pos[:], posi[:]))
                grid = [P, TT, 32]
                do(v.tensor_tensor(sin[:], pos[:].unsqueeze(2).to_broadcast(grid),
                                   invf[:].unsqueeze(1).to_broadcast(grid), ALU.mult))
                turns, rest = tab[:, 0], tab[:, 1]
                do(v.tensor_scalar(turns, sin[:], 1.0 / TWO_PI, None, ALU.mult))
                do(v.tensor_scalar(turns, turns, ROUND, None, ALU.add))
                do(v.tensor_scalar(turns, turns, ROUND, None, ALU.subtract))
                for part in TWO_PI_PARTS:
                    do(v.tensor_scalar(rest, turns, part, None, ALU.mult))
                    do(v.tensor_tensor(sin[:], sin[:], rest, ALU.subtract))
                do(v.tensor_scalar(cos[:], sin[:], TWO_PI / 4, None, ALU.add))
                do(v.tensor_scalar(rest, cos[:], PI_BELOW, TWO_PI, ALU.is_gt, ALU.mult))
                do(v.tensor_tensor(cos[:], cos[:], rest, ALU.subtract))
                do(v.tensor_scalar(cos[:], cos[:], PI_BELOW, -PI_BELOW, ALU.min, ALU.max))
                v.tensor_scalar(sin[:], sin[:], PI_BELOW, -PI_BELOW, ALU.min, ALU.max).then_inc(angles_ready, 1)

            def tables(gain):
                lo, hi = gain[:, 0:32], gain[:, 32:64]
                for k, (f, part) in enumerate(((cos, lo), (sin, hi), (cos, hi), (sin, lo))):
                    steps.did(v.tensor_tensor(tab[:, k], f[:], part.unsqueeze(1).to_broadcast([P, TT, 32]), ALU.mult))
                steps.settle()

            def rotary(src, dst, n, k, tmp):
                x1, x2 = src[:, :, :, 0:32], src[:, :, :, 32:64]
                d1, d2 = dst[:, :, :, 0:32], dst[:, :, :, 32:64]
                table = lambda i: tab[:, i].unsqueeze(2).to_broadcast([P, TT, n, 32])
                if k == 0:
                    do(v.tensor_tensor(tmp, x2, table(1), ALU.mult))
                elif k == 1:
                    do(v.tensor_tensor(d1, x1, table(0), ALU.mult))
                elif k == 2:
                    do(v.tensor_tensor(d1, d1, tmp, ALU.subtract))
                elif k == 3:
                    do(v.tensor_tensor(d2, x2, table(2), ALU.mult))
                elif k == 4:
                    do(v.tensor_tensor(tmp, x1, table(3), ALU.mult))
                else:
                    do(v.tensor_tensor(d2, d2, tmp, ALU.add))

            roots = [0]

            def mean_squares(pieces):
                for view, a, b, width in pieces:
                    steps.did(v.tensor_reduce(ss[:, a:b], view, X, ALU.add))
                steps.settle()
                for i, (view, a, b, width) in enumerate(pieces):
                    ins = v.tensor_scalar(ss[:, a:b], ss[:, a:b], 1.0 / width, EPS, ALU.mult, ALU.add)
                    if i + 1 < len(pieces):
                        steps.did(ins)
                        steps.settle()
                    else:
                        ins.then_inc(ms_ready, 1)
                roots[0] += 1

            def rooted():
                dve.wait_ge(rr_ready, roots[0])

            def post(group):
                out = []
                if group == G_KV:
                    out.append(angles)
                    heads = lambda a: a[:, :, 0:128].rearrange("p t (h d) -> p t h d", h=AKV)
                    split = lambda a: a.rearrange("p (t h) -> p t h", t=TT)

                    def squares():
                        dve.wait_ge(t_square, 1)
                        mean_squares([(heads(T), 0, 16, AD), (T[:, :, 256:512], 16, 24, BKVR)])
                        rooted()

                    out.append(squares)
                    out.append(lambda: do(v.tensor_tensor(heads(S), heads(S), split(rr[:, 0:16]).unsqueeze(3)
                                                          .to_broadcast([P, TT, AKV, AD]), ALU.mult)))
                    out.append(lambda: do(v.tensor_tensor(S[:, :, 256:512], S[:, :, 256:512], rr[:, 16:24].unsqueeze(2)
                                                          .to_broadcast([P, TT, BKVR]), ALU.mult)))
                    out.append(lambda: (dve.wait_ge(trig_ready, 2), tables(g_ak)))
                    tmp = T[:, :, 256:256 + 64].rearrange("p t (h d) -> p t h d", h=AKV)
                    for k in range(6):
                        out.append(lambda k=k: rotary(heads(S), heads(T), AKV, k, tmp))
                    out.append(lambda: do(v.tensor_copy(T[:, :, 128:256], S[:, :, 128:256])))

                    def finish():
                        return (v.tensor_tensor(T[:, :, 256:512], S[:, :, 256:512],
                                           g_ckv[:].unsqueeze(1).to_broadcast([P, TT, BKVR]), ALU.mult))
                elif group in (G_AQ0, G_AQ1):
                    heads = lambda a: a.rearrange("p t (h d) -> p t h d", h=8)
                    flat = lambda a: a.rearrange("p t (h d) -> p (t h) d", h=8)

                    def squares():
                        dve.wait_ge(t_square, group + 1)
                        mean_squares([(flat(T[:]), 0, 64, AD)])
                        rooted()

                    out.append(squares)
                    out.append(lambda: do(v.tensor_tensor(flat(S[:]), flat(S[:]), rr[:].unsqueeze(2).to_broadcast([P, 64, AD]),
                                                          ALU.mult)))
                    out.append(lambda: tables(g_aq))
                    x1, x2 = heads(S[:])[:, :, :, 0:32], heads(S[:])[:, :, :, 32:64]
                    d1, d2 = heads(T[:])[:, :, :, 0:32], heads(T[:])[:, :, :, 32:64]
                    table = lambda i: tab[:, i].unsqueeze(2).to_broadcast([P, TT, 8, 32])
                    out.append(lambda: do(v.tensor_tensor(d2, x2, table(1), ALU.mult)))
                    out.append(lambda: do(v.tensor_tensor(d1, x1, table(0), ALU.mult)))
                    out.append(lambda: do(v.tensor_tensor(d1, d1, d2, ALU.subtract)))
                    out.append(lambda: do(v.tensor_tensor(d2, x2, table(2), ALU.mult)))
                    out.append(lambda: do(v.tensor_tensor(x1, x1, table(3), ALU.mult)))

                    def finish():
                        return (v.tensor_tensor(d2, d2, x1, ALU.add))
                elif group in (G_CQ, G_MQ):
                    n, width, gain = (TT, BQR, g_cq) if group == G_CQ else (4 * TT, MD, g_mq)
                    flat = lambda a: a.rearrange("p t (h d) -> p (t h) d", d=width)

                    def squares():
                        dve.wait_ge(t_square, group + 1)
                        mean_squares([(flat(T[:]), 0, n, width)])
                        rooted()

                    out.append(squares)
                    out.append(lambda: do(v.tensor_tensor(flat(S[:]), flat(S[:]), rr[:, 0:n].unsqueeze(2)
                                                          .to_broadcast([P, n, width]), ALU.mult)))

                    def finish():
                        return (v.tensor_tensor(flat(T[:]), flat(S[:]), gain[:].unsqueeze(1).to_broadcast([P, n, width]),
                                           ALU.mult))
                else:
                    out.append(lambda: (dve.wait_ge(t_square, group + 1),
                                        do(v.tensor_scalar(T[:], T[:], 1.0, None, ALU.add))))
                    out.append(lambda: do(v.reciprocal(T[:], T[:])))

                    def finish():
                        return (v.tensor_tensor(T[:], T[:], S[:], ALU.mult))

                out.append(lambda: (finish().then_inc(t_ready, 1), dve.wait_ge(t_ready, group + 1)))
                return out

            def gate_out(group):
                dve.wait_ge(t_ready, group)
                for b in range(8):
                    if b < 7:
                        dve.wait_ge(acc_done, 7 * group + b + 1)
                    else:
                        dve.wait_ge(w_used, CPG * (group + 1))
                    half = b % 2
                    v.tensor_tensor(S[:, b, :], ps[:, b, :], rs_row[:, half * HALF:(half + 1) * HALF], ALU.mult
                                    ).then_inc(acc_free, 1)
                dve.wait_ge(acc_free, 8 * (group + 1))

            for group in range(1, NTOK + 1):
                todo = post(group - 1)
                count = CPG if group < NTOK else 1
                each = -(-len(todo) // (CPG - 1))
                for c in range(count):
                    low(CPG * group + c)
                    if c == 0 and group - 1 >= G_GATE0:
                        gate_out(group - 1)
                    if c >= 1:
                        for _ in range(each):
                            if todo:
                                todo.pop(0)()
                for f in todo:
                    f()

            dve.wait_ge(kr_back, 1)
            k_in = S[:, 4, :].rearrange("p (t d) -> p t d", t=TT)
            v.tensor_tensor(k_in, ps[:, 2, :].rearrange("p (t d) -> p t d", t=TT),
                            rs_col[:].unsqueeze(2).to_broadcast([P, TT, BR]), ALU.mult).then_inc(kr_nat, 1)
            dve.wait_ge(kr_sq, 1)
            mean_squares([(S[:, 5, :].rearrange("p (t d) -> p t d", t=TT), 0, 8, BR)])
            tables(g_kr)
            rooted()
            do(v.tensor_tensor(k_in, k_in, rr[:, 0:8].unsqueeze(2).to_broadcast([P, TT, BR]), ALU.mult))
            k_in4 = S[:, 4, :].rearrange("p (t h d) -> p t h d", t=TT, h=1)
            k_two = S[:, 2:4, :].rearrange("p a (t h d) -> p (a t) h d", h=2, d=BR)
            for k in range(6):
                rotary(k_in4, k_two[:, :, 0:1, :], 1, k, S[:, 6, 0:256].rearrange("p (t h d) -> p t h d", t=TT, h=1))
            v.tensor_copy(k_two[:, :, 1:2, :], k_two[:, :, 0:1, :]).then_inc(kr_norm, 1)

            dve.wait_ge(t_square, NTOK + 1)
            v.tensor_reduce(S[:, 7, 0:NMEM], T[:].rearrange("p a n -> p (a n)").rearrange("p (k s) -> p s k", k=KT),
                            X, ALU.add).then_inc(sum_ready, 1)
            v.tensor_tensor(mem_raw[:], mem_raw[:], g_mem[:].unsqueeze(2).to_broadcast([P, KT, NMEM]), ALU.mult
                            ).then_inc(mem_scaled, 1)
            dve.wait_ge(mem_scaled, 1)
            dve.wait_ge(m_hi_ready, 1)
            v.tensor_tensor(m_lo[:], mem_raw[:], m_hi[:].bitcast(F32), ALU.subtract).then_inc(m_lo_ready, 1)
            low(CH_MEM)
            low(CH_MEM + 1)
            dve.wait_ge(up_hi, 2)
            v.tensor_tensor(uq_lo[:], uq_raw[:], uq_hi[:].bitcast(F32), ALU.subtract).then_inc(up_lo, 1)
            v.tensor_tensor(ukv_lo[:], ukv_raw[:], ukv_hi[:].bitcast(F32), ALU.subtract).then_inc(up_lo, 1)
            for n in range(CH_MEM + 2, CH_MEM + CPG + 2):
                low(n)
            for m in range(2):
                if m == 0:
                    heads = lambda a: a[:, 0:2, :].rearrange("p t (h d) -> p (t h) d", d=MD)
                    dve.wait_ge(t_square, NTOK + 2)
                    mean_squares([(heads(T), 0, 8, MD)])
                    rooted()
                    do(v.tensor_tensor(heads(S), heads(S), rr[:, 0:8].unsqueeze(2).to_broadcast([P, 8, MD]), ALU.mult))
                    ins = v.tensor_tensor(heads(T), heads(S), g_mk[:].unsqueeze(1).to_broadcast([P, 8, MD]), ALU.mult)
                else:
                    dve.wait_ge(mem_free, 4)
                    dve.wait_ge(t_stored, 16 * (NTOK + 1))
                    ins = v.tensor_copy(T[:, 0:2, :], S[:, 0:2, :])
                ins.then_inc(t_ready, 1)
                if m == 0:
                    for n in range(CH_MEM + CPG + 2, CH_OUT):
                        low(n)

            tables(g_qr)

            def up_in(t):
                dve.wait_ge(u_chi, t + 1)
                v.tensor_tensor(c_lo[:].rearrange("p k s -> p (k s)"),
                                ps[:, 0:2, :].rearrange("p a n -> p (a n)")[:, 0:768],
                                c_hi[:].rearrange("p k s -> p (k s)").bitcast(F32), ALU.subtract).then_inc(u_clo, 1)

            up_in(0)
            for t in range(TT):
                if t + 1 < TT:
                    up_in(t + 1)
                nope = lambda a: a[:, 0:1024].rearrange("p (h d) -> p h d", d=BN)
                rope = lambda a: a[:, 1024:1280].rearrange("p (h d) -> p h d", d=BR)
                dve.wait_ge(u_sq, t + 1)
                steps.did(v.tensor_reduce(ss[:, 0:8], nope(u_fin), X, ALU.add))
                steps.did(v.tensor_reduce(ss[:, 8:12], rope(u_fin), X, ALU.add))
                steps.settle()
                steps.did(v.tensor_scalar(ss[:, 0:8], ss[:, 0:8], 1.0 / BN, EPS, ALU.mult, ALU.add))
                steps.settle()
                v.tensor_scalar(ss[:, 8:12], ss[:, 8:12], 1.0 / BR, EPS, ALU.mult, ALU.add).then_inc(u_ms, 1)
                dve.wait_ge(u_rr, t + 1)
                steps.did(v.tensor_tensor(nope(u_out), nope(u_out), rr[:, 0:8].unsqueeze(2).to_broadcast([P, 8, BN]),
                                          ALU.mult))
                steps.did(v.tensor_tensor(rope(u_out), rope(u_out), rr[:, 8:12].unsqueeze(2).to_broadcast([P, 4, BR]),
                                          ALU.mult))
                steps.settle()
                for k, gain in enumerate((g_qn, g_kn)):
                    part = lambda a: a[:, 512 * k:512 * (k + 1)].rearrange("p (h d) -> p h d", d=BN)
                    steps.did(v.tensor_tensor(part(u_fin), part(u_out), gain[:].unsqueeze(1).to_broadcast([P, BH, BN]),
                                              ALU.mult))
                x1, x2 = rope(u_out)[:, :, 0:32], rope(u_out)[:, :, 32:64]
                d1, d2 = rope(u_fin)[:, :, 0:32], rope(u_fin)[:, :, 32:64]
                table = lambda i: tab[:, i, t, :].unsqueeze(1).to_broadcast([P, BH, 32])
                steps.did(v.tensor_tensor(d1, x1, table(0), ALU.mult))
                steps.did(v.tensor_tensor(u_tmp[:, 0], x2, table(1), ALU.mult))
                steps.did(v.tensor_tensor(d2, x2, table(2), ALU.mult))
                steps.did(v.tensor_tensor(u_tmp[:, 1], x1, table(3), ALU.mult))
                steps.settle()
                steps.did(v.tensor_tensor(d1, d1, u_tmp[:, 0], ALU.subtract))
                v.tensor_tensor(d2, d2, u_tmp[:, 1], ALU.add).then_inc(u_done, 1)
                dve.wait_ge(u_kn, t + 1)
                v.tensor_copy(knT[:, :, t * P:(t + 1) * P], ps[:, 7, :].rearrange("p (h s) -> p h s", h=BH)
                              ).then_inc(u_kn_kept, 1)

            do(v.tensor_scalar(sinks[:], sinks[:], 1.0 / SCALE_A, None, ALU.mult))

            def a_first(c, par, first, pad=False):
                dve.wait_ge(A.k_turned, c + 1)
                if not first:
                    dve.wait_ge(A.scored, c - 1)
                v.tensor_copy(a_kT[:, par, :], ps[:, 1, 0:P]).then_inc(A.kT, 1)
                dve.wait_ge(A.scored, c + 1)
                sc = ps[:, 2 + 2 * par:4 + 2 * par, :].rearrange("p a (g k) -> p (a g) k", k=P)
                if pad:
                    do(v.memset(sc[:, :, 0:CHUNK], -BIG))
                do(v.tensor_reduce(st[:, par, 0, :], sc, X, ALU.max))
                do(v.tensor_tensor(st[:, par, 0, :], st[:, par, 0, :], sinks[:], ALU.max))
                do(v.tensor_tensor(st[:, par, 1, :], sinks[:], st[:, par, 0, :], ALU.subtract))
                if not first:
                    dve.wait_ge(A.p_turned, c - 1)
                v.tensor_tensor(a_p[:, par], sc, st[:, par, 0, :].unsqueeze(2).to_broadcast([P, 8, P]), ALU.subtract
                                ).then_inc(A.shifted, 1)

            def a_second(c, par):
                dve.wait_ge(A.exp, 2 * c + 2)
                do(v.tensor_reduce(st[:, par, 2, :], a_p[:, par], X, ALU.add))
                do(v.tensor_tensor(st[:, par, 2, :], st[:, par, 2, :], st[:, par, 1, :], ALU.add))
                do(v.reciprocal(st[:, par, 3, :], st[:, par, 2, :]))
                v.tensor_tensor(a_p[:, par], a_p[:, par], st[:, par, 3, :].unsqueeze(2).to_broadcast([P, 8, P]), ALU.mult
                                ).then_inc(A.p, 1)
                dve.wait_ge(A.pv, c + 1)
                v.tensor_tensor(mixed[:, 0:AJ, bass.ds(c * CHUNK, CHUNK)], ps[:, 1, :].rearrange("p (j s) -> p j s", j=AJ),
                                a_gate[:, par], ALU.mult).then_inc(A.gated, 1)

            def a_pair(i, first, last):
                c = 2 * i
                a_first(c + 1, 1, first)
                a_second(c, 0)
                if not last:
                    a_first(c + 2, 0, False)
                a_second(c + 1, 1)

            a_first(0, 0, True, pad=True)
            pipelined(dve, NCHUNK // 2, a_pair, [steps])

            def b_first(s):
                h, t = BSTEPS[s]
                width, par = (t + 1) * P, s % 2
                sc = ps[:, 2 + 2 * par:4 + 2 * par, :].rearrange("p a n -> p (a n)")
                dve.wait_ge(B.scored, s + 1)
                do(v.memset(sc[0:CHUNK, width - CHUNK:width], -BIG))
                do(v.tensor_reduce(st[:, par, 0, 0:1], sc[:, 0:width], X, ALU.max))
                v.tensor_scalar(st[:, par, 1, 0:1], st[:, par, 0, 0:1], -SCALE_B, None, ALU.mult).then_inc(B.shifted, 1)

            def b_second(s):
                h, t = BSTEPS[s]
                width, par = (t + 1) * P, s % 2
                dve.wait_ge(B.exp, s + 1)
                do(v.reciprocal(st[:, par, 3, 0:1], st[:, par, 2, 0:1]))
                v.tensor_scalar(b_p[:, par, 0:width], b_p[:, par, 0:width], st[:, par, 3, 0:1], None, ALU.mult
                                ).then_inc(B.p, 1)
                dve.wait_ge(B.pv, s + 1)
                dve.wait_ge(B.loaded[h % 2], 16 * (h // 2 + 1))
                v.tensor_tensor(mixed[:, AJ + h, t * P:(t + 1) * P], ps[:, par, 0:P], b_gate[:, h % 2, t * P:(t + 1) * P],
                                ALU.mult).then_inc(B.gated, 1)

            b_first(0)
            for s in range(len(BSTEPS)):
                if s + 1 < len(BSTEPS):
                    b_first(s + 1)
                b_second(s)

            def m_first(t, par, first):
                dve.wait_ge(M.scored, t + 1)
                sc = ps[:, 2 + 2 * par:4 + 2 * par, :].rearrange("p a (g k) -> p (a g) k", k=NMEM)
                do(v.tensor_reduce(st[:, par, 0, 0:MH], sc, X, ALU.max))
                if not first:
                    dve.wait_ge(M.p_turned, t - 1)
                v.tensor_tensor(c_p[:, par], sc, st[:, par, 0, 0:MH].unsqueeze(2).to_broadcast([P, MH, NMEM]),
                                ALU.subtract).then_inc(M.shifted, 1)

            def m_second(t, par, k):
                dve.wait_ge(M.exp, t + 1)
                do(v.tensor_reduce(st[:, par, 2, 0:MH], c_p[:, par], X, ALU.add))
                do(v.reciprocal(st[:, par, 3, 0:MH], st[:, par, 2, 0:MH]))
                v.tensor_tensor(c_p[:, par], c_p[:, par], st[:, par, 3, 0:MH].unsqueeze(2).to_broadcast([P, MH, NMEM]),
                                ALU.mult).then_inc(M.p, 1)
                dve.wait_ge(M.pv, t + 1)
                v.tensor_tensor(mixed[:, AJ + BH:KT, bass.ds(t * P, P)], ps[:, 1, :].rearrange("p (j s) -> p j s", j=MH),
                                c_gate[:, par], ALU.mult).then_inc(M.gated, 1)

            def m_pair(i, first, last):
                t = 2 * i
                m_first(t + 1, 1, first)
                m_second(t, 0, 0)
                if not last:
                    m_first(t + 2, 0, False)
                m_second(t + 1, 1, 1)

            m_first(0, 0, True)
            pipelined(dve, TT // 2, m_pair, [steps])

            dve.wait_ge(M.gated, TT)

            def add_residual(og):
                buf = (S, T)[og % 2]
                dve.wait_ge(res_loaded[og % 2], 16 * (og // 2 + 1))
                for t in range(TT):
                    if t < TT - 1:
                        dve.wait_ge(acc_done, (TT - 1) * (NTOK + og) + t + 1)
                    else:
                        dve.wait_ge(w_used, CH_OUT + CPG * (og + 1))
                    v.tensor_tensor(buf[:, t, :], ps[:, t, :], buf[:, t, :], ALU.add).then_inc(acc_free, 1)

            for c in range(CPG):
                for k in (2 * c, 2 * c + 1):
                    dve.wait_ge(h_hi_ready, KT + k + 1)
                    v.tensor_tensor(h_lo[:, k, :], mixed[:, k, :], h_hi[:, k, :].bitcast(F32), ALU.subtract
                                    ).then_inc(h_lo_ready, 1)
                low(CH_OUT + c)
            for n in range(CH_OUT + CPG, NCH):
                low(n)
                if (n - CH_OUT) % CPG == 0:
                    add_residual((n - CH_OUT) // CPG - 1)
            add_residual(OUT_GROUPS - 1)

        @block.tensor
        def _(pe):
            mm = nc.tensor.matmul

            def three(out, a_hi, a_lo, b_hi, b_lo, start, stop):
                mm(out, a_hi, b_hi, start=start, stop=False)
                mm(out, a_hi, b_lo, start=False, stop=False)
                return mm(out, a_lo, b_hi, start=False, stop=stop)

            def token_group(g, n0, tok_parts=None, gates=False, slot0=0):
                for c in range(CPG):
                    slot, n = (slot0 + c) % SPLIT, n0 + c
                    pe.wait_ge(lo_ready, n + 1)
                    for kk in range(2):
                        k = 2 * c + kk
                        if tok_parts is not None:
                            pe.wait_ge(h_lo_ready, tok_parts + k + 1)
                        for b in range(8):
                            if k == 0:
                                wait(pe, acc_free, g * 8 + (b - 7))
                            w = slice(kk * HALF, (kk + 1) * HALF)
                            if gates:
                                ct, half = b // 2, b % 2
                                col = slice(kk * HALF + ct * P, kk * HALF + (ct + 1) * P)
                                tok = slice(half * HALF, (half + 1) * HALF)
                                ins = three(ps[:, b, :], w_hi[:, slot, col], w_lo[:, slot, col],
                                            h_hi[:, k, tok], h_lo[:, k, tok], k == 0, k == KT - 1)
                            else:
                                tok = slice(b * P, (b + 1) * P)
                                ins = three(ps[:, b, :], h_hi[:, k, tok], h_lo[:, k, tok],
                                            w_hi[:, slot, w], w_lo[:, slot, w], k == 0, k == KT - 1)
                            if k == KT - 1 and b < 7:
                                ins.then_inc(acc_done, 1)
                    ins.then_inc(w_used, 1)

            token_group(0, 0, tok_parts=0)
            with pe.Fori(1, G_GATE0) as g:
                token_group(g, g * CPG)
            with pe.Fori(G_GATE0, NTOK) as g:
                token_group(g, g * CPG, gates=True)

            pe.wait_ge(lo_ready, CH_KR + 1)
            slot = CH_KR % SPLIT
            pe.wait_ge(acc_free, 8 * NTOK)
            for half in range(2):
                tok = slice(half * HALF, (half + 1) * HALF)
                for k in range(KT):
                    w = slice(k * BR, (k + 1) * BR)
                    ins = three(ps[0:BR, half, :], w_hi[:, slot, w], w_lo[:, slot, w], h_hi[:, k, tok], h_lo[:, k, tok],
                                k == 0, k == KT - 1)
            ins.then_inc(w_used, 1)
            turn = nc.tensor.transpose
            pe.wait_ge(pool_consts, 1)
            pe.wait_ge(kr_raw, 1)
            kr_in = S[0:BR, 0:2, :].rearrange("p a n -> p (a n)")
            for t in range(TT):
                ins = turn(ps[:, 2, t * BR:(t + 1) * BR], kr_in[:, t * P:(t + 1) * P], ident[0:BR, 0:BR])
            ins.then_inc(kr_back, 1)
            pe.wait_ge(kr_norm, 1)
            for t in range(TT):
                ins = turn(ps[:, 3 + t // 4, t % 4 * P:(t % 4 + 1) * P], S[:, 2 + t // 4, t % 4 * P:(t % 4 + 1) * P], ident[:])
            ins.then_inc(kr_turned, 1)

            pe.wait_ge(m_lo_ready, 1)
            for m in range(2):
                for c in range(CPG):
                    n = CH_MEM + CPG * m + c
                    pe.wait_ge(lo_ready, n + 1)
                    for kk in range(2):
                        k = 2 * c + kk
                        for t in range(2):
                            if k == 0:
                                wait(pe, mem_free, 2 * (m - 1) + t + 1 if m else 0)
                            tok, w = slice(t * P, (t + 1) * P), slice(kk * HALF, (kk + 1) * HALF)
                            ins = three(ps[:, 5 + t, :], m_hi[:, k, tok], m_lo[:, k, tok], w_hi[:, n % SPLIT, w],
                                        w_lo[:, n % SPLIT, w], k == 0, k == KT - 1)
                            if k == KT - 1 and t == 0:
                                ins.then_inc(mem_done, 1)
                    ins.then_inc(w_used, 1)

            def up(t):
                pe.wait_ge(u_loaded[t % 2], 32 * (t // 2 + 1))
                if t == 0:
                    pe.wait_ge(kr_kept, 1)
                    pe.wait_ge(up_lo, 2)
                    pe.wait_ge(mem_free, 4)
                wait(pe, u_clo, t)
                for k in range(6):
                    ins = turn(ps[:, k // 4, k % 4 * P:(k % 4 + 1) * P], u_in[:, t % 2, k * P:(k + 1) * P], ident[:])
                ins.then_inc(u_turned, 1)
                pe.wait_ge(u_clo, t + 1)
                wait(pe, u_ev, 2 * t)
                for k in range(4):
                    for bank, a, b in ((2, 0, 512), (4, 512, 768)):
                        three(ps[:, bank, 0:b - a], c_hi[:, k, :], c_lo[:, k, :], uq_hi[:, k, a:b], uq_lo[:, k, a:b],
                              k == 0, k == 3)
                for k in range(2):
                    for bank, a, b in ((3, 0, 512), (5, 512, 1024)):
                        ins = three(ps[:, bank, :], c_hi[:, 4 + k, :], c_lo[:, 4 + k, :], ukv_hi[:, k, a:b],
                                    ukv_lo[:, k, a:b], k == 0, k == 1)
                ins.then_inc(u_up, 1)

            up(0)
            for t in range(TT):
                if t + 1 < TT:
                    up(t + 1)
                pe.wait_ge(u_done, t + 1)
                wait(pe, u_qr_kept, t)
                for h in range(BH):
                    ins = turn(ps[:, 6, h * P:(h + 1) * P], u_fin[:, h * P:(h + 1) * P], ident[:])
                ins.then_inc(u_qn, 1)
                wait(pe, u_kn_kept, t)
                for h in range(BH):
                    ins = turn(ps[:, 7, h * P:(h + 1) * P], u_fin[:, 512 + h * P:512 + (h + 1) * P], ident[:])
                ins.then_inc(u_kn, 1)
                pe.wait_ge(u_qn_kept, t + 1)
                for h in range(2):
                    ins = turn(ps[:, 6, h * P:(h + 1) * P], u_fin[:, 1024 + h * P:1024 + (h + 1) * P], ident[:])
                ins.then_inc(u_qr, 1)

            def a_first(c, par, i, first):
                pe.wait_ge(A.loaded[par], 48 * (i + 1))
                if not first:
                    pe.wait_ge(A.qT, c)
                    pe.wait_ge(A.gated, c - 1)
                    pe.wait_ge(A.kT, c)
                turn(ps[:, 1, 0:P], a_kv[:, par, 0:P], ident[:]).then_inc(A.k_turned, 1)
                for j in range(AJ):
                    ins = turn(ps[:, 0, j * CHUNK:(j + 1) * CHUNK], a_q[:, par, j * P:(j + 1) * P], ident[0:CHUNK, 0:CHUNK])
                ins.then_inc(A.q_turned, 1)
                pe.wait_ge(A.qT, c + 1)
                pe.wait_ge(A.kT, c + 1)
                if not first:
                    pe.wait_ge(A.shifted, c - 1)
                for g in range(AKV):
                    rows = slice(64 * g, 64 * g + 64)
                    for jp in range(AJ // 2):
                        ins = mm(ps[:, 2 + 2 * par + g, jp * P:(jp + 1) * P],
                                 a_qT[rows, par, 2 * jp:2 * jp + 2, :].rearrange("p j s -> p (j s)"), a_kT[rows, par, :],
                                 start=True, stop=True)
                ins.then_inc(A.scored, 1)

            def a_second(c, par, first, last):
                pe.wait_ge(A.p, c + 1)
                if not first:
                    pe.wait_ge(A.pT, 2 * c)
                for g in range(AKV):
                    for jp in range(AJ // 2):
                        ins = turn(ps[:, 6 + g, jp * P:(jp + 1) * P], a_p[:, par, 4 * g + jp, :], ident[:])
                ins.then_inc(A.p_turned, 1)
                pe.wait_ge(A.pT, 2 * c + 2)
                if not last:
                    pe.wait_ge(A.kT, c + 2)
                if not first:
                    pe.wait_ge(A.gated, c)
                for g in range(AKV):
                    rows = slice(64 * g, 64 * g + 64)
                    ins = mm(ps[rows, 1, :], a_kv[:, par, P + 64 * g:P + 64 * g + 64], a_pT[:, g, :], start=True, stop=True)
                ins.then_inc(A.pv, 1)

            def a_pair(i, first, last):
                c = 2 * i
                a_first(c + 1, 1, i, first)
                a_second(c, 0, first, False)
                if not last:
                    a_first(c + 2, 0, i + 1, False)
                a_second(c + 1, 1, False, last)

            a_first(0, 0, 0, True)
            pipelined(pe, NCHUNK // 2, a_pair)

            pe.wait_ge(A.gated, NCHUNK)

            def b_first(s):
                h, t = BSTEPS[s]
                width, par = (t + 1) * P, s % 2
                if s == 0:
                    pe.wait_ge(u_qr_kept, TT)
                    pe.wait_ge(u_kn_kept, TT)
                wait(pe, B.exp, s - 1)
                q, r = slice(t * P, (t + 1) * P), slice(64 * (h % 2), 64 * (h % 2) + 64)
                for a in range(0, width, HALF):
                    b = min(width, a + HALF)
                    out = ps[:, 2 + 2 * par + a // HALF, 0:b - a]
                    mm(out, qnT[:, h, q], knT[:, h, a:b], start=True, stop=False)
                    ins = mm(out, qrT[r, h // 2, q], krT[r, a:b], start=False, stop=True)
                ins.then_inc(B.scored, 1)

            def b_second(s):
                h, t = BSTEPS[s]
                par = s % 2
                pe.wait_ge(B.p, s + 1)
                wait(pe, B.pT, s)
                for k in range(t + 1):
                    ins = turn(ps[:, 6 + k // 4, k % 4 * P:(k % 4 + 1) * P], b_p[:, par, k * P:(k + 1) * P], ident[:])
                ins.then_inc(B.p_turned, 1)
                pe.wait_ge(B.pT, s + 1)
                wait(pe, B.gated, s - 1)
                for k in range(t + 1):
                    ins = mm(ps[:, par, 0:P], vB[:, k, h * BV:(h + 1) * BV], b_pT[:, k * P:(k + 1) * P],
                             start=(k == 0), stop=(k == t))
                ins.then_inc(B.pv, 1)

            b_first(0)
            for s in range(len(BSTEPS)):
                if s + 1 < len(BSTEPS):
                    b_first(s + 1)
                b_second(s)

            pe.wait_ge(B.gated, len(BSTEPS))
            pe.wait_ge(km_loaded, 16)
            for h in range(MH):
                for t in range(2):
                    i = 2 * h + t
                    ins = turn(ps[:, 6 + i // 4, i % 4 * P:(i % 4 + 1) * P], c_km[:, t, h * P:(h + 1) * P], ident[:])
            ins.then_inc(km_turned, 1)
            pe.wait_ge(km_kept, 1)
            pe.wait_ge(vm_loaded, 16)

            def m_first(t, par, i, first):
                pe.wait_ge(M.loaded[par], 32 * (i + 1))
                if not first:
                    pe.wait_ge(M.qT, t)
                for j in range(MH):
                    ins = turn(ps[:, 0, j * P:(j + 1) * P], c_q[:, par, j * P:(j + 1) * P], ident[:])
                ins.then_inc(M.q_turned, 1)
                pe.wait_ge(M.qT, t + 1)
                if not first:
                    pe.wait_ge(M.shifted, t - 1)
                for h in range(MH):
                    ins = mm(ps[:, 2 + 2 * par + h // 2, h % 2 * NMEM:(h % 2 + 1) * NMEM], c_qT[:, par, h, :], kmT[:, h, :],
                             start=True, stop=True)
                ins.then_inc(M.scored, 1)

            def m_second(t, par, first):
                pe.wait_ge(M.p, t + 1)
                if not first:
                    pe.wait_ge(M.pT, 2 * t)
                for kb in range(2):
                    for h in range(MH):
                        ins = turn(ps[:, 6 + kb, h * P:(h + 1) * P], c_p[:, par, h, kb * P:(kb + 1) * P], ident[:])
                ins.then_inc(M.p_turned, 1)
                pe.wait_ge(M.pT, 2 * t + 2)
                if not first:
                    pe.wait_ge(M.gated, t)
                for h in range(MH):
                    for kb in range(2):
                        ins = mm(ps[:, 1, h * P:(h + 1) * P], vM[:, kb, h * MD:(h + 1) * MD], c_pT[:, kb, h * P:(h + 1) * P],
                                 start=(kb == 0), stop=(kb == 1))
                ins.then_inc(M.pv, 1)

            def m_pair(i, first, last):
                t = 2 * i
                m_first(t + 1, 1, i, first)
                m_second(t, 0, first)
                if not last:
                    m_first(t + 2, 0, i + 1, False)
                m_second(t + 1, 1, False)

            m_first(0, 0, 0, True)
            pipelined(pe, TT // 2, m_pair)

            pe.wait_ge(M.gated, TT)
            token_group(NTOK, CH_OUT, tok_parts=KT, slot0=CH_OUT % SPLIT)
            with pe.Fori(1, OUT_GROUPS) as og:
                token_group(og + NTOK, og * CPG + CH_OUT, slot0=CH_OUT % SPLIT)


def kernel(x, mem, positions, g_in, w_in, a_g_q, a_g_k, a_sinks, b_g_cq, b_w_q_up, b_g_ckv, b_w_kv_up, b_g_q_nope,
           b_g_q_rope, b_g_k_nope, b_g_k_rope, m_g_mem, m_w_kv, m_g_q, m_g_k, w_o):
    import concourse.bacc as bacc
    from concourse.bass_utils import run_bass_kernel_spmd

    f = lambda a: np.ascontiguousarray(np.asarray(a))
    tiles = lambda a: a.reshape(-1, P, a.shape[-1])
    x0, mem0 = f(x)[0], f(mem)[0]
    w = f(w_in)[0]
    cuts = np.cumsum([AH * AD, AKV * AD, AKV * AD, AH * AD, BQR, BKVR, BR, BH * BV, MH * MD, MH * MD])
    aq, ak, av, ag, cq, ckv, kr, bg, mq, mg = np.split(w, cuts[:-1], axis=1)
    paired = lambda a: a.reshape(a.shape[0], AKV, AJ, AD).transpose(0, 2, 1, 3).reshape(a.shape[0], -1)
    wo = f(w_o)[0]
    wo = np.concatenate([paired(wo[:AH * AD].T).T, wo[AH * AD:]], 0)

    def chunks(a):
        a = a.reshape(CPG, 2, P, -1, HALF)
        return a.transpose(3, 0, 2, 1, 4).reshape(-1, P, 2 * HALF)

    front = np.concatenate([ak, av, ckv, cq, paired(aq), mq, paired(ag), bg, mg], 1)
    stream = np.concatenate([
        chunks(front),
        kr.reshape(KT, P, BR).transpose(1, 0, 2).reshape(1, P, KT * BR),
        chunks(f(m_w_kv)[0]),
        chunks(wo),
    ], 0)
    assert stream.shape[0] == NCH
    q_up = f(b_w_q_up)[0].reshape(BQR, BH, BN + BR)
    q_up = np.concatenate([q_up[:, :, :BN].reshape(BQR, -1), q_up[:, :, BN:].reshape(BQR, -1)], 1)
    kv_up = f(b_w_kv_up)[0].reshape(BKVR, BH, BN + BV)
    kv_up = np.concatenate([kv_up[:, :, :BN].reshape(BKVR, -1), kv_up[:, :, BN:].reshape(BKVR, -1)], 1)
    arrays = {
        "w": stream, "xT": tiles(x0.T), "memT": tiles(mem0.T), "x": x0,
        "w_q_up": tiles(q_up), "w_kv_up": tiles(kv_up),
        "g_in": f(g_in)[0].reshape(KT, P).T, "m_g_mem": f(m_g_mem)[0].reshape(KT, P).T,
        "positions": f(positions)[0].reshape(TT, P).T.astype(np.int32),
        "sinks": f(a_sinks)[0].reshape(AJ, 2).T,
        "invf": (10000.0 ** (-np.arange(0, AD, 2, dtype=np.float64) / AD)).astype(np.float32)[None],
        "a_g_q": f(a_g_q), "a_g_k": f(a_g_k), "b_g_cq": f(b_g_cq), "b_g_ckv": f(b_g_ckv),
        "b_g_q_nope": f(b_g_q_nope), "b_g_q_rope": f(b_g_q_rope), "b_g_k_nope": f(b_g_k_nope),
        "b_g_k_rope": f(b_g_k_rope), "m_g_q": f(m_g_q), "m_g_k": f(m_g_k),
    }
    nc = bacc.Bacc("TRN2", target_bir_lowering=False, num_devices=1)
    sent, io = {}, {}
    for name, a in arrays.items():
        a = np.ascontiguousarray(a)
        sent[f"in_{name}"] = a
        io[name] = nc.dram_tensor(f"in_{name}", a.shape, mybir.dt.from_np(a.dtype), kind="ExternalInput").ap()
    io["y"] = nc.dram_tensor("out_y", (SEQ, D), F32, kind="ExternalOutput").ap()
    layer(nc, io)
    r = run_bass_kernel_spmd(nc, [sent], core_ids=[0])
    return r.results[0]["out_y"].reshape(1, SEQ, D)
```

```python
from contextlib import ExitStack

import concourse.bass as bass
import numpy as np
from concourse import mybir

F32 = mybir.dt.float32
F32R = mybir.dt.float32r
I32 = mybir.dt.int32
ALU = mybir.AluOpType
ACT = mybir.ActivationFunctionType
X = mybir.AxisListType.X

P = 128
D = 2048
SEQ = 1024
KT = D // P
TT = SEQ // P
HALF = 512
NMEM = 256
CHUNK = 64
NCHUNK = SEQ // CHUNK
AH, AKV, AD = 16, 2, 64
AJ = AH // AKV
BH, BN, BR, BV = 4, 128, 64, 128
BQR, BKVR = 512, 256
MH, MD = 4, 128
EPS = 1e-6
SCALE_A = AD ** -0.5
SCALE_B = (BN + BR) ** -0.5
SCALE_M = MD ** -0.5
BIG = 3.0e38
TWO_PI = 2 * float(np.pi)
PI_BELOW = 3.1415925
ROUND = 1.5 * 2.0 ** 23
_C1 = 6.28125
_C2 = float(np.round((TWO_PI - _C1) * 2.0 ** 20) / 2.0 ** 20)
TWO_PI_PARTS = (_C1, _C2, TWO_PI - _C1 - _C2)

G_KV, G_CQ, G_AQ0, G_AQ1, G_MQ, G_GATE0 = 0, 1, 2, 3, 4, 5
NGATE = 4
G_MEM0 = G_GATE0 + NGATE
CPG = KT // 2
CH_KR = G_MEM0 * CPG
CH_MEM = CH_KR + 1
CH_OUT = CH_MEM + 2 * CPG
NCH = CH_OUT + (D // HALF) * CPG
RAW = 3
SPLIT = 2


def wait(e, sem, value):
    if isinstance(value, int) and value <= 0:
        return
    e.wait_ge(sem, value)


class Steps:

    def __init__(self, engine, sem):
        self.engine, self.sem, self.n = engine, sem, 0

    def did(self, ins):
        ins.then_inc(self.sem, 1)
        self.n = self.n + 1

    def settle(self):
        self.engine.wait_ge(self.sem, self.n)


def pipelined(engine, n, body, steps=(), tail=2):
    before = [s.n for s in steps]
    body(0)
    per = [s.n - b for s, b in zip(steps, before)]
    with engine.Fori(1, n - tail) as i:
        for s, b, k in zip(steps, before, per):
            s.n = i * k + b
        body(i)
    for last in range(n - tail, n):
        for s, b, k in zip(steps, before, per):
            s.n = b + last * k
        body(last)


def below(c, n):
    return c < n if isinstance(c, int) else True


def layer(nc, io):
    with ExitStack() as ctx:
        def sem(name):
            return ctx.enter_context(nc.semaphore(name))

        top = [(nc.sbuf_base + 31) // 32 * 32]

        def region(size):
            at = top[0]
            top[0] += size
            assert top[0] <= nc.sbuf_usable_end, top[0] - nc.sbuf_usable_end
            return at

        def at(name, shape, dt, offset):
            return nc.alloc_sbuf_tensor_at(name, shape, dt, offset=offset)

        R0, R1 = region(KT * SEQ * 4), region(KT * SEQ * 4)
        WRAW = region(RAW * 4096)
        WHI, WLO = region(SPLIT * 4096), region(SPLIT * 4096)
        RS, RT = region(16384), region(16384)

        def small(name, shape, dt=F32):
            size = int(np.prod(shape[1:])) * 4
            return at(name, shape, dt, region((size + 31) // 32 * 32))

        def inside(start, size):
            where = [start]

            def place(name, shape, dt=F32):
                t = at(name, shape, dt, where[0])
                where[0] += int(np.prod(shape[1:])) * 4
                assert where[0] <= start + size, name
                return t
            return place

        h_hi = at("h_hi", [P, KT, SEQ], F32R, R0)
        h_lo = at("h_lo", [P, KT, SEQ], F32R, R1)
        x_raw = at("x_raw", [P, KT, SEQ], F32, R1)
        m_hi = at("m_hi", [P, KT, NMEM], F32R, R0)
        m_lo = at("m_lo", [P, KT, NMEM], F32R, R1)
        mem_raw = at("mem_raw", [P, KT, NMEM], F32, R1)
        m_sq = at("m_sq", [P, KT, NMEM], F32, R0 + 16384)
        m_sums = at("m_sums", [P, NMEM], F32, RS + 8192)
        kr_a = at("kr_a", [BR, SEQ], F32, R0 + 33792)
        kr_b = at("kr_b", [P, TT, 1, BR], F32, R0 + 37888)
        kr_c = at("kr_c", [P, TT, BR], F32, R0 + 39936)
        kr_d = at("kr_d", [P, TT, 2, BR], F32, R0 + 41984)
        kr_t = at("kr_t", [P, TT, 1, 32], F32, R0 + 46080)
        mixed = at("mixed", [P, KT, SEQ], F32, R1)
        w_raw = at("w_raw", [P, RAW, 1024], F32, WRAW)
        w_hi = at("w_hi", [P, SPLIT, 1024], F32R, WHI)
        w_lo = at("w_lo", [P, SPLIT, 1024], F32R, WLO)
        S = at("S", [P, 8, HALF], F32, RS)
        T = at("T", [P, 8, HALF], F32, RT)

        qnT = at("qnT", [P, BH, SEQ], F32, R0)
        knT = at("knT", [P, BH, SEQ], F32, R0 + 16384)
        vB = at("vB", [P, TT, BH * BV], F32, R0 + 32768)
        qrT = at("qrT", [P, BH // 2, SEQ], F32, R0 + 49152)
        krT = at("krT", [P, 2, SEQ], F32, R0 + 57344)

        ident = small("ident", [P, P])
        cos = small("cos", [P, TT, 32])
        sin = small("sin", [P, TT, 32])
        tab_at = top[0]
        tab = small("tab", [P, 4, TT, 32])
        sumsq = at("sumsq", [P, SEQ], F32, RS)
        sum_row = at("sum_row", [P, SEQ], F32, RS + 4096)
        rs_row_at = top[0]
        rs_row = small("rs_row", [P, SEQ])
        rs_col = small("rs_col", [P, TT])
        ms_col = small("ms_col", [P, 2])
        cols = small("cols", [P, 2 * KT + 2])
        g_x, g_mem = cols[:, 0:KT], cols[:, KT:2 * KT]
        g_qn, g_kn = cols[:, 2 * KT:2 * KT + 1], cols[:, 2 * KT + 1:2 * KT + 2]
        row_names = (("a_g_q", AD), ("a_g_k", AD), ("b_g_cq", BQR), ("b_g_ckv", BKVR), ("b_g_q_rope", BR),
                     ("b_g_k_rope", BR), ("m_g_q", MD), ("m_g_k", MD), ("invf", 32))
        row_gains = small("row_gains", [P, sum(n for _, n in row_names)])
        ends = np.cumsum([n for _, n in row_names])
        g_aq, g_ak, g_cq, g_ckv, g_qr, g_kr, g_mq, g_mk, invf = (
            row_gains[:, int(e) - n:int(e)] for e, (_, n) in zip(ends, row_names))
        sinks = small("sinks", [P, AJ])
        posi = small("posi", [P, TT], I32)
        pos = small("pos", [P, TT])
        mhalf = small("mhalf", [P, 1])
        kmT = at("kmT", [P, MH, NMEM], F32, rs_row_at)
        vM = at("vM", [P, 2, MH * MD], F32, tab_at)
        ss = small("ss", [P, 64])
        rr = small("rr", [P, 64])
        st = small("st", [P, 2, 5, 8])

        up_at = inside(R1 + 16384, 40960)
        uq_hi = up_at("uq_hi", [P, 4, 768], F32R)
        uq_raw_at = R1 + 16384 + 12288
        uq_lo = up_at("uq_lo", [P, 4, 768], F32R)
        ukv_hi = up_at("ukv_hi", [P, 2, 1024], F32R)
        ukv_raw_at = R1 + 16384 + 24576 + 8192
        ukv_lo = up_at("ukv_lo", [P, 2, 1024], F32R)
        uq_raw = at("uq_raw", [P, 4, 768], F32, uq_raw_at)
        ukv_raw = at("ukv_raw", [P, 2, 1024], F32, ukv_raw_at)
        u_in = at("u_in", [P, 2, 768], F32, R1 + 57344)
        put = inside(R1, 16384)
        c_hi = put("c_hi", [P, 2, 6, P], F32R)
        c_lo = put("c_lo", [P, 2, 6, P], F32R)
        u_tmp = put("u_tmp", [P, 2, 4, 32])
        u_out = at("u_out", [P, 2, 1280], F32, RS + 4096)
        u_fin = at("u_fin", [P, 2, 1280], F32, RT + 4096)
        put = inside(RS, 32768)
        a_kT = at("a_kT", [P, AKV, SEQ], F32, WLO)
        a_kn = at("a_kn", [P, TT, P], F32, WHI)
        a_q = put("a_q", [CHUNK, 2, AJ * P])
        a_v = put("a_v", [P, 2, P])
        a_gate = put("a_gate", [P, 2, AJ, CHUNK])
        a_qT = put("a_qT", [P, 2, AJ, CHUNK])
        a_pT = put("a_pT", [P, 2, 2 * HALF])
        a_p = at("a_p", [P, 2, 8, P], F32, WHI)
        put = inside(RS, 32768)
        c_q = put("c_q", [P, 2, MH * MD])
        c_gate = put("c_gate", [P, 2, MH, P])
        c_qT = put("c_qT", [P, 2, MH, P])
        c_p = put("c_p", [P, 2, MH, NMEM])
        c_pT = put("c_pT", [P, 2, 2 * HALF])
        c_km = at("c_km", [P, 2, HALF], F32, WHI)
        put = inside(RS, 32768)
        b_p = put("b_p", [P, 2, SEQ])
        b_pT = put("b_pT", [P, 2, SEQ])
        b_gate = put("b_gate", [P, 2, SEQ])

        ps = ctx.enter_context(nc.psum_tensor("ps", [P, 8, HALF], F32))

        def scratch(name, shape):
            return nc.dram_tensor(name, shape, F32, kind="Internal").ap()

        kv_s = scratch("kv_s", [SEQ, HALF])
        cq_s = scratch("cq_s", [SEQ, BQR])
        aq_s = scratch("aq_s", [SEQ, 2, HALF])
        mq_s = scratch("mq_s", [SEQ, HALF])
        gate_s = scratch("gate_s", [KT, P, SEQ])
        km_s = scratch("km_s", [NMEM, HALF])
        vm_s = scratch("vm_s", [NMEM, HALF])
        row_s = scratch("row_s", [3, SEQ])

        w_loaded = [sem(f"w_loaded{i}") for i in range(RAW)]
        hi_ready, lo_ready, w_used = sem("hi_ready"), sem("lo_ready"), sem("w_used")
        x0_loaded = [sem(f"x0_loaded{i}") for i in range(2)]
        x_loaded = [sem(f"x_loaded{i}") for i in range(KT // 2)]
        h_hi_ready, h_lo_ready = sem("h_hi_ready"), sem("h_lo_ready")
        sq_ready, sq_used, sum_ready = sem("sq_ready"), sem("sq_used"), sem("sum_ready")
        row_stored, col_loaded, col_ready = sem("row_stored"), sem("col_loaded"), sem("col_ready")
        rs_stored, rs_row_loaded = sem("rs_stored"), sem("rs_row_loaded")
        consts_loaded, pool_consts = sem("consts_loaded"), sem("pool_consts")
        angles_ready, trig_ready = sem("angles_ready"), sem("trig_ready")
        acc_done, acc_free, mem_done, mem_free = sem("acc_done"), sem("acc_free"), sem("mem_done"), sem("mem_free")
        t_square, t_ready = sem("t_square"), sem("t_ready")
        t_stored, ms_ready, rr_ready = sem("t_stored"), sem("ms_ready"), sem("rr_ready")
        dve_sem, act_sem, pool_sem = sem("dve_steps"), sem("act_steps"), sem("pool_steps")
        mem_loaded = [sem(f"mem_loaded{i}") for i in range(4)]
        m_hi_ready, m_lo_ready, m_squared = sem("m_hi_ready"), sem("m_lo_ready"), sem("m_squared")
        g_loaded = sem("g_loaded")
        h_quarter_used = sem("h_quarter_used")
        kr_raw, kr_back, kr_nat, kr_sq, kr_norm, kr_turned, kr_kept = (
            sem("kr_raw"), sem("kr_back"), sem("kr_nat"), sem("kr_sq"), sem("kr_norm"), sem("kr_turned"), sem("kr_kept"))
        up_w_loaded, up_hi, up_lo = sem("up_w_loaded"), sem("up_hi"), sem("up_lo")
        u_loaded = [sem(f"u_loaded{i}") for i in range(2)]
        u_turned, u_chi, u_clo, u_up_q, u_up, u_sq = (
            sem("u_turned"), sem("u_chi"), sem("u_clo"), sem("u_up_q"), sem("u_up"), sem("u_sq"))
        u_q_out, u_kv_out = sem("u_q_out"), sem("u_kv_out")
        u_ms, u_rr, u_done, u_qn, u_kn, u_qr = (
            sem("u_ms"), sem("u_rr"), sem("u_done"), sem("u_qn"), sem("u_kn"), sem("u_qr"))
        u_qn_kept, u_kn_kept, u_qr_kept = sem("u_qn_kept"), sem("u_kn_kept"), sem("u_qr_kept")

        class Attention:

            def __init__(self, b):
                self.qk_loaded = [sem(f"{b}_qk_loaded{i}") for i in range(2)]
                self.vg_loaded = [sem(f"{b}_vg_loaded{i}") for i in range(2)]
                self.turned, self.qT, self.kT = sem(f"{b}_turned"), sem(f"{b}_qT"), sem(f"{b}_kT")
                self.scored, self.max, self.exp = sem(f"{b}_scored"), sem(f"{b}_max"), sem(f"{b}_exp")
                self.p, self.p_turned, self.pT = sem(f"{b}_p"), sem(f"{b}_p_turned"), sem(f"{b}_pT")
                self.pv, self.gated = sem(f"{b}_pv"), sem(f"{b}_gated")

        A, B, M = Attention("a"), Attention("b"), Attention("m")
        kn_loaded, kn_turned, kn_kept, zeroed = sem("kn_loaded"), sem("kn_turned"), sem("kn_kept"), sem("zeroed")
        km_loaded, vm_loaded, km_turned, km_kept = sem("km_loaded"), sem("vm_loaded"), sem("km_turned"), sem("km_kept")
        res_loaded = [sem(f"res_loaded{i}") for i in range(2)]
        out_stored = sem("out_stored")

        N_CONSTS = 4

        block = ctx.enter_context(nc.Block())

        NTOK = G_MEM0
        POST_MEM = NTOK
        NPOST = NTOK + 2
        ROOTS = {G_KV: 24, G_CQ: 8, G_AQ0: 64, G_AQ1: 64, G_MQ: 32}
        OUT_GROUPS = D // HALF

        BSTEPS = [(h, t) for h in range(BH) for t in range(TT)]

        @block.sync
        def _(sp):
            def load_w(n, slot, first=False):
                if not first:
                    sp.wait_ge(hi_ready, n - (RAW - 1))
                    sp.wait_ge(lo_ready, n - (RAW - 1))
                sp.dma_start(w_raw[:, slot, :], io["w"][n]).then_inc(w_loaded[slot], 16)

            def load_x(k2):
                sp.dma_start(x_raw[:, 2 * k2:2 * k2 + 2, :],
                             io["xT"][2 * k2:2 * k2 + 2].rearrange("k p s -> p k s")).then_inc(x_loaded[k2], 16)

            load_w(0, 0, first=True)
            for k in range(2):
                sp.dma_start(x_raw[:, k, :], io["xT"][k]).then_inc(x0_loaded[k], 16)
            load_w(1, 1, first=True)
            load_x(1)
            load_w(2, 2, first=True)
            for k2 in range(2, KT // 2):
                load_x(k2)
            mid = (CH_OUT + RAW) // RAW * RAW - RAW
            with sp.Fori(1, mid // RAW) as i:
                for s in range(RAW):
                    load_w(i * RAW + s, s)
            n = mid
            while n < CH_OUT + RAW:
                load_w(n, n % RAW)
                n += 1

            sp.wait_ge(w_used, CH_KR + 1)
            for t in range(TT):
                if t >= 2:
                    sp.wait_ge(u_turned, t - 1)
                sp.dma_start(u_in[:, t % 2, 0:BQR], cq_s[t * P:(t + 1) * P, :]).then_inc(u_loaded[t % 2], 16)
                sp.dma_start(u_in[:, t % 2, BQR:], kv_s[t * P:(t + 1) * P, 256:]).then_inc(u_loaded[t % 2], 16)

            sp.wait_ge(u_up, TT)
            sp.dma_start(a_kn[:], kv_s[:, 0:P].rearrange("(t p) n -> p t n", p=P)).then_inc(kn_loaded, 16)
            sp.wait_ge(u_qn_kept, TT)
            sp.wait_ge(u_kn_kept, TT)
            sp.wait_ge(t_stored, 16 * NPOST)
            aq = aq_s.rearrange("s a n -> s (a n)")

            def load_q(c, par):
                wait(sp, A.turned, c - 1)
                sp.dma_start(a_q[:, par, :], aq[bass.ds(c * CHUNK, CHUNK), :]).then_inc(A.qk_loaded[par], 16)

            def load_vg(c, par):
                wait(sp, A.gated, c - 1)
                row = max(c - 1, 0) if isinstance(c, int) else c - 1
                sp.dma_start(a_v[:, par, :], kv_s[bass.ds(row * CHUNK, P), P:2 * P]).then_inc(A.vg_loaded[par], 16)
                sp.dma_start(a_gate[:, par], gate_s[0:AJ, :, bass.ds(c * CHUNK, CHUNK)].rearrange("j p s -> p j s")
                             ).then_inc(A.vg_loaded[par], 16)

            def load_a(i):
                for par in range(2):
                    c = i * 2 + par
                    load_vg(c, par)
                    if below(c + 4, NCHUNK):
                        load_q(c + 4, par)

            for c in range(4):
                load_q(c, c % 2)
            pipelined(sp, NCHUNK // 2, load_a)

            sp.wait_ge(A.gated, NCHUNK)
            for h in range(BH):
                if h >= 2:
                    sp.wait_ge(B.gated, TT * (h - 1))
                sp.dma_start(b_gate[:, h % 2, :], gate_s[AJ + h]).then_inc(B.vg_loaded[h % 2], 16)

            sp.dma_start(c_km[:], km_s.rearrange("(t p) n -> p t n", p=P)).then_inc(km_loaded, 16)
            sp.dma_start(vM[:], vm_s.rearrange("(t p) n -> p t n", p=P)).then_inc(vm_loaded, 16)
            sp.wait_ge(B.gated, len(BSTEPS))

            def load_mq(t, par):
                wait(sp, M.turned, t - 1)
                sp.dma_start(c_q[:, par, :], mq_s[bass.ds(t * P, P), :]).then_inc(M.qk_loaded[par], 16)

            def load_mg(t, par):
                wait(sp, M.gated, t - 1)
                sp.dma_start(c_gate[:, par], gate_s[AJ + BH:KT, :, bass.ds(t * P, P)].rearrange("j p s -> p j s")
                             ).then_inc(M.vg_loaded[par], 16)

            def load_m(i):
                for par in range(2):
                    t = i * 2 + par
                    load_mg(t, par)
                    if below(t + 4, TT):
                        load_mq(t + 4, par)

            for t in range(4):
                load_mq(t, t % 2)
            pipelined(sp, TT // 2, load_m)

            while n % RAW:
                load_w(n, n % RAW)
                n += 1
            with sp.Fori(n // RAW, NCH // RAW) as i:
                for s in range(RAW):
                    load_w(i * RAW + s, s)
            for n in range(NCH // RAW * RAW, NCH):
                load_w(n, n % RAW)

        @block.gpsimd
        def _(pool):
            steps = Steps(pool, pool_sem)
            g = nc.gpsimd
            steps.did(g.memset(ident[:], 0.0))
            steps.settle()
            g.affine_select(out=ident[:], in_=ident[:], compare_op=ALU.not_equal, fill=1.0, base=0,
                            pattern=[[-1, P]], channel_multiplier=1).then_inc(pool_consts, 1)
            g.memset(mhalf[:], -0.5).then_inc(pool_consts, 1)
            pool.wait_ge(pool_consts, 2)

            def rms_col(wave, sums, width, col):
                row = sum_row[:, 0:width]
                steps.did(g.partition_all_reduce(row, sums, P, bass.bass_isa.ReduceOp.add))
                steps.settle()
                pool.dma_start(row_s[wave:wave + 1, 0:width], row[0:1, :]).then_inc(row_stored, 16)
                pool.wait_ge(row_stored, 16 * (wave + 1))
                pool.dma_start(col[:], row_s[wave, 0:width].rearrange("(t p) -> p t", p=P),
                               allow_slow_non_contiguous=True).then_inc(col_loaded, 16)
                pool.wait_ge(col_loaded, 16 * (wave + 1))
                steps.did(g.tensor_scalar(col[:], col[:], 1.0 / D, EPS, ALU.mult, ALU.add))
                steps.settle()
                g.tensor_tensor(col[:], col[:], mhalf[:].to_broadcast([P, width // P]), ALU.pow).then_inc(col_ready, 1)
                pool.wait_ge(col_ready, wave + 1)

            roots = [0]

            def root(width):
                pool.wait_ge(ms_ready, roots[0] + 1)
                g.tensor_tensor(rr[:, 0:width], ss[:, 0:width], mhalf[:].to_broadcast([P, width]),
                                ALU.pow).then_inc(rr_ready, 1)
                roots[0] += 1

            pool.wait_ge(sq_used, KT)
            rms_col(0, sumsq[:], SEQ, rs_col)
            pool.dma_start(row_s[2].rearrange("(t p) -> p t", p=P), rs_col[:], allow_slow_non_contiguous=True
                           ).then_inc(rs_stored, 16)
            pool.wait_ge(rs_stored, 16)
            pool.dma_start(rs_row[:], row_s[2:3, :].to_broadcast([P, SEQ])).then_inc(rs_row_loaded, 16)
            rows = lambda a: a.rearrange("(t p) n -> p t n", p=P)
            for post in range(NTOK):
                if post in ROOTS:
                    root(ROOTS[post])
                if post < G_GATE0:
                    dst = {G_KV: kv_s, G_CQ: cq_s, G_AQ0: aq_s[:, 0, :], G_AQ1: aq_s[:, 1, :],
                           G_MQ: mq_s}[post]
                    dst, src = rows(dst), T[:]
                else:
                    j = 4 * (post - G_GATE0)
                    dst = gate_s[j:j + 4].rearrange("c p s -> p c s")
                    src = T[:].rearrange("p (c h) n -> p c (h n)", h=2)
                if post == NTOK - 1:
                    pool.wait_ge(h_quarter_used, 1)
                    for q in range(4):
                        pool.dma_start(mem_raw[:, 4 * q:4 * q + 4, :], io["memT"][4 * q:4 * q + 4].rearrange("k p s -> p k s")
                                       ).then_inc(mem_loaded[q], 16)
                pool.wait_ge(t_ready, post + 1)
                pool.dma_start(dst, src).then_inc(t_stored, 16)
            pool.wait_ge(sum_ready, 1)
            rms_col(1, m_sums[:], NMEM, ms_col)
            pool.wait_ge(w_used, CH_KR + 1)
            pool.dma_start(uq_raw[:], io["w_q_up"].rearrange("k p n -> p k n")).then_inc(up_w_loaded, 16)
            pool.dma_start(ukv_raw[:], io["w_kv_up"].rearrange("k p n -> p k n")).then_inc(up_w_loaded, 16)
            root(8)
            root(8)
            for m in range(2):
                pool.wait_ge(t_ready, POST_MEM + m + 1)
                pool.dma_start(rows(km_s if m == 0 else vm_s), T[:, 0:2, :]).then_inc(t_stored, 16)
            for t in range(TT):
                pool.wait_ge(u_ms, t + 1)
                g.tensor_tensor(rr[:, 0:12], ss[:, 0:12], mhalf[:].to_broadcast([P, 12]), ALU.pow).then_inc(u_rr, 1)
            xr = io["x"].rearrange("(t p) n -> p t n", p=P)
            yr = io["y"].rearrange("(t p) n -> p t n", p=P)
            pool.wait_ge(M.gated, TT)
            for og in range(OUT_GROUPS + 2):
                if og >= 2:
                    buf = (S, T)[og % 2]
                    parts = 1 if og - 2 < OUT_GROUPS - 1 else 4
                    for part in range(parts):
                        a, b = TT * part // parts, TT * (part + 1) // parts
                        pool.wait_ge(acc_free, TT * (NTOK + og - 2) + b)
                        pool.dma_start(yr[:, a:b, (og - 2) * HALF:(og - 1) * HALF], buf[:, a:b, :]).then_inc(out_stored, 16)
                if og < OUT_GROUPS:
                    if og >= 2:
                        pool.wait_ge(out_stored, 16 * (og - 1))
                    buf = (S, T)[og % 2]
                    pool.dma_start(buf[:], xr[:, :, og * HALF:(og + 1) * HALF]).then_inc(res_loaded[og % 2], 16)
            pool.wait_ge(out_stored, 16 * (OUT_GROUPS + 3))

        def gate_sigmoid(act, a, group):
            act.wait_ge(acc_free, TT * (group + 1))
            act.wait_ge(t_stored, 16 * group)
            a.activation(T[:], S[:], ACT.Sigmoid).then_inc(t_square, 1)

        @block.scalar
        def _(act):
            a = nc.scalar
            steps = Steps(act, act_sem)
            act.dma_start(cols[:], io["cols"]).then_inc(g_loaded, 16)
            act.dma_start(row_gains[:], io["rows"].to_broadcast([P, row_gains.shape[-1]])).then_inc(consts_loaded, 16)
            act.dma_start(posi[:], io["positions"]).then_inc(consts_loaded, 16)
            for o in range(2):
                act.dma_start(sinks[64 * o:64 * o + 64, :], io["sinks"][o:o + 1, :].to_broadcast([64, AJ])
                              ).then_inc(consts_loaded, 16)

            def high(n):
                act.wait_ge(w_loaded[n % RAW], 16 * (n // RAW + 1))
                wait(act, w_used, n - SPLIT + 1)
                a.activation(w_hi[:, n % SPLIT, :], w_raw[:, n % RAW, :], ACT.Copy).then_inc(hi_ready, 1)

            act.wait_ge(g_loaded, 16)
            for c in range(CPG):
                high(c)
                for k in (2 * c, 2 * c + 1):
                    act.wait_ge(x_loaded[c] if c else x0_loaded[k], 16)
                    a.activation(h_hi[:, k, :], x_raw[:, k, :], ACT.Copy, scale=g_x[:, k:k + 1]).then_inc(h_hi_ready, 1)
                    if k >= 4:
                        act.wait_ge(sq_used, k - 3)
                    sq = T[:, 2 * (k % 4):2 * (k % 4) + 2, :].rearrange("p a n -> p (a n)")
                    a.activation(sq, x_raw[:, k, :], ACT.Square).then_inc(sq_ready, 1)

            def evacuate(group):
                if group == 0:
                    act.wait_ge(col_ready, 1)
                wait(act, t_ready, group)
                for t in range(TT):
                    if t < TT - 1:
                        act.wait_ge(acc_done, (TT - 1) * group + t + 1)
                    else:
                        act.wait_ge(w_used, CPG * (group + 1))
                    a.activation(S[:, t, :], ps[:, t, :], ACT.Copy, scale=rs_col[:, t:t + 1]).then_inc(acc_free, 1)
                if group == 0:
                    act.wait_ge(sq_used, KT)
                else:
                    act.wait_ge(t_stored, 16 * group)
                act.wait_ge(acc_free, TT * (group + 1))
                a.activation(T[:], S[:], ACT.Square).then_inc(t_square, 1)

            for group in range(1, NTOK + 1):
                for c in range(CPG if group < NTOK else 1):
                    high(CPG * group + c)
                    if c == 0 and group - 1 < G_GATE0:
                        evacuate(group - 1)
                    if c == 1 and group == 1:
                        act.wait_ge(angles_ready, 1)
                        for tile in (sin, cos):
                            a.activation(tile[:], tile[:], ACT.Sin).then_inc(trig_ready, 1)
                    if c == 1 and group - 1 >= G_GATE0:
                        gate_sigmoid(act, a, group - 1)

            high(CH_MEM)
            gate_sigmoid(act, a, NTOK - 1)
            act.wait_ge(consts_loaded, 16 * N_CONSTS)
            act.wait_ge(h_quarter_used, 2)
            for q in range(4):
                act.wait_ge(mem_loaded[q], 16)
                part = slice(4 * q, 4 * q + 4)
                a.activation(m_sq[:, part, :], mem_raw[:, part, :], ACT.Square).then_inc(m_squared, 1)
                for k in range(4 * q, 4 * q + 4):
                    a.activation(m_hi[:, k, :], mem_raw[:, k, :], ACT.Copy, scale=g_mem[:, k:k + 1]
                                 ).then_inc(m_hi_ready, 1)
            act.wait_ge(w_used, CH_KR + 1)
            a.activation(kr_a[:], ps[0:BR, 0:2, :].rearrange("p a n -> p (a n)"), ACT.Copy).then_inc(kr_raw, 1)
            for c in range(1, CPG):
                high(CH_MEM + c)
            n = CH_MEM + CPG
            high(n)
            for m in range(2):
                if m == 0:
                    act.wait_ge(col_ready, 2)
                act.wait_ge(t_ready, NTOK + m)
                for t in range(2):
                    act.wait_ge(mem_done, m + 1) if t == 0 else act.wait_ge(w_used, CH_MEM + CPG * (m + 1))
                    a.activation(S[:, t, :], ps[:, 5 + t, :], ACT.Copy, scale=ms_col[:, t:t + 1]).then_inc(mem_free, 1)
                if m == 0:
                    act.wait_ge(mem_free, 2)
                    act.wait_ge(t_stored, 16 * NTOK)
                    a.activation(T[:, 0:2, :], S[:, 0:2, :], ACT.Square).then_inc(t_square, 1)
                    high(n + 1)
                    high(n + 2)
                    act.wait_ge(kr_nat, 1)
                    a.activation(kr_c[:], kr_b[:, :, 0, :], ACT.Square).then_inc(kr_sq, 1)
                    for k in range(n + 3, n + 6):
                        high(k)
                    act.wait_ge(up_w_loaded, 32)
                    a.activation(uq_hi[:], uq_raw[:], ACT.Copy).then_inc(up_hi, 1)
                    high(n + 6)
                    a.activation(ukv_hi[:], ukv_raw[:], ACT.Copy).then_inc(up_hi, 1)
                    high(n + 7)
            act.wait_ge(kr_turned, 1)
            act.wait_ge(zeroed, 2)
            for g in range(2):
                rows = slice(64 * g, 64 * g + 64)
                a.activation(krT[rows, g, :], ps[rows, 3:5, :].rearrange("p a n -> p (a n)"), ACT.Copy).then_inc(kr_kept, 1)

            def up_in(t):
                act.wait_ge(u_turned, t + 1)
                wait(act, u_up, t - 1)
                a.activation(c_hi[:, t % 2].rearrange("p k s -> p (k s)"),
                             ps[:, 0:2, :].rearrange("p a n -> p (a n)")[:, 0:768], ACT.Copy).then_inc(u_chi, 1)

            def up_out(t):
                if t == 0:
                    act.wait_ge(t_ready, NTOK)
                    act.wait_ge(t_stored, 16 * NTOK)
                act.wait_ge(u_up_q, t + 1)
                wait(act, u_done, t - 1)
                a.activation(u_out[:, t % 2, 0:768], ps[:, 2:4, :].rearrange("p a n -> p (a n)")[:, 256:1024], ACT.Copy
                             ).then_inc(u_q_out, 1)
                act.wait_ge(u_up, t + 1)
                a.activation(u_out[:, t % 2, 768:1280], ps[:, 4, :], ACT.Copy).then_inc(u_kv_out, 1)
                a.activation(vB[:, t, :], ps[:, 5, :], ACT.Copy).then_inc(u_kv_out, 1)

            def up_square(t):
                wait(act, u_kn, t - 1)
                act.wait_ge(u_q_out, t + 1)
                act.wait_ge(u_kv_out, 2 * (t + 1))
                a.activation(u_fin[:, t % 2], u_out[:, t % 2], ACT.Square).then_inc(u_sq, 1)

            def up_keep(t):
                act.wait_ge(u_qr, t + 1)
                a.activation(qrT[:, :, t * P:(t + 1) * P], ps[:, 2, 0:256].rearrange("p (h s) -> p h s", h=2), ACT.Copy
                             ).then_inc(u_qr_kept, 1)
                act.wait_ge(u_qn, t + 1)
                a.activation(qnT[:, :, t * P:(t + 1) * P], ps[:, 6, :].rearrange("p (h s) -> p h s", h=BH), ACT.Copy,
                             scale=g_qn).then_inc(u_qn_kept, 1)

            for step in range(TT + 3):
                if step < TT:
                    up_in(step)
                if 0 <= step - 1 < TT:
                    up_out(step - 1)
                if step >= 3:
                    up_keep(step - 3)
                if 0 <= step - 1 < TT:
                    up_square(step - 1)

            act.wait_ge(kn_turned, 1)
            act.wait_ge(zeroed, 4)
            for g in range(AKV):
                rows = slice(64 * g, 64 * g + 64)
                a.activation(a_kT[rows, g, :], ps[rows, 6:8, :].rearrange("p a n -> p (a n)"), ACT.Copy).then_inc(kn_kept, 1)

            def tiles_of(at_, n, qT, queries, exps, p_wide, pT):
                def turn_q(c, par):
                    act.wait_ge(at_.turned, c + 1)
                    wait(act, at_.scored, c - 1)
                    a.activation(qT[:, par], queries, ACT.Copy).then_inc(at_.qT, 1)

                def exponents(c, par):
                    act.wait_ge(at_.max, c + 1)
                    wait(act, at_.p_turned, c - 1)
                    exps(par).then_inc(at_.exp, 1)

                def keep_pT(c, par):
                    act.wait_ge(at_.p_turned, c + 1)
                    wait(act, at_.pv, c - 1)
                    a.activation(pT[:, par, :], ps[:, 6:8, :].rearrange("p a n -> p (a n)"), ACT.Copy
                                 ).then_inc(at_.pT, 1)

                def body(i):
                    for par in range(2):
                        c = i * 2 + par
                        if below(c + 1, n):
                            exponents(c + 1, 1 - par)
                        if below(c + 3, n):
                            turn_q(c + 3, 1 - par)
                        keep_pT(c, par)

                for c in range(3):
                    turn_q(c, c % 2)
                exponents(0, 0)
                pipelined(act, n // 2, body)

            def a_exps(par):
                a.activation(st[:, par, 4, :], st[:, par, 4, :], ACT.Exp, scale=SCALE_A)
                for e in range(8):
                    ins = a.activation(a_p[:, par, e, :], ps[:, 2 + 2 * par + e // 4, e % 4 * P:(e % 4 + 1) * P], ACT.Exp,
                                       bias=st[:, par, 1, e:e + 1], scale=SCALE_A, accum_out=st[:, par, 2, e:e + 1])
                return ins

            tiles_of(A, NCHUNK, a_qT, ps[:, 0, :].rearrange("p (j s) -> p j s", j=AJ), a_exps, P, a_pT)

            def b_exp(s):
                h, t = BSTEPS[s]
                width, par = (t + 1) * P, s % 2
                act.wait_ge(B.max, s + 1)
                wait(act, B.p_turned, s - 1)
                a.activation(b_p[:, par, 0:width], ps[:, 2 + 2 * par:4 + 2 * par, :].rearrange("p a n -> p (a n)")[:, 0:width],
                             ACT.Exp, bias=st[:, par, 1, 0:1], scale=SCALE_B, accum_out=st[:, par, 2, 0:1]
                             ).then_inc(B.exp, 1)

            def b_keep(s):
                h, t = BSTEPS[s]
                width = (t + 1) * P
                act.wait_ge(B.p_turned, s + 1)
                wait(act, B.pv, s - 1)
                a.activation(b_pT[:, s % 2, 0:width], ps[:, 6:8, :].rearrange("p a n -> p (a n)")[:, 0:width], ACT.Copy
                             ).then_inc(B.pT, 1)

            b_exp(0)
            for s in range(len(BSTEPS)):
                if s + 1 < len(BSTEPS):
                    b_exp(s + 1)
                b_keep(s)

            act.wait_ge(km_turned, 1)
            a.activation(kmT[:].rearrange("p h s -> p (h s)"), ps[:, 6:8, :].rearrange("p a n -> p (a n)"), ACT.Copy
                         ).then_inc(km_kept, 1)

            def m_exps(par):
                for h in range(MH):
                    ins = a.activation(c_p[:, par, h, :], ps[:, 2 + 2 * par + h // 2, h % 2 * NMEM:(h % 2 + 1) * NMEM],
                                       ACT.Exp, bias=st[:, par, 1, h:h + 1], scale=SCALE_M,
                                       accum_out=st[:, par, 2, h:h + 1])
                return ins

            tiles_of(M, TT, c_qT, ps[:, 0, :].rearrange("p (j s) -> p j s", j=MH), m_exps, NMEM, c_pT)

            act.wait_ge(M.gated, TT)
            for c in range(CPG):
                for k in (2 * c, 2 * c + 1):
                    a.activation(h_hi[:, k, :], mixed[:, k, :], ACT.Copy).then_inc(h_hi_ready, 1)
                high(CH_OUT + c)
            for n in range(CH_OUT + CPG, NCH):
                high(n)

        @block.vector
        def _(dve):
            v = nc.vector
            steps = Steps(dve, dve_sem)

            def do(ins):
                steps.did(ins)
                steps.settle()

            def low(n):
                dve.wait_ge(hi_ready, n + 1)
                wait(dve, w_used, n - SPLIT + 1)
                v.tensor_tensor(w_lo[:, n % SPLIT, :], w_raw[:, n % RAW, :], w_hi[:, n % SPLIT, :].bitcast(F32),
                                ALU.subtract).then_inc(lo_ready, 1)

            dve.wait_ge(g_loaded, 16)
            do(v.memset(sumsq[:], 0.0))
            for c in range(CPG):
                low(c)
                for k in (2 * c, 2 * c + 1):
                    dve.wait_ge(sq_ready, k + 1)
                    dve.wait_ge(h_hi_ready, k + 1)
                    v.scalar_tensor_tensor(out=h_lo[:, k, :], in0=x_raw[:, k, :], scalar=g_x[:, k:k + 1],
                                           in1=h_hi[:, k, :].bitcast(F32), op0=ALU.mult, op1=ALU.subtract
                                           ).then_inc(h_lo_ready, 1)
                    sq = T[:, 2 * (k % 4):2 * (k % 4) + 2, :].rearrange("p a n -> p (a n)")
                    wait(dve, sq_used, k)
                    v.tensor_tensor(sumsq[:], sumsq[:], sq, ALU.add).then_inc(sq_used, 1)

            def angles():
                dve.wait_ge(consts_loaded, 16 * N_CONSTS)
                do(v.tensor_copy(pos[:], posi[:]))
                grid = [P, TT, 32]
                do(v.tensor_tensor(sin[:], pos[:].unsqueeze(2).to_broadcast(grid),
                                   invf.unsqueeze(1).to_broadcast(grid), ALU.mult))
                turns, rest = tab[:, 0], tab[:, 1]
                do(v.tensor_scalar(turns, sin[:], 1.0 / TWO_PI, None, ALU.mult))
                do(v.tensor_scalar(turns, turns, ROUND, None, ALU.add))
                do(v.tensor_scalar(turns, turns, ROUND, None, ALU.subtract))
                for part in TWO_PI_PARTS:
                    do(v.tensor_scalar(rest, turns, part, None, ALU.mult))
                    do(v.tensor_tensor(sin[:], sin[:], rest, ALU.subtract))
                do(v.tensor_scalar(cos[:], sin[:], TWO_PI / 4, None, ALU.add))
                do(v.tensor_scalar(rest, cos[:], PI_BELOW, TWO_PI, ALU.is_gt, ALU.mult))
                do(v.tensor_tensor(cos[:], cos[:], rest, ALU.subtract))
                do(v.tensor_scalar(cos[:], cos[:], PI_BELOW, -PI_BELOW, ALU.min, ALU.max))
                v.tensor_scalar(sin[:], sin[:], PI_BELOW, -PI_BELOW, ALU.min, ALU.max).then_inc(angles_ready, 1)

            def tables(gain):
                lo, hi = gain[:, 0:32], gain[:, 32:64]
                for k, (f, part) in enumerate(((cos, lo), (sin, hi), (cos, hi), (sin, lo))):
                    steps.did(v.tensor_tensor(tab[:, k], f[:], part.unsqueeze(1).to_broadcast([P, TT, 32]), ALU.mult))
                steps.settle()

            def rotary(src, dst, n, k, tmp):
                x1, x2 = src[:, :, :, 0:32], src[:, :, :, 32:64]
                d1, d2 = dst[:, :, :, 0:32], dst[:, :, :, 32:64]
                table = lambda i: tab[:, i].unsqueeze(2).to_broadcast([P, TT, n, 32])
                if k == 0:
                    do(v.tensor_tensor(tmp, x2, table(1), ALU.mult))
                elif k == 1:
                    do(v.tensor_tensor(d1, x1, table(0), ALU.mult))
                elif k == 2:
                    do(v.tensor_tensor(d1, d1, tmp, ALU.subtract))
                elif k == 3:
                    do(v.tensor_tensor(d2, x2, table(2), ALU.mult))
                elif k == 4:
                    do(v.tensor_tensor(tmp, x1, table(3), ALU.mult))
                else:
                    do(v.tensor_tensor(d2, d2, tmp, ALU.add))

            roots = [0]

            def mean_squares(pieces):
                for view, a, b, width in pieces:
                    steps.did(v.tensor_reduce(ss[:, a:b], view, X, ALU.add))
                steps.settle()
                for i, (view, a, b, width) in enumerate(pieces):
                    ins = v.tensor_scalar(ss[:, a:b], ss[:, a:b], 1.0 / width, EPS, ALU.mult, ALU.add)
                    if i + 1 < len(pieces):
                        steps.did(ins)
                        steps.settle()
                    else:
                        ins.then_inc(ms_ready, 1)
                roots[0] += 1

            def rooted():
                dve.wait_ge(rr_ready, roots[0])

            def wait_a_chunk():
                pass

            def post(group):
                out = []
                if group == G_KV:
                    out.append(angles)
                    heads = lambda a: a[:, :, 0:128].rearrange("p t (h d) -> p t h d", h=AKV)
                    split = lambda a: a.rearrange("p (t h) -> p t h", t=TT)

                    def squares():
                        dve.wait_ge(t_square, 1)
                        mean_squares([(heads(T), 0, 16, AD), (T[:, :, 256:512], 16, 24, BKVR)])

                    out.append(squares)
                    out.append(rooted)
                    out.append(lambda: do(v.tensor_tensor(heads(S), heads(S), split(rr[:, 0:16]).unsqueeze(3)
                                                          .to_broadcast([P, TT, AKV, AD]), ALU.mult)))
                    out.append(lambda: do(v.tensor_tensor(S[:, :, 256:512], S[:, :, 256:512], rr[:, 16:24].unsqueeze(2)
                                                          .to_broadcast([P, TT, BKVR]), ALU.mult)))
                    out.append(lambda: (dve.wait_ge(trig_ready, 2), tables(g_ak)))
                    tmp = T[:, :, 256:256 + 64].rearrange("p t (h d) -> p t h d", h=AKV)
                    for k in range(6):
                        out.append(lambda k=k: rotary(heads(S), heads(T), AKV, k, tmp))
                    out.append(lambda: do(v.tensor_copy(T[:, :, 128:256], S[:, :, 128:256])))

                    def finish():
                        return (v.tensor_tensor(T[:, :, 256:512], S[:, :, 256:512],
                                           g_ckv.unsqueeze(1).to_broadcast([P, TT, BKVR]), ALU.mult))
                elif group in (G_AQ0, G_AQ1):
                    heads = lambda a: a.rearrange("p t (h d) -> p t h d", h=8)
                    flat = lambda a: a.rearrange("p t (h d) -> p (t h) d", h=8)

                    def squares():
                        dve.wait_ge(t_square, group + 1)
                        mean_squares([(flat(T[:]), 0, 64, AD)])

                    out.append(squares)
                    out.append(wait_a_chunk)
                    out.append(rooted)
                    out.append(lambda: do(v.tensor_tensor(flat(S[:]), flat(S[:]), rr[:].unsqueeze(2).to_broadcast([P, 64, AD]),
                                                          ALU.mult)))
                    out.append(lambda: tables(g_aq))
                    x1, x2 = heads(S[:])[:, :, :, 0:32], heads(S[:])[:, :, :, 32:64]
                    d1, d2 = heads(T[:])[:, :, :, 0:32], heads(T[:])[:, :, :, 32:64]
                    table = lambda i: tab[:, i].unsqueeze(2).to_broadcast([P, TT, 8, 32])
                    out.append(lambda: do(v.tensor_tensor(d2, x2, table(1), ALU.mult)))
                    out.append(lambda: do(v.tensor_tensor(d1, x1, table(0), ALU.mult)))
                    out.append(lambda: do(v.tensor_tensor(d1, d1, d2, ALU.subtract)))
                    out.append(lambda: do(v.tensor_tensor(d2, x2, table(2), ALU.mult)))
                    out.append(lambda: do(v.tensor_tensor(x1, x1, table(3), ALU.mult)))

                    def finish():
                        return (v.tensor_tensor(d2, d2, x1, ALU.add))
                elif group in (G_CQ, G_MQ):
                    n, width, gain = (TT, BQR, g_cq) if group == G_CQ else (4 * TT, MD, g_mq)
                    flat = lambda a: a.rearrange("p t (h d) -> p (t h) d", d=width)

                    def squares():
                        dve.wait_ge(t_square, group + 1)
                        mean_squares([(flat(T[:]), 0, n, width)])

                    out.append(squares)
                    out.append(wait_a_chunk)
                    out.append(rooted)
                    out.append(lambda: do(v.tensor_tensor(flat(S[:]), flat(S[:]), rr[:, 0:n].unsqueeze(2)
                                                          .to_broadcast([P, n, width]), ALU.mult)))

                    def finish():
                        return (v.tensor_tensor(flat(T[:]), flat(S[:]), gain[:].unsqueeze(1).to_broadcast([P, n, width]),
                                           ALU.mult))
                else:
                    out += [wait_a_chunk, wait_a_chunk, lambda: dve.wait_ge(t_square, group + 1)]

                    def finish():
                        return (v.tensor_tensor(T[:], T[:], S[:], ALU.mult))

                out.append(lambda: (finish().then_inc(t_ready, 1), dve.wait_ge(t_ready, group + 1)))
                return out

            def gate_out(group):
                if group == G_GATE0:
                    dve.wait_ge(rs_row_loaded, 16)
                dve.wait_ge(t_ready, group)
                for b in range(8):
                    if b < 7:
                        dve.wait_ge(acc_done, 7 * group + b + 1)
                    else:
                        dve.wait_ge(w_used, CPG * (group + 1))
                    half = b % 2
                    v.tensor_tensor(S[:, b, :], ps[:, b, :], rs_row[:, half * HALF:(half + 1) * HALF], ALU.mult
                                    ).then_inc(acc_free, 1)
                dve.wait_ge(acc_free, 8 * (group + 1))

            for group in range(1, NTOK + 1):
                todo = post(group - 1)
                if group == NTOK:
                    low(CPG * group)
                    gate_out(group - 1)
                    break
                count = CPG
                for c in range(count):
                    low(CPG * group + c)
                    if c == 0 and group - 1 >= G_GATE0:
                        gate_out(group - 1)
                    if c >= 1:
                        for step in todo[2 * c - 2:2 * c]:
                            step()
                assert len(todo) <= 2 * (CPG - 1)

            low(CH_MEM)
            for step in todo:
                step()
            for k in range(KT):
                dve.wait_ge(m_hi_ready, k + 1)
                v.scalar_tensor_tensor(out=m_lo[:, k, :], in0=mem_raw[:, k, :], scalar=g_mem[:, k:k + 1],
                                       in1=m_hi[:, k, :].bitcast(F32), op0=ALU.mult, op1=ALU.subtract
                                       ).then_inc(m_lo_ready, 1)
            dve.wait_ge(m_squared, 4)
            v.tensor_reduce(m_sums[:], m_sq[:].rearrange("p k s -> p s k"), X, ALU.add).then_inc(sum_ready, 1)
            for c in range(1, CPG):
                low(CH_MEM + c)
            n = CH_MEM + CPG
            low(n)
            low(n + 1)
            heads = lambda a: a[:, 0:2, :].rearrange("p t (h d) -> p (t h) d", d=MD)
            dve.wait_ge(t_square, NTOK + 1)
            mean_squares([(heads(T), 0, 8, MD)])
            rooted()
            do(v.tensor_tensor(heads(S), heads(S), rr[:, 0:8].unsqueeze(2).to_broadcast([P, 8, MD]), ALU.mult))
            v.tensor_tensor(heads(T), heads(S), g_mk.unsqueeze(1).to_broadcast([P, 8, MD]), ALU.mult
                            ).then_inc(t_ready, 1)
            low(n + 2)
            dve.wait_ge(kr_back, 1)
            v.tensor_tensor(kr_b[:, :, 0, :], ps[:, 2, :].rearrange("p (t d) -> p t d", t=TT),
                            rs_col[:].unsqueeze(2).to_broadcast([P, TT, BR]), ALU.mult).then_inc(kr_nat, 1)
            tables(g_kr)
            dve.wait_ge(kr_sq, 1)
            mean_squares([(kr_c[:], 0, 8, BR)])
            low(n + 3)
            rooted()
            do(v.tensor_tensor(kr_b[:, :, 0, :], kr_b[:, :, 0, :], rr[:, 0:8].unsqueeze(2).to_broadcast([P, TT, BR]),
                               ALU.mult))
            for k in range(6):
                rotary(kr_b[:], kr_d[:, :, 0:1, :], 1, k, kr_t[:])
            low(n + 4)
            v.tensor_copy(kr_d[:, :, 1:2, :], kr_d[:, :, 0:1, :]).then_inc(kr_norm, 1)
            for g in range(2):
                rows = slice(64 - 64 * g, 128 - 64 * g)
                v.memset(krT[rows, g, :], 0.0).then_inc(zeroed, 1)
            low(n + 5)
            low(n + 6)
            dve.wait_ge(up_hi, 1)
            v.tensor_tensor(uq_lo[:], uq_raw[:], uq_hi[:].bitcast(F32), ALU.subtract).then_inc(up_lo, 1)
            low(n + 7)
            dve.wait_ge(up_hi, 2)
            v.tensor_tensor(ukv_lo[:], ukv_raw[:], ukv_hi[:].bitcast(F32), ALU.subtract).then_inc(up_lo, 1)
            dve.wait_ge(mem_free, 4)
            dve.wait_ge(t_stored, 16 * (NTOK + 1))
            v.tensor_copy(T[:, 0:2, :], S[:, 0:2, :]).then_inc(t_ready, 1)

            tables(g_qr)

            def up_in(t):
                dve.wait_ge(u_chi, t + 1)
                v.tensor_tensor(c_lo[:, t % 2].rearrange("p k s -> p (k s)"),
                                ps[:, 0:2, :].rearrange("p a n -> p (a n)")[:, 0:768],
                                c_hi[:, t % 2].rearrange("p k s -> p (k s)").bitcast(F32), ALU.subtract
                                ).then_inc(u_clo, 1)

            def up_squares(t):
                rope, nope = u_fin[:, t % 2, 0:256], u_fin[:, t % 2, 256:1280]
                dve.wait_ge(u_sq, t + 1)
                wait(dve, u_rr, t)
                steps.did(v.tensor_reduce(ss[:, 0:8], nope.rearrange("p (h d) -> p h d", d=BN), X, ALU.add))
                steps.did(v.tensor_reduce(ss[:, 8:12], rope.rearrange("p (h d) -> p h d", d=BR), X, ALU.add))
                steps.settle()
                steps.did(v.tensor_scalar(ss[:, 0:8], ss[:, 0:8], 1.0 / BN, EPS, ALU.mult, ALU.add))
                steps.settle()
                v.tensor_scalar(ss[:, 8:12], ss[:, 8:12], 1.0 / BR, EPS, ALU.mult, ALU.add).then_inc(u_ms, 1)

            def up_norm(t):
                nope = lambda a: a[:, t % 2, 256:1280].rearrange("p (h d) -> p h d", d=BN)
                rope = lambda a: a[:, t % 2, 0:256].rearrange("p (h d) -> p h d", d=BR)
                dve.wait_ge(u_rr, t + 1)
                steps.did(v.tensor_tensor(rope(u_out), rope(u_out), rr[:, 8:12].unsqueeze(2).to_broadcast([P, 4, BR]),
                                          ALU.mult))
                steps.did(v.tensor_tensor(nope(u_fin), nope(u_out), rr[:, 0:8].unsqueeze(2).to_broadcast([P, 8, BN]),
                                          ALU.mult))
                steps.settle()
                x1, x2 = rope(u_out)[:, :, 0:32], rope(u_out)[:, :, 32:64]
                d1, d2 = rope(u_fin)[:, :, 0:32], rope(u_fin)[:, :, 32:64]
                table = lambda i: tab[:, i, t, :].unsqueeze(1).to_broadcast([P, BH, 32])
                steps.did(v.tensor_tensor(d1, x1, table(0), ALU.mult))
                steps.did(v.tensor_tensor(u_tmp[:, 0], x2, table(1), ALU.mult))
                steps.did(v.tensor_tensor(d2, x2, table(2), ALU.mult))
                steps.did(v.tensor_tensor(u_tmp[:, 1], x1, table(3), ALU.mult))
                steps.settle()
                steps.did(v.tensor_tensor(d1, d1, u_tmp[:, 0], ALU.subtract))
                v.tensor_tensor(d2, d2, u_tmp[:, 1], ALU.add).then_inc(u_done, 1)

            def up_keep(t):
                dve.wait_ge(u_kn, t + 1)
                v.tensor_scalar(knT[:, :, t * P:(t + 1) * P], ps[:, 7, :].rearrange("p (h s) -> p h s", h=BH),
                                g_kn, None, ALU.mult).then_inc(u_kn_kept, 1)

            up_in(0)
            for step in range(TT + 3):
                if 0 <= step - 1 < TT:
                    up_squares(step - 1)
                if step >= 3:
                    up_keep(step - 3)
                if step + 1 < TT:
                    up_in(step + 1)
                if 0 <= step - 1 < TT:
                    up_norm(step - 1)

            do(v.tensor_scalar(sinks[:], sinks[:], 1.0 / SCALE_A, None, ALU.mult))

            dve.wait_ge(u_up, TT)
            for g in range(AKV):
                rows = slice(64 - 64 * g, 128 - 64 * g)
                v.memset(a_kT[rows, g, :], 0.0).then_inc(zeroed, 1)

            def tiles_of(at_, n, maxima, normal, gated, out):
                def body(i):
                    for par in range(2):
                        c = i * 2 + par
                        dve.wait_ge(at_.exp, c + 1)
                        normal(par).then_inc(at_.p, 1)
                        if below(c + 2, n):
                            dve.wait_ge(at_.scored, c + 3)
                            maxima(par).then_inc(at_.max, 1)
                        if isinstance(c, int) and c == 0:
                            continue
                        gate(c - 1, 1 - par)

                def gate(c, par):
                    dve.wait_ge(at_.pv, c + 1)
                    gated(c, par).then_inc(at_.gated, 1)

                for c in range(2):
                    dve.wait_ge(at_.scored, c + 1)
                    maxima(c, first=(c == 0)).then_inc(at_.max, 1)
                pipelined(dve, n // 2, body, [steps])
                gate(n - 1, 1)

            def a_maxima(par, first=False):
                sc = ps[:, 2 + 2 * par:4 + 2 * par, :].rearrange("p a (g k) -> p (a g) k", k=P)
                if first:
                    do(v.memset(sc[:, :, CHUNK:P], -BIG))
                do(v.tensor_reduce(st[:, par, 0, :], sc, X, ALU.max))
                do(v.tensor_tensor(st[:, par, 0, :], st[:, par, 0, :], sinks[:], ALU.max))
                steps.did(v.tensor_tensor(st[:, par, 4, :], sinks[:], st[:, par, 0, :], ALU.subtract))
                return v.tensor_scalar(st[:, par, 1, :], st[:, par, 0, :], -SCALE_A, None, ALU.mult)

            def a_normal(par):
                do(v.tensor_tensor(st[:, par, 2, :], st[:, par, 2, :], st[:, par, 4, :], ALU.add))
                do(v.reciprocal(st[:, par, 3, :], st[:, par, 2, :]))
                return v.tensor_tensor(a_p[:, par], a_p[:, par], st[:, par, 3, :].unsqueeze(2).to_broadcast([P, 8, P]),
                                       ALU.mult)

            def a_gated(c, par):
                return v.tensor_tensor(mixed[:, 0:AJ, bass.ds(c * CHUNK, CHUNK)],
                                       ps[:, 1, :].rearrange("p (j s) -> p j s", j=AJ), a_gate[:, par], ALU.mult)

            tiles_of(A, NCHUNK, a_maxima, a_normal, a_gated, a_p)

            def b_max(s):
                h, t = BSTEPS[s]
                width, par = (t + 1) * P, s % 2
                sc = ps[:, 2 + 2 * par:4 + 2 * par, :].rearrange("p a n -> p (a n)")
                dve.wait_ge(B.scored, s + 1)
                do(v.memset(sc[0:CHUNK, width - CHUNK:width], -BIG))
                do(v.tensor_reduce(st[:, par, 0, 0:1], sc[:, 0:width], X, ALU.max))
                v.tensor_scalar(st[:, par, 1, 0:1], st[:, par, 0, 0:1], -SCALE_B, None, ALU.mult).then_inc(B.max, 1)

            def b_normal(s):
                h, t = BSTEPS[s]
                width, par = (t + 1) * P, s % 2
                dve.wait_ge(B.exp, s + 1)
                do(v.reciprocal(st[:, par, 3, 0:1], st[:, par, 2, 0:1]))
                v.tensor_scalar(b_p[:, par, 0:width], b_p[:, par, 0:width], st[:, par, 3, 0:1], None, ALU.mult
                                ).then_inc(B.p, 1)

            def b_gated(s):
                h, t = BSTEPS[s]
                dve.wait_ge(B.pv, s + 1)
                dve.wait_ge(B.vg_loaded[h % 2], 16 * (h // 2 + 1))
                v.tensor_tensor(mixed[:, AJ + h, t * P:(t + 1) * P], ps[:, s % 2, 0:P],
                                b_gate[:, h % 2, t * P:(t + 1) * P], ALU.mult).then_inc(B.gated, 1)

            b_max(0)
            b_max(1)
            for s in range(len(BSTEPS)):
                b_normal(s)
                if s + 2 < len(BSTEPS):
                    b_max(s + 2)
                if s >= 1:
                    b_gated(s - 1)
            b_gated(len(BSTEPS) - 1)

            def m_maxima(par, first=False):
                sc = ps[:, 2 + 2 * par:4 + 2 * par, :].rearrange("p a (g k) -> p (a g) k", k=NMEM)
                do(v.tensor_reduce(st[:, par, 0, 0:MH], sc, X, ALU.max))
                return v.tensor_scalar(st[:, par, 1, 0:MH], st[:, par, 0, 0:MH], -SCALE_M, None, ALU.mult)

            def m_normal(par):
                do(v.reciprocal(st[:, par, 3, 0:MH], st[:, par, 2, 0:MH]))
                return v.tensor_tensor(c_p[:, par], c_p[:, par], st[:, par, 3, 0:MH].unsqueeze(2)
                                       .to_broadcast([P, MH, NMEM]), ALU.mult)

            def m_gated(t, par):
                return v.tensor_tensor(mixed[:, AJ + BH:KT, bass.ds(t * P, P)],
                                       ps[:, 1, :].rearrange("p (j s) -> p j s", j=MH), c_gate[:, par], ALU.mult)

            tiles_of(M, TT, m_maxima, m_normal, m_gated, c_p)

            dve.wait_ge(M.gated, TT)

            def add_residual(og):
                buf = (S, T)[og % 2]
                dve.wait_ge(res_loaded[og % 2], 16 * (og // 2 + 1))
                for t in range(TT):
                    if t < TT - 1:
                        dve.wait_ge(acc_done, (TT - 1) * (NTOK + og) + t + 1)
                    else:
                        dve.wait_ge(w_used, CH_OUT + CPG * (og + 1))
                    v.tensor_tensor(buf[:, t, :], ps[:, t, :], buf[:, t, :], ALU.add).then_inc(acc_free, 1)

            for c in range(CPG):
                for k in (2 * c, 2 * c + 1):
                    dve.wait_ge(h_hi_ready, KT + k + 1)
                    v.tensor_tensor(h_lo[:, k, :], mixed[:, k, :], h_hi[:, k, :].bitcast(F32), ALU.subtract
                                    ).then_inc(h_lo_ready, 1)
                low(CH_OUT + c)
            for n in range(CH_OUT + CPG, NCH):
                low(n)
                if (n - CH_OUT) % CPG == 0:
                    add_residual((n - CH_OUT) // CPG - 1)
            add_residual(OUT_GROUPS - 1)

        @block.tensor
        def _(pe):
            mm = nc.tensor.matmul

            def three(out, a_hi, a_lo, b_hi, b_lo, start, stop):
                mm(out, a_hi, b_hi, start=start, stop=False)
                mm(out, a_hi, b_lo, start=False, stop=False)
                return mm(out, a_lo, b_hi, start=False, stop=stop)

            def token_group(g, n0, tok_parts=None, gates=False, slot0=0):
                for c in range(CPG):
                    slot, n = (slot0 + c) % SPLIT, n0 + c
                    pe.wait_ge(lo_ready, n + 1)
                    for kk in range(2):
                        k = 2 * c + kk
                        if tok_parts is not None:
                            pe.wait_ge(h_lo_ready, tok_parts + k + 1)
                        for b in range(8):
                            if k == 0:
                                wait(pe, acc_free, g * 8 + (b - 7))
                            w = slice(kk * HALF, (kk + 1) * HALF)
                            if gates:
                                ct, half = b // 2, b % 2
                                col = slice(kk * HALF + ct * P, kk * HALF + (ct + 1) * P)
                                tok = slice(half * HALF, (half + 1) * HALF)
                                ins = three(ps[:, b, :], w_hi[:, slot, col], w_lo[:, slot, col],
                                            h_hi[:, k, tok], h_lo[:, k, tok], k == 0, k == KT - 1)
                            else:
                                tok = slice(b * P, (b + 1) * P)
                                ins = three(ps[:, b, :], h_hi[:, k, tok], h_lo[:, k, tok],
                                            w_hi[:, slot, w], w_lo[:, slot, w], k == 0, k == KT - 1)
                            if k == KT - 1 and b < 7:
                                ins.then_inc(acc_done, 1)
                    ins.then_inc(w_used, 1)

            token_group(0, 0, tok_parts=0)
            with pe.Fori(1, G_GATE0) as g:
                token_group(g, g * CPG)
            with pe.Fori(G_GATE0, NTOK) as g:
                token_group(g, g * CPG, gates=True)

            pe.wait_ge(lo_ready, CH_KR + 1)
            slot = CH_KR % SPLIT
            pe.wait_ge(acc_free, 8 * (NTOK - 1) + 2)
            for k in range(KT):
                w = slice(k * BR, (k + 1) * BR)
                for half in range(2):
                    tok = slice(half * HALF, (half + 1) * HALF)
                    ins = three(ps[0:BR, half, :], w_hi[:, slot, w], w_lo[:, slot, w], h_hi[:, k, tok], h_lo[:, k, tok],
                                k == 0, k == KT - 1)
                if k in (KT // 4 - 1, KT // 2 - 1):
                    ins.then_inc(h_quarter_used, 1)
            ins.then_inc(w_used, 1)
            turn = nc.tensor.transpose

            for m in range(2):
                for c in range(CPG):
                    n = CH_MEM + CPG * m + c
                    pe.wait_ge(lo_ready, n + 1)
                    for kk in range(2):
                        k = 2 * c + kk
                        if m == 0:
                            pe.wait_ge(m_lo_ready, k + 1)
                        for t in range(2):
                            if k == 0:
                                pe.wait_ge(acc_free, 8 * NTOK)
                                wait(pe, mem_free, 2 * (m - 1) + t + 1 if m else 0)
                            tok, w = slice(t * P, (t + 1) * P), slice(kk * HALF, (kk + 1) * HALF)
                            ins = three(ps[:, 5 + t, :], m_hi[:, k, tok], m_lo[:, k, tok], w_hi[:, n % SPLIT, w],
                                        w_lo[:, n % SPLIT, w], k == 0, k == KT - 1)
                            if k == KT - 1 and t == 0:
                                ins.then_inc(mem_done, 1)
                    ins.then_inc(w_used, 1)
                if m == 0:
                    pe.wait_ge(pool_consts, 1)
                    pe.wait_ge(kr_raw, 1)
                    for t in range(TT):
                        ins = turn(ps[:, 2, t * BR:(t + 1) * BR], kr_a[:, t * P:(t + 1) * P], ident[0:BR, 0:BR])
                    ins.then_inc(kr_back, 1)
                else:
                    pe.wait_ge(kr_norm, 1)
                    for t in range(TT):
                        ins = turn(ps[:, 3 + t // 4, t % 4 * P:(t % 4 + 1) * P],
                                   kr_d[:, t].rearrange("p a d -> p (a d)"), ident[:])
                    ins.then_inc(kr_turned, 1)

            def up_in(t):
                pe.wait_ge(u_loaded[t % 2], 32 * (t // 2 + 1))
                wait(pe, u_clo, t)
                for k in range(6):
                    ins = turn(ps[:, k // 4, k % 4 * P:(k % 4 + 1) * P], u_in[:, t % 2, k * P:(k + 1) * P], ident[:])
                ins.then_inc(u_turned, 1)

            def up(t):
                hi, lo = c_hi[:, t % 2], c_lo[:, t % 2]
                pe.wait_ge(u_clo, t + 1)
                if t == 0:
                    pe.wait_ge(kr_kept, 2)
                    pe.wait_ge(up_lo, 2)
                    pe.wait_ge(mem_free, 4)
                wait(pe, u_q_out, t)
                wait(pe, u_qr_kept, t - 2)
                for k in range(4):
                    for out, a, b in ((ps[:, 3, :], 0, 512), (ps[:, 2, 256:512], 512, 768)):
                        ins = three(out, hi[:, k, :], lo[:, k, :], uq_hi[:, k, a:b], uq_lo[:, k, a:b], k == 0, k == 3)
                ins.then_inc(u_up_q, 1)
                wait(pe, u_kv_out, 2 * t)
                for k in range(2):
                    for bank, a, b in ((4, 0, 512), (5, 512, 1024)):
                        ins = three(ps[:, bank, :], hi[:, 4 + k, :], lo[:, 4 + k, :], ukv_hi[:, k, a:b],
                                    ukv_lo[:, k, a:b], k == 0, k == 1)
                ins.then_inc(u_up, 1)

            def up_back(t):
                fin = u_fin[:, t % 2]
                pe.wait_ge(u_done, t + 1)
                wait(pe, u_qr_kept, t)
                wait(pe, u_q_out, min(t + 3, TT))
                for h in range(2):
                    ins = turn(ps[:, 2, h * P:(h + 1) * P], fin[:, h * P:(h + 1) * P], ident[:])
                ins.then_inc(u_qr, 1)
                wait(pe, u_qn_kept, t)
                for h in range(BH):
                    ins = turn(ps[:, 6, h * P:(h + 1) * P], fin[:, 256 + h * P:256 + (h + 1) * P], ident[:])
                ins.then_inc(u_qn, 1)
                wait(pe, u_kn_kept, t)
                for h in range(BH):
                    ins = turn(ps[:, 7, h * P:(h + 1) * P], fin[:, 768 + h * P:768 + (h + 1) * P], ident[:])
                ins.then_inc(u_kn, 1)

            for step in range(TT + 3):
                if step < TT:
                    up_in(step)
                if 0 <= step - 1 < TT:
                    up(step - 1)
                if step >= 3:
                    up_back(step - 3)

            pe.wait_ge(kn_loaded, 16)
            pe.wait_ge(u_qn_kept, TT)
            pe.wait_ge(u_kn_kept, TT)
            for t in range(TT):
                ins = turn(ps[:, 6 + t // 4, t % 4 * P:(t % 4 + 1) * P], a_kn[:, t, :], ident[:])
            ins.then_inc(kn_turned, 1)
            pe.wait_ge(kn_kept, 2)

            def tiles_of(at_, n, queries, scores, p_turn, values):
                def queries_ready(c, par, u):
                    pe.wait_ge(at_.qk_loaded[par], u * 16 + 16)
                    wait(pe, at_.qT, c)

                def turn_q(par):
                    queries(par).then_inc(at_.turned, 1)

                def scores_ready(c):
                    pe.wait_ge(at_.qT, c + 1)
                    wait(pe, at_.exp, c - 1)

                def score(c, par):
                    scores(c, par).then_inc(at_.scored, 1)

                def turn_p(c, par):
                    pe.wait_ge(at_.p, c + 1)
                    wait(pe, at_.pT, c)
                    p_turn(par).then_inc(at_.p_turned, 1)

                def value(c, par, u):
                    pe.wait_ge(at_.pT, c + 1)
                    pe.wait_ge(at_.vg_loaded[par], u * VG[at_] + VG[at_])
                    wait(pe, at_.gated, c)
                    values(par).then_inc(at_.pv, 1)

                def body(i):
                    for par in range(2):
                        c = i * 2 + par
                        if below(c + 2, n):
                            scores_ready(c + 2)
                            if below(c + 3, n):
                                queries_ready(c + 3, 1 - par, i + 1 + par)
                            score(c + 2, par)
                            if below(c + 3, n):
                                turn_q(1 - par)
                        turn_p(c, par)
                        if isinstance(c, int) and c == 0:
                            continue
                        value(c - 1, 1 - par, i if par else i - 1)

                for c in range(3):
                    queries_ready(c, c % 2, c // 2)
                    turn_q(c % 2)
                    if c < 2:
                        scores_ready(c)
                        score(c, c)
                pipelined(pe, n // 2, body)
                value(n - 1, 1, n // 2 - 1)

            VG = {A: 32, M: 16}

            def a_queries(par):
                for j in range(AJ):
                    ins = turn(ps[:, 0, j * CHUNK:(j + 1) * CHUNK], a_q[:, par, j * P:(j + 1) * P], ident[0:CHUNK, 0:CHUNK])
                return ins

            def a_scores(c, par):
                row = max(c - 1, 0) if isinstance(c, int) else c - 1
                for jp in range(AJ // 2):
                    ins = mm(ps[:, 2 + 2 * par + jp // 2, jp % 2 * 2 * P:(jp % 2 + 1) * 2 * P]
                             .rearrange("p (g k) -> p g k", g=AKV),
                             a_qT[:, par, 2 * jp:2 * jp + 2, :].rearrange("p j s -> p (j s)"),
                             a_kT[:, :, bass.ds(row * CHUNK, P)], start=True, stop=True)
                return ins

            def a_turn_p(par):
                for g in range(AKV):
                    for jp in range(AJ // 2):
                        ins = turn(ps[:, 6 + g, jp * P:(jp + 1) * P], a_p[:, par, 2 * jp + g, :], ident[:])
                return ins

            def a_values(par):
                for g in range(AKV):
                    ins = mm(ps[64 * g:64 * g + 64, 1, :], a_v[:, par, 64 * g:64 * g + 64],
                             a_pT[:, par, g * HALF:(g + 1) * HALF], start=True, stop=True)
                return ins

            tiles_of(A, NCHUNK, a_queries, a_scores, a_turn_p, a_values)

            pe.wait_ge(A.gated, NCHUNK)

            def b_score(s):
                h, t = BSTEPS[s]
                width, par = (t + 1) * P, s % 2
                wait(pe, B.exp, s - 1)
                q = slice(t * P, (t + 1) * P)
                for a in range(0, width, HALF):
                    b = min(width, a + HALF)
                    out = ps[:, 2 + 2 * par + a // HALF, 0:b - a]
                    mm(out, qnT[:, h, q], knT[:, h, a:b], start=True, stop=False)
                    ins = mm(out, qrT[:, h // 2, q], krT[:, h % 2, a:b], start=False, stop=True)
                ins.then_inc(B.scored, 1)

            def b_turn_p(s):
                h, t = BSTEPS[s]
                pe.wait_ge(B.p, s + 1)
                wait(pe, B.pT, s)
                for k in range(t + 1):
                    ins = turn(ps[:, 6 + k // 4, k % 4 * P:(k % 4 + 1) * P], b_p[:, s % 2, k * P:(k + 1) * P], ident[:])
                ins.then_inc(B.p_turned, 1)

            def b_values(s):
                h, t = BSTEPS[s]
                pe.wait_ge(B.pT, s + 1)
                wait(pe, B.gated, s - 1)
                for k in range(t + 1):
                    ins = mm(ps[:, s % 2, 0:P], vB[:, k, h * BV:(h + 1) * BV], b_pT[:, s % 2, k * P:(k + 1) * P],
                             start=(k == 0), stop=(k == t))
                ins.then_inc(B.pv, 1)

            b_score(0)
            b_score(1)
            for s in range(len(BSTEPS)):
                if s + 2 < len(BSTEPS):
                    b_score(s + 2)
                b_turn_p(s)
                if s >= 1:
                    b_values(s - 1)
            b_values(len(BSTEPS) - 1)

            pe.wait_ge(B.gated, len(BSTEPS))
            pe.wait_ge(km_loaded, 16)
            for h in range(MH):
                for t in range(2):
                    i = 2 * h + t
                    ins = turn(ps[:, 6 + i // 4, i % 4 * P:(i % 4 + 1) * P], c_km[:, t, h * P:(h + 1) * P], ident[:])
            ins.then_inc(km_turned, 1)
            pe.wait_ge(km_kept, 1)
            pe.wait_ge(vm_loaded, 16)

            def m_queries(par):
                for j in range(MH):
                    ins = turn(ps[:, 0, j * P:(j + 1) * P], c_q[:, par, j * P:(j + 1) * P], ident[:])
                return ins

            def m_scores(t, par):
                for h in range(MH):
                    ins = mm(ps[:, 2 + 2 * par + h // 2, h % 2 * NMEM:(h % 2 + 1) * NMEM], c_qT[:, par, h, :], kmT[:, h, :],
                             start=True, stop=True)
                return ins

            def m_turn_p(par):
                for kb in range(2):
                    for h in range(MH):
                        ins = turn(ps[:, 6 + kb, h * P:(h + 1) * P], c_p[:, par, h, kb * P:(kb + 1) * P], ident[:])
                return ins

            def m_values(par):
                for h in range(MH):
                    for kb in range(2):
                        at_ = kb * HALF + h * P
                        ins = mm(ps[:, 1, h * P:(h + 1) * P], vM[:, kb, h * MD:(h + 1) * MD], c_pT[:, par, at_:at_ + P],
                                 start=(kb == 0), stop=(kb == 1))
                return ins

            tiles_of(M, TT, m_queries, m_scores, m_turn_p, m_values)

            pe.wait_ge(M.gated, TT)
            token_group(NTOK, CH_OUT, tok_parts=KT, slot0=CH_OUT % SPLIT)
            with pe.Fori(1, OUT_GROUPS) as og:
                token_group(og + NTOK, og * CPG + CH_OUT, slot0=CH_OUT % SPLIT)


def kernel(x, mem, positions, g_in, w_in, a_g_q, a_g_k, a_sinks, b_g_cq, b_w_q_up, b_g_ckv, b_w_kv_up, b_g_q_nope,
           b_g_q_rope, b_g_k_nope, b_g_k_rope, m_g_mem, m_w_kv, m_g_q, m_g_k, w_o):
    import concourse.bacc as bacc
    from concourse.bass_utils import run_bass_kernel_spmd

    f = lambda a: np.ascontiguousarray(np.asarray(a))
    tiles = lambda a: a.reshape(-1, P, a.shape[-1])
    x0, mem0 = f(x)[0], f(mem)[0]
    w = f(w_in)[0]
    cuts = np.cumsum([AH * AD, AKV * AD, AKV * AD, AH * AD, BQR, BKVR, BR, BH * BV, MH * MD, MH * MD])
    aq, ak, av, ag, cq, ckv, kr, bg, mq, mg = np.split(w, cuts[:-1], axis=1)
    paired = lambda a: a.reshape(a.shape[0], AKV, AJ, AD).transpose(0, 2, 1, 3).reshape(a.shape[0], -1)
    wo = f(w_o)[0]
    wo = np.concatenate([paired(wo[:AH * AD].T).T, wo[AH * AD:]], 0)

    def chunks(a):
        a = a.reshape(CPG, 2, P, -1, HALF)
        return a.transpose(3, 0, 2, 1, 4).reshape(-1, P, 2 * HALF)

    front = np.concatenate([ak, av, ckv, cq, paired(aq), mq, paired(ag), bg, mg], 1)
    stream = np.concatenate([
        chunks(front),
        kr.reshape(KT, P, BR).transpose(1, 0, 2).reshape(1, P, KT * BR),
        chunks(f(m_w_kv)[0]),
        chunks(wo),
    ], 0)
    assert stream.shape[0] == NCH
    q_up = f(b_w_q_up)[0].reshape(BQR, BH, BN + BR)
    q_up = np.concatenate([q_up[:, :, :BN].reshape(BQR, -1), q_up[:, :, BN:].reshape(BQR, -1)], 1)
    kv_up = f(b_w_kv_up)[0].reshape(BKVR, BH, BN + BV)
    kv_up = np.concatenate([kv_up[:, :, :BN].reshape(BKVR, -1), kv_up[:, :, BN:].reshape(BKVR, -1)], 1)
    arrays = {
        "w": stream, "xT": tiles(x0.T), "memT": tiles(mem0.T), "x": x0,
        "w_q_up": tiles(q_up), "w_kv_up": tiles(kv_up),
        "positions": f(positions)[0].reshape(TT, P).T.astype(np.int32),
        "sinks": f(a_sinks)[0].reshape(AKV, AJ // 2, 2).transpose(2, 1, 0).reshape(2, AJ),
        "cols": np.concatenate([f(g_in)[0].reshape(KT, P).T, f(m_g_mem)[0].reshape(KT, P).T, f(b_g_q_nope).T,
                                f(b_g_k_nope).T], 1),
        "rows": np.concatenate([f(a_g_q), f(a_g_k), f(b_g_cq), f(b_g_ckv), f(b_g_q_rope), f(b_g_k_rope), f(m_g_q),
                                f(m_g_k), (10000.0 ** (-np.arange(0, AD, 2, dtype=np.float64) / AD)
                                           ).astype(np.float32)[None]], 1),
    }
    nc = bacc.Bacc("TRN2", target_bir_lowering=False, num_devices=1)
    sent, io = {}, {}
    for name, a in arrays.items():
        a = np.ascontiguousarray(a)
        sent[f"in_{name}"] = a
        io[name] = nc.dram_tensor(f"in_{name}", a.shape, mybir.dt.from_np(a.dtype), kind="ExternalInput").ap()
    io["y"] = nc.dram_tensor("out_y", (SEQ, D), F32, kind="ExternalOutput").ap()
    layer(nc, io)
    r = run_bass_kernel_spmd(nc, [sent], core_ids=[0])
    return r.results[0]["out_y"].reshape(1, SEQ, D)
```

```python
from contextlib import ExitStack

import concourse.bass as bass
import numpy as np
from concourse import mybir

F32 = mybir.dt.float32
F32R = mybir.dt.float32r
I32 = mybir.dt.int32
ALU = mybir.AluOpType
ACT = mybir.ActivationFunctionType
X = mybir.AxisListType.X

P = 128
D = 2048
SEQ = 1024
KT = D // P
TT = SEQ // P
HALF = 512
NMEM = 256
CHUNK = 64
NCHUNK = SEQ // CHUNK
AH, AKV, AD = 16, 2, 64
AJ = AH // AKV
BH, BN, BR, BV = 4, 128, 64, 128
BQR, BKVR = 512, 256
MH, MD = 4, 128
EPS = 1e-6
SCALE_A = AD ** -0.5
SCALE_B = (BN + BR) ** -0.5
SCALE_M = MD ** -0.5
BIG = 3.0e38
TWO_PI = 2 * float(np.pi)
PI_BELOW = 3.1415925
ROUND = 1.5 * 2.0 ** 23
_C1 = 6.28125
_C2 = float(np.round((TWO_PI - _C1) * 2.0 ** 20) / 2.0 ** 20)
TWO_PI_PARTS = (_C1, _C2, TWO_PI - _C1 - _C2)

G_KV, G_CQ, G_AQ0, G_AQ1, G_MQ, G_GATE0 = 0, 1, 2, 3, 4, 5
NGATE = 4
G_MEM0 = G_GATE0 + NGATE
CPG = KT // 2
CH_KR = G_MEM0 * CPG
CH_MEM = CH_KR + 1
CH_OUT = CH_MEM + 2 * CPG
NCH = CH_OUT + (D // HALF) * CPG
RAW = 3
SPLIT = 2


def wait(e, sem, value):
    if isinstance(value, int) and value <= 0:
        return
    e.wait_ge(sem, value)


class Steps:

    def __init__(self, engine, sem):
        self.engine, self.sem, self.n = engine, sem, 0

    def did(self, ins):
        ins.then_inc(self.sem, 1)
        self.n = self.n + 1

    def settle(self):
        self.engine.wait_ge(self.sem, self.n)


def pipelined(engine, n, body, steps=(), tail=2):
    before = [s.n for s in steps]
    body(0)
    per = [s.n - b for s, b in zip(steps, before)]
    with engine.Fori(1, n - tail) as i:
        for s, b, k in zip(steps, before, per):
            s.n = i * k + b
        body(i)
    for last in range(n - tail, n):
        for s, b, k in zip(steps, before, per):
            s.n = b + last * k
        body(last)


def below(c, n):
    return c < n if isinstance(c, int) else True


def layer(nc, io):
    with ExitStack() as ctx:
        def sem(name):
            return ctx.enter_context(nc.semaphore(name))

        top = [(nc.sbuf_base + 31) // 32 * 32]

        def region(size):
            at = top[0]
            top[0] += size
            assert top[0] <= nc.sbuf_usable_end, top[0] - nc.sbuf_usable_end
            return at

        def at(name, shape, dt, offset):
            return nc.alloc_sbuf_tensor_at(name, shape, dt, offset=offset)

        R0, R1 = region(KT * SEQ * 4), region(KT * SEQ * 4)
        WRAW = region(RAW * 4096)
        WHI, WLO = region(SPLIT * 4096), region(SPLIT * 4096)
        RS, RT = region(16384), region(16384)

        def small(name, shape, dt=F32):
            size = int(np.prod(shape[1:])) * 4
            return at(name, shape, dt, region((size + 31) // 32 * 32))

        def inside(start, size):
            where = [start]

            def place(name, shape, dt=F32):
                t = at(name, shape, dt, where[0])
                where[0] += int(np.prod(shape[1:])) * 4
                assert where[0] <= start + size, name
                return t
            return place

        h_hi = at("h_hi", [P, KT, SEQ], F32R, R0)
        h_lo = at("h_lo", [P, KT, SEQ], F32R, R1)
        x_raw = at("x_raw", [P, KT, SEQ], F32, R1)
        m_hi = at("m_hi", [P, KT, NMEM], F32R, R0)
        m_lo = at("m_lo", [P, KT, NMEM], F32R, R1)
        mem_raw = at("mem_raw", [P, KT, NMEM], F32, R1)
        m_sq = at("m_sq", [P, KT, NMEM], F32, R0 + 16384)
        m_sums = at("m_sums", [P, NMEM], F32, R1 + 20480)
        m_parts = at("m_parts", [P, 4, NMEM], F32, R1 + 16384)
        kr_a = at("kr_a", [BR, SEQ], F32, R0 + 33792)
        kr_b = at("kr_b", [P, TT, 1, BR], F32, R0 + 37888)
        kr_c = at("kr_c", [P, TT, BR], F32, R0 + 39936)
        kr_d = at("kr_d", [P, TT, 2, BR], F32, R0 + 41984)
        kr_t = at("kr_t", [P, TT, 1, 32], F32, R0 + 46080)
        mixed = at("mixed", [P, KT, SEQ], F32, R1)
        w_raw = at("w_raw", [P, RAW, 1024], F32, WRAW)
        w_hi = at("w_hi", [P, SPLIT, 1024], F32R, WHI)
        w_lo = at("w_lo", [P, SPLIT, 1024], F32R, WLO)
        S = at("S", [P, 8, HALF], F32, RS)
        T = at("T", [P, 8, HALF], F32, RT)

        qnT = at("qnT", [P, BH, SEQ], F32, R0)
        knT = at("knT", [P, BH, SEQ], F32, R0 + 16384)
        vB = at("vB", [P, TT, BH * BV], F32, R0 + 32768)
        qrT = at("qrT", [P, BH // 2, SEQ], F32, R0 + 49152)
        krT = at("krT", [P, 2, SEQ], F32, R0 + 57344)

        ident = small("ident", [P, P])
        cos = small("cos", [P, TT, 32])
        sin = small("sin", [P, TT, 32])
        tab_at = top[0]
        tab = small("tab", [P, 4, TT, 32])
        sumsq = at("sumsq", [P, SEQ], F32, RS)
        sum_row = at("sum_row", [P, SEQ], F32, RS + 4096)
        rs_row_at = top[0]
        rs_row = small("rs_row", [P, SEQ])
        rs_col = small("rs_col", [P, TT])
        ms_col = small("ms_col", [P, 2])
        cols = small("cols", [P, 2 * KT + 2])
        g_x, g_mem = cols[:, 0:KT], cols[:, KT:2 * KT]
        g_qn, g_kn = cols[:, 2 * KT:2 * KT + 1], cols[:, 2 * KT + 1:2 * KT + 2]
        row_names = (("a_g_q", AD), ("a_g_k", AD), ("b_g_cq", BQR), ("b_g_ckv", BKVR), ("b_g_q_rope", BR),
                     ("b_g_k_rope", BR), ("m_g_q", MD), ("m_g_k", MD), ("invf", 32))
        row_gains = small("row_gains", [P, sum(n for _, n in row_names)])
        ends = np.cumsum([n for _, n in row_names])
        g_aq, g_ak, g_cq, g_ckv, g_qr, g_kr, g_mq, g_mk, invf = (
            row_gains[:, int(e) - n:int(e)] for e, (_, n) in zip(ends, row_names))
        sinks = small("sinks", [P, AJ])
        posi = small("posi", [P, TT], I32)
        pos = small("pos", [P, TT])
        mhalf = small("mhalf", [P, 1])
        kmT = at("kmT", [P, MH, NMEM], F32, rs_row_at)
        vM = at("vM", [P, 2, MH * MD], F32, tab_at)
        ss = small("ss", [P, 64])
        rr = small("rr", [P, 64])
        st = small("st", [P, 2, 5, 8])

        up_at = inside(R1 + 16384, 40960)
        uq_hi = up_at("uq_hi", [P, 4, 768], F32R)
        uq_raw_at = R1 + 16384 + 12288
        uq_lo = up_at("uq_lo", [P, 4, 768], F32R)
        ukv_hi = up_at("ukv_hi", [P, 2, 1024], F32R)
        ukv_raw_at = R1 + 16384 + 24576 + 8192
        ukv_lo = up_at("ukv_lo", [P, 2, 1024], F32R)
        uq_raw = at("uq_raw", [P, 4, 768], F32, uq_raw_at)
        ukv_raw = at("ukv_raw", [P, 2, 1024], F32, ukv_raw_at)
        u_in = at("u_in", [P, 2, 768], F32, R1 + 57344)
        put = inside(R1, 16384)
        c_hi = put("c_hi", [P, 2, 6, P], F32R)
        c_lo = put("c_lo", [P, 2, 6, P], F32R)
        u_tmp = put("u_tmp", [P, 2, 4, 32])
        u_out = at("u_out", [P, 2, 1280], F32, RS + 4096)
        u_fin = at("u_fin", [P, 2, 1280], F32, RT + 4096)
        a_kT = at("a_kT", [P, AKV, SEQ], F32, WLO)
        a_kn = at("a_kn", [P, TT, P], F32, WHI)
        a_p = at("a_p", [P, 2, 8, P], F32, WHI)
        a_q_at = at("a_q_at", [CHUNK, 2, 4096], F32, RS)
        a_q = a_q_at[:, :, 0:AJ * P]
        a_qT = at("a_qT", [P, 2, AJ, CHUNK], F32, WRAW + 8192)
        a_pT = at("a_pT", [P, 2, 2 * HALF], F32, RS + 8192)
        a_v = small("a_v", [P, 2, P])
        nothing = small("nothing", [P, 1])
        b_p = at("b_p", [P, 2, SEQ], F32, WRAW)
        b_pT = at("b_pT", [P, 2, SEQ], F32, RT + 8192)
        c_km = at("c_km", [P, 2, HALF], F32, WHI + 4096)
        c_q = at("c_q", [P, 2, MH * MD], F32, RS)
        c_qT = at("c_qT", [P, 2, MH, P], F32, RS + 4096)
        c_pT = at("c_pT", [P, 2, 2 * HALF], F32, RS + 8192)
        c_p = at("c_p", [P, 2, MH, NMEM], F32, RT)

        ps = ctx.enter_context(nc.psum_tensor("ps", [P, 8, HALF], F32))

        def scratch(name, shape):
            return nc.dram_tensor(name, shape, F32, kind="Internal").ap()

        kv_s = scratch("kv_s", [SEQ, HALF])
        cq_s = scratch("cq_s", [SEQ, BQR])
        aq_s = scratch("aq_s", [SEQ, 2, HALF])
        mq_s = scratch("mq_s", [SEQ, HALF])
        gate_s = scratch("gate_s", [KT, P, SEQ])
        km_s = scratch("km_s", [NMEM, HALF])
        vm_s = scratch("vm_s", [NMEM, HALF])
        row_s = scratch("row_s", [3, SEQ])

        w_loaded = [sem(f"w_loaded{i}") for i in range(RAW)]
        hi_ready, lo_ready, w_used = sem("hi_ready"), sem("lo_ready"), sem("w_used")
        x0_loaded = [sem(f"x0_loaded{i}") for i in range(2)]
        x_loaded = [sem(f"x_loaded{i}") for i in range(KT // 2)]
        h_hi_ready, h_lo_ready = sem("h_hi_ready"), sem("h_lo_ready")
        sq_ready, sq_used, sum_ready = sem("sq_ready"), sem("sq_used"), sem("sum_ready")
        row_stored, col_loaded, col_ready = sem("row_stored"), sem("col_loaded"), sem("col_ready")
        rs_stored, rs_row_loaded = sem("rs_stored"), sem("rs_row_loaded")
        consts_loaded, pool_consts = sem("consts_loaded"), sem("pool_consts")
        angles_ready, trig_ready = sem("angles_ready"), sem("trig_ready")
        acc_done, acc_free, mem_done, mem_free = sem("acc_done"), sem("acc_free"), sem("mem_done"), sem("mem_free")
        t_square, t_ready = sem("t_square"), sem("t_ready")
        t_stored, ms_ready, rr_ready = sem("t_stored"), sem("ms_ready"), sem("rr_ready")
        dve_sem, pool_sem = sem("dve_steps"), sem("pool_steps")
        mem_loaded = [sem(f"mem_loaded{i}") for i in range(4)]
        m_hi_ready, m_lo_ready, m_squared = sem("m_hi_ready"), sem("m_lo_ready"), sem("m_squared")
        g_loaded = sem("g_loaded")
        h_quarter_used = sem("h_quarter_used")
        kr_raw, kr_back, kr_nat, kr_sq, kr_norm, kr_turned, kr_kept = (
            sem("kr_raw"), sem("kr_back"), sem("kr_nat"), sem("kr_sq"), sem("kr_norm"), sem("kr_turned"), sem("kr_kept"))
        uq_loaded, ukv_loaded, up_hi, up_lo = sem("uq_loaded"), sem("ukv_loaded"), sem("up_hi"), sem("up_lo")
        u_loaded = [sem(f"u_loaded{i}") for i in range(2)]
        u_turned, u_chi, u_clo, u_up_q, u_up, u_sq = (
            sem("u_turned"), sem("u_chi"), sem("u_clo"), sem("u_up_q"), sem("u_up"), sem("u_sq"))
        u_q_out, u_kv_out = sem("u_q_out"), sem("u_kv_out")
        u_ms, u_rr, u_done, u_qn, u_kn, u_qr = (
            sem("u_ms"), sem("u_rr"), sem("u_done"), sem("u_qn"), sem("u_kn"), sem("u_qr"))
        u_qn_kept, u_kn_kept, u_qr_kept = sem("u_qn_kept"), sem("u_kn_kept"), sem("u_qr_kept")

        class Attention:

            def __init__(self, b):
                self.q_loaded = [sem(f"{b}_q_loaded{i}") for i in range(2)]
                self.gates_loaded = sem(f"{b}_gates_loaded")
                self.turned, self.qT = sem(f"{b}_turned"), sem(f"{b}_qT")
                self.scored, self.max, self.exp = sem(f"{b}_scored"), sem(f"{b}_max"), sem(f"{b}_exp")
                self.p, self.p_turned, self.pT = sem(f"{b}_p"), sem(f"{b}_p_turned"), sem(f"{b}_pT")
                self.pv, self.gated = sem(f"{b}_pv"), sem(f"{b}_gated")

        A, B, M = Attention("a"), Attention("b"), Attention("m")
        a_v_loaded = [sem(f"a_v_loaded{i}") for i in range(2)]
        kn_loaded, kn_turned, kn_kept, zeroed = sem("kn_loaded"), sem("kn_turned"), sem("kn_kept"), sem("zeroed")
        km_loaded, vm_loaded, km_turned, km_kept = sem("km_loaded"), sem("vm_loaded"), sem("km_turned"), sem("km_kept")
        res_loaded = [sem(f"res_loaded{i}") for i in range(2)]
        out_stored = sem("out_stored")

        N_CONSTS = 4

        block = ctx.enter_context(nc.Block())

        NTOK = G_MEM0
        POST_MEM = NTOK
        NPOST = NTOK + 2
        ROOTS = {G_KV: 24, G_CQ: 8, G_AQ0: 64, G_AQ1: 64, G_MQ: 32}
        OUT_GROUPS = D // HALF
        X_TILES = ((0, 1), (2, 3), (4, 5, 6), (7, 8, 9), (10, 11, 12), (13, 14, 15), (), ())
        MEM_BANKS = ((5, 6), (7, 2))

        BSTEPS = [(h, t) for h in range(BH) for t in range(TT)]

        @block.sync
        def _(sp):
            def load_w(n, slot, first=False):
                if not first:
                    sp.wait_ge(hi_ready, n - (RAW - 1))
                    sp.wait_ge(lo_ready, n - (RAW - 1))
                sp.dma_start(w_raw[:, slot, :], io["w"][n]).then_inc(w_loaded[slot], 16)

            def load_x(k2):
                sp.dma_start(x_raw[:, 2 * k2:2 * k2 + 2, :],
                             io["xT"][2 * k2:2 * k2 + 2].rearrange("k p s -> p k s")).then_inc(x_loaded[k2], 16)

            load_w(0, 0, first=True)
            for k in range(2):
                sp.dma_start(x_raw[:, k, :], io["xT"][k]).then_inc(x0_loaded[k], 16)
            load_w(1, 1, first=True)
            load_x(1)
            load_w(2, 2, first=True)
            for k2 in range(2, KT // 2):
                load_x(k2)
            mid = CH_OUT // RAW * RAW
            with sp.Fori(1, mid // RAW) as i:
                for s in range(RAW):
                    load_w(i * RAW + s, s)
            n = mid
            while n < CH_OUT:
                load_w(n, n % RAW)
                n += 1

            sp.wait_ge(w_used, CH_KR + 1)
            for t in range(TT):
                if t >= 2:
                    sp.wait_ge(u_turned, t - 1)
                sp.dma_start(u_in[:, t % 2, 0:BQR], cq_s[t * P:(t + 1) * P, :]).then_inc(u_loaded[t % 2], 16)
                sp.dma_start(u_in[:, t % 2, BQR:], kv_s[t * P:(t + 1) * P, 256:]).then_inc(u_loaded[t % 2], 16)

            sp.wait_ge(w_used, CH_OUT)
            sp.wait_ge(t_stored, 16 * NPOST)
            sp.dma_start(a_kn[:], kv_s[:, 0:P].rearrange("(t p) n -> p t n", p=P)).then_inc(kn_loaded, 16)
            sp.dma_start(c_km[:], km_s.rearrange("(t p) n -> p t n", p=P)).then_inc(km_loaded, 16)

            aq = aq_s.rearrange("s a n -> s (a n)")

            def load_q(c, par):
                wait(sp, A.turned, c - 1)
                sp.dma_start(a_q[:, par, :], aq[bass.ds(c * CHUNK, CHUNK), :]).then_inc(A.q_loaded[par], 16)

            def load_v(c, par):
                wait(sp, A.pv, c - 1)
                row = max(c - 1, 0) if isinstance(c, int) else c - 1
                sp.dma_start(a_v[:, par, :], kv_s[bass.ds(row * CHUNK, P), P:2 * P]).then_inc(a_v_loaded[par], 16)

            def load_a(i):
                for par in range(2):
                    c = i * 2 + par
                    load_v(c, par)
                    if below(c + 4, NCHUNK):
                        load_q(c + 4, par)

            load_q(0, 0)
            load_q(1, 1)
            sp.wait_ge(u_done, TT)
            sp.dma_start(vM[:], vm_s.rearrange("(t p) n -> p t n", p=P)).then_inc(vm_loaded, 16)
            load_q(2, 0)
            load_q(3, 1)
            pipelined(sp, NCHUNK // 2, load_a)

            def load_mq(t, par):
                wait(sp, M.turned, t - 1)
                sp.dma_start(c_q[:, par, :], mq_s[bass.ds(t * P, P), :]).then_inc(M.q_loaded[par], 16)

            sp.wait_ge(A.turned, NCHUNK)
            for t in range(6):
                load_mq(t, t % 2)
            sp.wait_ge(B.p_turned, len(BSTEPS))
            while n < CH_OUT + RAW:
                load_w(n, n % RAW)
                n += 1
            for t in range(6, TT):
                load_mq(t, t % 2)

            while n % RAW:
                load_w(n, n % RAW)
                n += 1
            with sp.Fori(n // RAW, NCH // RAW) as i:
                for s in range(RAW):
                    load_w(i * RAW + s, s)
            for n in range(NCH // RAW * RAW, NCH):
                load_w(n, n % RAW)

        @block.gpsimd
        def _(pool):
            steps = Steps(pool, pool_sem)
            g = nc.gpsimd
            steps.did(g.memset(ident[:], 0.0))
            steps.settle()
            g.affine_select(out=ident[:], in_=ident[:], compare_op=ALU.not_equal, fill=1.0, base=0,
                            pattern=[[-1, P]], channel_multiplier=1).then_inc(pool_consts, 1)
            g.memset(mhalf[:], -0.5).then_inc(pool_consts, 1)
            pool.dma_start(row_gains[:], io["rows"].to_broadcast([P, row_gains.shape[-1]])).then_inc(consts_loaded, 16)
            pool.dma_start(posi[:], io["positions"]).then_inc(consts_loaded, 16)
            for o in range(2):
                pool.dma_start(sinks[64 * o:64 * o + 64, :], io["sinks"][o:o + 1, :].to_broadcast([64, AJ])
                              ).then_inc(consts_loaded, 16)
            pool.wait_ge(pool_consts, 2)

            def rms_col(wave, sums, width, col):
                row = sum_row[:, 0:width]
                steps.did(g.partition_all_reduce(row, sums, P, bass.bass_isa.ReduceOp.add))
                steps.settle()
                pool.dma_start(row_s[wave:wave + 1, 0:width], row[0:1, :]).then_inc(row_stored, 16)
                pool.wait_ge(row_stored, 16 * (wave + 1))
                pool.dma_start(col[:], row_s[wave, 0:width].rearrange("(t p) -> p t", p=P),
                               allow_slow_non_contiguous=True).then_inc(col_loaded, 16)
                pool.wait_ge(col_loaded, 16 * (wave + 1))
                steps.did(g.tensor_scalar(col[:], col[:], 1.0 / D, EPS, ALU.mult, ALU.add))
                steps.settle()
                g.tensor_tensor(col[:], col[:], mhalf[:].to_broadcast([P, width // P]), ALU.pow).then_inc(col_ready, 1)
                pool.wait_ge(col_ready, wave + 1)

            roots = [0]

            def root(width):
                pool.wait_ge(ms_ready, roots[0] + 1)
                g.tensor_tensor(rr[:, 0:width], ss[:, 0:width], mhalf[:].to_broadcast([P, width]),
                                ALU.pow).then_inc(rr_ready, 1)
                roots[0] += 1

            pool.wait_ge(sq_used, KT)
            rms_col(0, sumsq[:], SEQ, rs_col)
            pool.dma_start(row_s[2].rearrange("(t p) -> p t", p=P), rs_col[:], allow_slow_non_contiguous=True
                           ).then_inc(rs_stored, 16)
            pool.wait_ge(rs_stored, 16)
            pool.dma_start(rs_row[:], row_s[2:3, :].to_broadcast([P, SEQ])).then_inc(rs_row_loaded, 16)
            rows = lambda a: a.rearrange("(t p) n -> p t n", p=P)
            for post in range(NTOK):
                if post in ROOTS:
                    root(ROOTS[post])
                if post < G_GATE0:
                    dst = {G_KV: kv_s, G_CQ: cq_s, G_AQ0: aq_s[:, 0, :], G_AQ1: aq_s[:, 1, :],
                           G_MQ: mq_s}[post]
                    dst, src = rows(dst), T[:]
                else:
                    j = 4 * (post - G_GATE0)
                    dst = gate_s[j:j + 4].rearrange("c p s -> p c s")
                    src = T[:].rearrange("p (c h) n -> p c (h n)", h=2)
                if post == NTOK - 1:
                    pool.wait_ge(h_quarter_used, 1)
                    for q in range(4):
                        pool.dma_start(mem_raw[:, 4 * q:4 * q + 4, :], io["memT"][4 * q:4 * q + 4].rearrange("k p s -> p k s")
                                       ).then_inc(mem_loaded[q], 16)
                pool.wait_ge(t_ready, post + 1)
                pool.dma_start(dst, src).then_inc(t_stored, 16)
            root(8)
            pool.wait_ge(sum_ready, 1)
            rms_col(1, m_sums[:], NMEM, ms_col)
            pool.wait_ge(w_used, CH_KR + 1)
            for q in range(2):
                pool.wait_ge(w_used, CH_MEM + CPG - 1 + q)
                pool.dma_start(uq_raw[:, 2 * q:2 * q + 2, :], io["w_q_up"][2 * q:2 * q + 2].rearrange("k p n -> p k n")
                               ).then_inc(uq_loaded, 16)
            root(8)
            for q in range(2):
                pool.wait_ge(w_used, CH_MEM + CPG + 2 + q)
                pool.dma_start(ukv_raw[:, q, :], io["w_kv_up"][q]).then_inc(ukv_loaded, 16)
            for m in range(2):
                pool.wait_ge(t_ready, POST_MEM + m + 1)
                pool.dma_start(rows(km_s if m == 0 else vm_s), T[:, 0:2, :]).then_inc(t_stored, 16)
            for t in range(TT):
                pool.wait_ge(u_ms, t + 1)
                g.tensor_tensor(rr[:, 0:12], ss[:, 0:12], mhalf[:].to_broadcast([P, 12]), ALU.pow).then_inc(u_rr, 1)
            pool.wait_ge(u_up, TT)
            pool.wait_ge(u_done, TT)
            for i in range(NCHUNK // 2):
                wait(pool, A.gates_loaded, 16 * i)
                wait(pool, A.gated, 2 * i - 4)
                tok = slice(i * P, (i + 1) * P)
                pool.dma_start(mixed[:, 0:AJ, tok], gate_s[0:AJ, :, tok].rearrange("j p s -> p j s")
                               ).then_inc(A.gates_loaded, 16)
            for h in range(BH):
                wait(pool, B.gates_loaded, 16 * h)
                pool.wait_ge(A.gated, NCHUNK - 2 * (BH - h))
                pool.dma_start(mixed[:, AJ + h, :], gate_s[AJ + h]).then_inc(B.gates_loaded, 16)
            for i in range(TT // 2):
                wait(pool, M.gates_loaded, 16 * i)
                pool.wait_ge(B.gated, TT * (i + 1) - 1)
                tok = slice(2 * i * P, 2 * (i + 1) * P)
                pool.dma_start(mixed[:, AJ + BH:KT, tok], gate_s[AJ + BH:KT, :, tok].rearrange("j p s -> p j s")
                               ).then_inc(M.gates_loaded, 16)
            xr = io["x"].rearrange("(t p) n -> p t n", p=P)
            yr = io["y"].rearrange("(t p) n -> p t n", p=P)
            pool.wait_ge(M.gated, TT)
            for og in range(OUT_GROUPS + 2):
                if og >= 2:
                    buf = (S, T)[og % 2]
                    parts = 1 if og - 2 < OUT_GROUPS - 1 else 4
                    for part in range(parts):
                        a, b = TT * part // parts, TT * (part + 1) // parts
                        pool.wait_ge(acc_free, TT * (NTOK + og - 2) + b)
                        pool.dma_start(yr[:, a:b, (og - 2) * HALF:(og - 1) * HALF], buf[:, a:b, :]).then_inc(out_stored, 16)
                if og < OUT_GROUPS:
                    if og >= 2:
                        pool.wait_ge(out_stored, 16 * (og - 1))
                    buf = (S, T)[og % 2]
                    pool.dma_start(buf[:], xr[:, :, og * HALF:(og + 1) * HALF]).then_inc(res_loaded[og % 2], 16)
            pool.wait_ge(out_stored, 16 * (OUT_GROUPS + 3))

        def gate_sigmoid(act, a, group):
            act.wait_ge(acc_free, TT * (group + 1))
            act.wait_ge(t_stored, 16 * group)
            a.activation(T[:], S[:], ACT.Sigmoid).then_inc(t_square, 1)

        @block.scalar
        def _(act):
            a = nc.scalar
            act.dma_start(cols[:], io["cols"]).then_inc(g_loaded, 16)

            def high(n):
                act.wait_ge(w_loaded[n % RAW], 16 * (n // RAW + 1))
                wait(act, w_used, n - SPLIT + 1)
                a.activation(w_hi[:, n % SPLIT, :], w_raw[:, n % RAW, :], ACT.Copy).then_inc(hi_ready, 1)

            def bring_in(function):
                a.activation(nothing[:], ident[:, 0:1], function)

            act.wait_ge(pool_consts, 2)
            bring_in(ACT.Square)

            act.wait_ge(g_loaded, 16)
            for c in range(CPG):
                high(c)
                for k in X_TILES[c]:
                    act.wait_ge(x_loaded[k // 2] if k >= 2 else x0_loaded[k], 16)
                    a.activation(h_hi[:, k, :], x_raw[:, k, :], ACT.Copy, scale=g_x[:, k:k + 1]).then_inc(h_hi_ready, 1)
                    if k >= 4:
                        act.wait_ge(sq_used, k - 3)
                    sq = T[:, 2 * (k % 4):2 * (k % 4) + 2, :].rearrange("p a n -> p (a n)")
                    a.activation(sq, x_raw[:, k, :], ACT.Square).then_inc(sq_ready, 1)

            def evacuate(group):
                if group == 0:
                    act.wait_ge(col_ready, 1)
                wait(act, t_ready, group)
                for t in range(TT):
                    if t < TT - 1:
                        act.wait_ge(acc_done, (TT - 1) * group + t + 1)
                    else:
                        act.wait_ge(w_used, CPG * (group + 1))
                    a.activation(S[:, t, :], ps[:, t, :], ACT.Copy, scale=rs_col[:, t:t + 1]).then_inc(acc_free, 1)
                if group == 0:
                    act.wait_ge(sq_used, KT)
                else:
                    act.wait_ge(t_stored, 16 * group)
                act.wait_ge(acc_free, TT * (group + 1))
                a.activation(T[:], S[:], ACT.Square).then_inc(t_square, 1)

            for group in range(1, NTOK + 1):
                for c in range(CPG if group < NTOK else 1):
                    high(CPG * group + c)
                    if c == 0 and group - 1 < G_GATE0:
                        evacuate(group - 1)
                    if c == 1 and group == 1:
                        act.wait_ge(angles_ready, 1)
                        for tile in (sin, cos):
                            a.activation(tile[:], tile[:], ACT.Sin).then_inc(trig_ready, 1)
                    if c == 1 and group - 1 >= G_GATE0:
                        gate_sigmoid(act, a, group - 1)

            high(CH_MEM)
            gate_sigmoid(act, a, NTOK - 1)
            act.wait_ge(consts_loaded, 16 * N_CONSTS)
            act.wait_ge(h_quarter_used, 2)
            def memory_parts(q):
                act.wait_ge(mem_loaded[q], 16)
                part = slice(4 * q, 4 * q + 4)
                a.activation(m_sq[:, part, :], mem_raw[:, part, :], ACT.Square).then_inc(m_squared, 1)
                for k in range(4 * q, 4 * q + 4):
                    a.activation(m_hi[:, k, :], mem_raw[:, k, :], ACT.Copy, scale=g_mem[:, k:k + 1]
                                 ).then_inc(m_hi_ready, 1)

            for q in range(4):
                memory_parts(q)
            act.wait_ge(w_used, CH_KR + 1)
            a.activation(kr_a[:], ps[0:BR, 0:2, :].rearrange("p a n -> p (a n)"), ACT.Copy).then_inc(kr_raw, 1)
            for c in range(1, CPG):
                high(CH_MEM + c)
                if c == 3:
                    act.wait_ge(kr_nat, 1)
                    a.activation(kr_c[:], kr_b[:, :, 0, :], ACT.Square).then_inc(kr_sq, 1)

            def up_in(t):
                act.wait_ge(u_turned, t + 1)
                wait(act, u_up, t - 1)
                a.activation(c_hi[:, t % 2].rearrange("p k s -> p (k s)"),
                             ps[:, 0:2, :].rearrange("p a n -> p (a n)")[:, 0:768], ACT.Copy).then_inc(u_chi, 1)

            n = CH_MEM + CPG
            for k in range(n, n + 3):
                high(k)
            for m in range(2):
                if m == 0:
                    act.wait_ge(col_ready, 2)
                act.wait_ge(t_ready, NTOK + m)
                for t in range(2):
                    act.wait_ge(mem_done, m + 1) if t == 0 else act.wait_ge(w_used, CH_MEM + CPG * (m + 1))
                    a.activation(S[:, t, :], ps[:, MEM_BANKS[m][t], :], ACT.Copy, scale=ms_col[:, t:t + 1]
                                 ).then_inc(mem_free, 1)
                if m == 0:
                    act.wait_ge(mem_free, 2)
                    act.wait_ge(t_stored, 16 * NTOK)
                    a.activation(T[:, 0:2, :], S[:, 0:2, :], ACT.Square).then_inc(t_square, 1)
                    for k in range(n + 3, n + 6):
                        high(k)
                    act.wait_ge(kr_turned, 1)
                    act.wait_ge(zeroed, 2)
                    for g in range(2):
                        rows = slice(64 * g, 64 * g + 64)
                        a.activation(krT[rows, g, :], ps[rows, 3:5, :].rearrange("p a n -> p (a n)"), ACT.Copy).then_inc(kr_kept, 1)
                    act.wait_ge(uq_loaded, 32)
                    a.activation(uq_hi[:], uq_raw[:], ACT.Copy).then_inc(up_hi, 1)
                    high(n + 6)
                    act.wait_ge(ukv_loaded, 32)
                    a.activation(ukv_hi[:], ukv_raw[:], ACT.Copy).then_inc(up_hi, 1)
                    high(n + 7)
                    up_in(0)

            def up_out(t):
                if t == 0:
                    act.wait_ge(t_ready, NTOK)
                    act.wait_ge(t_stored, 16 * NTOK)
                act.wait_ge(u_up_q, t + 1)
                wait(act, u_done, t - 1)
                a.activation(u_out[:, t % 2, 0:768], ps[:, 2:4, :].rearrange("p a n -> p (a n)")[:, 256:1024], ACT.Copy
                             ).then_inc(u_q_out, 1)
                act.wait_ge(u_up, t + 1)
                a.activation(u_out[:, t % 2, 768:1280], ps[:, 4, :], ACT.Copy).then_inc(u_kv_out, 1)
                a.activation(vB[:, t, :], ps[:, 5, :], ACT.Copy).then_inc(u_kv_out, 1)

            def up_square(t):
                wait(act, u_kn, t - 1)
                act.wait_ge(u_q_out, t + 1)
                act.wait_ge(u_kv_out, 2 * (t + 1))
                a.activation(u_fin[:, t % 2], u_out[:, t % 2], ACT.Square).then_inc(u_sq, 1)

            def up_keep(t):
                act.wait_ge(u_qr, t + 1)
                a.activation(qrT[:, :, t * P:(t + 1) * P],
                             ps[:, 2 if t < TT - 1 else 1, 0:256].rearrange("p (h s) -> p h s", h=2), ACT.Copy
                             ).then_inc(u_qr_kept, 1)
                act.wait_ge(u_qn, t + 1)
                a.activation(qnT[:, :, t * P:(t + 1) * P], ps[:, 6, :].rearrange("p (h s) -> p h s", h=BH), ACT.Copy,
                             scale=g_qn).then_inc(u_qn_kept, 1)

            def keys_kept():
                act.wait_ge(kn_turned, 1)
                act.wait_ge(zeroed, 4)
                for g in range(AKV):
                    rows = slice(64 * g, 64 * g + 64)
                    a.activation(a_kT[rows, g, :], ps[rows, 0:2, :].rearrange("p a n -> p (a n)"), ACT.Copy
                                 ).then_inc(kn_kept, 1)

            def memory_keys_kept():
                act.wait_ge(km_turned, 1)
                a.activation(kmT[:].rearrange("p h s -> p (h s)"), ps[:, 0:2, :].rearrange("p a n -> p (a n)"), ACT.Copy
                             ).then_inc(km_kept, 1)

            banks = lambda a, b: ps[:, a:b, :].rearrange("p a n -> p (a n)")

            def turn_q(at_, c, par):
                act.wait_ge(at_.turned, c + 1)
                wait(act, at_.scored, c - 1)
                qT = a_qT if at_ is A else c_qT
                a.activation(qT[:, par].rearrange("p j s -> p (j s)"), ps[:, 0, :], ACT.Copy).then_inc(at_.qT, 1)

            def exponents(at_, c, par):
                act.wait_ge(at_.max, c + 1)
                wait(act, at_.p_turned, c - 1)
                if at_ is A:
                    a.activation(st[:, par, 4, :], st[:, par, 4, :], ACT.Exp, scale=SCALE_A)
                    for e in range(8):
                        ins = a.activation(a_p[:, par, e, :], ps[:, 2 + 2 * par + e // 4, e % 4 * P:(e % 4 + 1) * P],
                                           ACT.Exp, bias=st[:, par, 1, e:e + 1], scale=SCALE_A,
                                           accum_out=st[:, par, 2, e:e + 1])
                elif at_ is B:
                    width = (BSTEPS[c][1] + 1) * P
                    ins = a.activation(b_p[:, par, 0:width], banks(2 + 2 * par, 4 + 2 * par)[:, 0:width], ACT.Exp,
                                       bias=st[:, par, 1, 0:1], scale=SCALE_B, accum_out=st[:, par, 2, 0:1])
                else:
                    for h in range(MH):
                        ins = a.activation(c_p[:, par, h, :],
                                           ps[:, 2 + 2 * par + h // 2, h % 2 * NMEM:(h % 2 + 1) * NMEM], ACT.Exp,
                                           bias=st[:, par, 1, h:h + 1], scale=SCALE_M, accum_out=st[:, par, 2, h:h + 1])
                ins.then_inc(at_.exp, 1)

            def keep_pT(at_, c, par):
                act.wait_ge(at_.p_turned, c + 1)
                wait(act, at_.pv, c - 1)
                pT = {A: a_pT, B: b_pT, M: c_pT}[at_]
                width = (BSTEPS[c][1] + 1) * P if at_ is B else 2 * HALF
                a.activation(pT[:, par, 0:width], banks(6, 8)[:, 0:width], ACT.Copy).then_inc(at_.pT, 1)

            def tiles_of(at_, n, after=None, beside=None):
                def body(i):
                    for par in range(2):
                        c = i * 2 + par
                        if below(c + 1, n):
                            exponents(at_, c + 1, 1 - par)
                        elif after:
                            exponents(after, 0, 0)
                        if below(c + 3, n):
                            turn_q(at_, c + 3, 1 - par)
                        elif after is M:
                            turn_q(M, c + 3 - n, (c + 3 - n) % 2)
                        keep_pT(at_, c, par)
                        if beside:
                            beside(c)
                return body

            for step in range(TT + 3):
                if 1 <= step < TT:
                    up_in(step)
                if 0 <= step - 1 < TT:
                    up_out(step - 1)
                if step == TT + 2:
                    turn_q(A, 0, 0)
                    turn_q(A, 1, 1)
                if step >= 3:
                    up_keep(step - 3)
                if 0 <= step - 1 < TT:
                    up_square(step - 1)
                if step == TT:
                    keys_kept()
                if step == TT + 1:
                    memory_keys_kept()
                    bring_in(ACT.Exp)

            exponents(A, 0, 0)
            turn_q(A, 2, 0)
            pipelined(act, NCHUNK // 2, tiles_of(A, NCHUNK, after=B))

            for s in range(len(BSTEPS)):
                if s + 1 < len(BSTEPS):
                    exponents(B, s + 1, (s + 1) % 2)
                else:
                    exponents(M, 0, 0)
                k = s + 3 - len(BSTEPS)
                if k >= 0:
                    turn_q(M, k, k % 2)
                keep_pT(B, s, s % 2)

            def high_mixed(k):
                if k == AJ + BH:
                    act.wait_ge(M.gated, TT)
                a.activation(h_hi[:, k, :], mixed[:, k, :], ACT.Copy).then_inc(h_hi_ready, 1)

            def ahead(c):
                if isinstance(c, int) and TT - 4 <= c < TT - 1:
                    if c == TT - 4:
                        high(CH_OUT)
                    else:
                        high_mixed(c - TT + 3)

            pipelined(act, TT // 2, tiles_of(M, TT, beside=ahead))
            for c in range(1, CPG):
                for k in (2 * c, 2 * c + 1):
                    high_mixed(k)
                high(CH_OUT + c)
            for n in range(CH_OUT + CPG, NCH):
                high(n)

        @block.vector
        def _(dve):
            v = nc.vector
            steps = Steps(dve, dve_sem)

            def do(ins):
                steps.did(ins)
                steps.settle()

            def low(n):
                dve.wait_ge(hi_ready, n + 1)
                wait(dve, w_used, n - SPLIT + 1)
                v.tensor_tensor(w_lo[:, n % SPLIT, :], w_raw[:, n % RAW, :], w_hi[:, n % SPLIT, :].bitcast(F32),
                                ALU.subtract).then_inc(lo_ready, 1)

            dve.wait_ge(g_loaded, 16)
            do(v.memset(sumsq[:], 0.0))
            for c in range(CPG):
                low(c)
                for k in X_TILES[c]:
                    dve.wait_ge(sq_ready, k + 1)
                    dve.wait_ge(h_hi_ready, k + 1)
                    v.scalar_tensor_tensor(out=h_lo[:, k, :], in0=x_raw[:, k, :], scalar=g_x[:, k:k + 1],
                                           in1=h_hi[:, k, :].bitcast(F32), op0=ALU.mult, op1=ALU.subtract
                                           ).then_inc(h_lo_ready, 1)
                    sq = T[:, 2 * (k % 4):2 * (k % 4) + 2, :].rearrange("p a n -> p (a n)")
                    wait(dve, sq_used, k)
                    v.tensor_tensor(sumsq[:], sumsq[:], sq, ALU.add).then_inc(sq_used, 1)

            def angles():
                dve.wait_ge(consts_loaded, 16 * N_CONSTS)
                do(v.tensor_copy(pos[:], posi[:]))
                grid = [P, TT, 32]
                do(v.tensor_tensor(sin[:], pos[:].unsqueeze(2).to_broadcast(grid),
                                   invf.unsqueeze(1).to_broadcast(grid), ALU.mult))
                turns, rest = tab[:, 0], tab[:, 1]
                do(v.tensor_scalar(turns, sin[:], 1.0 / TWO_PI, None, ALU.mult))
                do(v.tensor_scalar(turns, turns, ROUND, None, ALU.add))
                do(v.tensor_scalar(turns, turns, ROUND, None, ALU.subtract))
                for part in TWO_PI_PARTS:
                    do(v.tensor_scalar(rest, turns, part, None, ALU.mult))
                    do(v.tensor_tensor(sin[:], sin[:], rest, ALU.subtract))
                do(v.tensor_scalar(cos[:], sin[:], TWO_PI / 4, None, ALU.add))
                do(v.tensor_scalar(rest, cos[:], PI_BELOW, TWO_PI, ALU.is_gt, ALU.mult))
                do(v.tensor_tensor(cos[:], cos[:], rest, ALU.subtract))
                do(v.tensor_scalar(cos[:], cos[:], PI_BELOW, -PI_BELOW, ALU.min, ALU.max))
                v.tensor_scalar(sin[:], sin[:], PI_BELOW, -PI_BELOW, ALU.min, ALU.max).then_inc(angles_ready, 1)

            def tables(gain):
                lo, hi = gain[:, 0:32], gain[:, 32:64]
                for k, (f, part) in enumerate(((cos, lo), (sin, hi), (cos, hi), (sin, lo))):
                    steps.did(v.tensor_tensor(tab[:, k], f[:], part.unsqueeze(1).to_broadcast([P, TT, 32]), ALU.mult))
                steps.settle()

            def rotary(src, dst, n, k, tmp):
                x1, x2 = src[:, :, :, 0:32], src[:, :, :, 32:64]
                d1, d2 = dst[:, :, :, 0:32], dst[:, :, :, 32:64]
                table = lambda i: tab[:, i].unsqueeze(2).to_broadcast([P, TT, n, 32])
                if k == 0:
                    do(v.tensor_tensor(tmp, x2, table(1), ALU.mult))
                elif k == 1:
                    do(v.tensor_tensor(d1, x1, table(0), ALU.mult))
                elif k == 2:
                    do(v.tensor_tensor(d1, d1, tmp, ALU.subtract))
                elif k == 3:
                    do(v.tensor_tensor(d2, x2, table(2), ALU.mult))
                elif k == 4:
                    do(v.tensor_tensor(tmp, x1, table(3), ALU.mult))
                else:
                    do(v.tensor_tensor(d2, d2, tmp, ALU.add))

            roots = [0]

            def mean_squares(pieces):
                for view, a, b, width in pieces:
                    steps.did(v.tensor_reduce(ss[:, a:b], view, X, ALU.add))
                steps.settle()
                for i, (view, a, b, width) in enumerate(pieces):
                    ins = v.tensor_scalar(ss[:, a:b], ss[:, a:b], 1.0 / width, EPS, ALU.mult, ALU.add)
                    if i + 1 < len(pieces):
                        steps.did(ins)
                        steps.settle()
                    else:
                        ins.then_inc(ms_ready, 1)
                roots[0] += 1

            def rooted():
                dve.wait_ge(rr_ready, roots[0])

            def wait_a_chunk():
                pass

            def post(group):
                out = []
                if group == G_KV:
                    out.append(angles)
                    heads = lambda a: a[:, :, 0:128].rearrange("p t (h d) -> p t h d", h=AKV)
                    split = lambda a: a.rearrange("p (t h) -> p t h", t=TT)

                    def squares():
                        dve.wait_ge(t_square, 1)
                        mean_squares([(heads(T), 0, 16, AD), (T[:, :, 256:512], 16, 24, BKVR)])

                    out.append(squares)
                    out.append(rooted)
                    out.append(lambda: do(v.tensor_tensor(heads(S), heads(S), split(rr[:, 0:16]).unsqueeze(3)
                                                          .to_broadcast([P, TT, AKV, AD]), ALU.mult)))
                    out.append(lambda: do(v.tensor_tensor(S[:, :, 256:512], S[:, :, 256:512], rr[:, 16:24].unsqueeze(2)
                                                          .to_broadcast([P, TT, BKVR]), ALU.mult)))
                    out.append(lambda: (dve.wait_ge(trig_ready, 2), tables(g_ak)))
                    tmp = T[:, :, 256:256 + 64].rearrange("p t (h d) -> p t h d", h=AKV)
                    for k in range(6):
                        out.append(lambda k=k: rotary(heads(S), heads(T), AKV, k, tmp))
                    out.append(lambda: do(v.tensor_copy(T[:, :, 128:256], S[:, :, 128:256])))

                    def finish():
                        return (v.tensor_tensor(T[:, :, 256:512], S[:, :, 256:512],
                                           g_ckv.unsqueeze(1).to_broadcast([P, TT, BKVR]), ALU.mult))
                elif group in (G_AQ0, G_AQ1):
                    heads = lambda a: a.rearrange("p t (h d) -> p t h d", h=8)
                    flat = lambda a: a.rearrange("p t (h d) -> p (t h) d", h=8)

                    def squares():
                        dve.wait_ge(t_square, group + 1)
                        mean_squares([(flat(T[:]), 0, 64, AD)])

                    out.append(squares)
                    out.append(wait_a_chunk)
                    out.append(rooted)
                    out.append(lambda: do(v.tensor_tensor(flat(S[:]), flat(S[:]), rr[:].unsqueeze(2).to_broadcast([P, 64, AD]),
                                                          ALU.mult)))
                    out.append(lambda: tables(g_aq))
                    x1, x2 = heads(S[:])[:, :, :, 0:32], heads(S[:])[:, :, :, 32:64]
                    d1, d2 = heads(T[:])[:, :, :, 0:32], heads(T[:])[:, :, :, 32:64]
                    table = lambda i: tab[:, i].unsqueeze(2).to_broadcast([P, TT, 8, 32])
                    out.append(lambda: do(v.tensor_tensor(d2, x2, table(1), ALU.mult)))
                    out.append(lambda: do(v.tensor_tensor(d1, x1, table(0), ALU.mult)))
                    out.append(lambda: do(v.tensor_tensor(d1, d1, d2, ALU.subtract)))
                    out.append(lambda: do(v.tensor_tensor(d2, x2, table(2), ALU.mult)))
                    out.append(lambda: do(v.tensor_tensor(x1, x1, table(3), ALU.mult)))

                    def finish():
                        return (v.tensor_tensor(d2, d2, x1, ALU.add))
                elif group in (G_CQ, G_MQ):
                    n, width, gain = (TT, BQR, g_cq) if group == G_CQ else (4 * TT, MD, g_mq)
                    flat = lambda a: a.rearrange("p t (h d) -> p (t h) d", d=width)

                    def squares():
                        dve.wait_ge(t_square, group + 1)
                        mean_squares([(flat(T[:]), 0, n, width)])

                    out.append(squares)
                    out.append(wait_a_chunk)
                    out.append(rooted)
                    out.append(lambda: do(v.tensor_tensor(flat(S[:]), flat(S[:]), rr[:, 0:n].unsqueeze(2)
                                                          .to_broadcast([P, n, width]), ALU.mult)))

                    def finish():
                        return (v.tensor_tensor(flat(T[:]), flat(S[:]), gain[:].unsqueeze(1).to_broadcast([P, n, width]),
                                           ALU.mult))
                else:
                    out += [wait_a_chunk, wait_a_chunk, lambda: dve.wait_ge(t_square, group + 1)]

                    def finish():
                        return (v.tensor_tensor(T[:], T[:], S[:], ALU.mult))

                out.append(lambda: (finish().then_inc(t_ready, 1), dve.wait_ge(t_ready, group + 1)))
                return out

            def gate_out(group):
                if group == G_GATE0:
                    dve.wait_ge(rs_row_loaded, 16)
                dve.wait_ge(t_ready, group)
                for b in range(8):
                    if b < 7:
                        dve.wait_ge(acc_done, 7 * group + b + 1)
                    else:
                        dve.wait_ge(w_used, CPG * (group + 1))
                    half = b % 2
                    v.tensor_tensor(S[:, b, :], ps[:, b, :], rs_row[:, half * HALF:(half + 1) * HALF], ALU.mult
                                    ).then_inc(acc_free, 1)
                dve.wait_ge(acc_free, 8 * (group + 1))

            for group in range(1, NTOK + 1):
                todo = post(group - 1)
                if group == NTOK:
                    low(CPG * group)
                    gate_out(group - 1)
                    break
                for c in range(CPG):
                    low(CPG * group + c)
                    if c == 0 and group - 1 >= G_GATE0:
                        gate_out(group - 1)
                    if c >= 1:
                        for step in todo[2 * c - 2:2 * c]:
                            step()
                assert len(todo) <= 2 * (CPG - 1)

            def memory_parts(q):
                for k in range(4 * q, 4 * q + 4):
                    dve.wait_ge(m_hi_ready, k + 1)
                    v.scalar_tensor_tensor(out=m_lo[:, k, :], in0=mem_raw[:, k, :], scalar=g_mem[:, k:k + 1],
                                           in1=m_hi[:, k, :].bitcast(F32), op0=ALU.mult, op1=ALU.subtract
                                           ).then_inc(m_lo_ready, 1)
                dve.wait_ge(m_squared, q + 1)
                steps.did(v.tensor_reduce(m_parts[:, q, :], m_sq[:, 4 * q:4 * q + 4, :].rearrange("p k s -> p s k"), X,
                                          ALU.add))

            low(CH_MEM)
            for step in todo:
                step()
            for q in range(4):
                memory_parts(q)
            steps.settle()
            v.tensor_reduce(m_sums[:], m_parts[:].rearrange("p q s -> p s q"), X, ALU.add).then_inc(sum_ready, 1)
            for c in range(1, CPG):
                low(CH_MEM + c)
                if c == 2:
                    dve.wait_ge(kr_back, 1)
                    v.tensor_tensor(kr_b[:, :, 0, :], ps[:, 2, :].rearrange("p (t d) -> p t d", t=TT),
                                    rs_col[:].unsqueeze(2).to_broadcast([P, TT, BR]), ALU.mult).then_inc(kr_nat, 1)
                    tables(g_kr)
                if c == 3:
                    dve.wait_ge(kr_sq, 1)
                    mean_squares([(kr_c[:], 0, 8, BR)])
                if c == 5:
                    rooted()
                    do(v.tensor_tensor(kr_b[:, :, 0, :], kr_b[:, :, 0, :],
                                       rr[:, 0:8].unsqueeze(2).to_broadcast([P, TT, BR]), ALU.mult))
                if c in (6, 7):
                    for k in range(3 * c - 18, 3 * c - 15):
                        rotary(kr_b[:], kr_d[:, :, 0:1, :], 1, k, kr_t[:])
            n = CH_MEM + CPG
            low(n)
            v.tensor_copy(kr_d[:, :, 1:2, :], kr_d[:, :, 0:1, :]).then_inc(kr_norm, 1)
            low(n + 1)
            for g in range(2):
                rows = slice(64 - 64 * g, 128 - 64 * g)
                v.memset(krT[rows, g, :], 0.0).then_inc(zeroed, 1)

            def up_in(t):
                dve.wait_ge(u_chi, t + 1)
                v.tensor_tensor(c_lo[:, t % 2].rearrange("p k s -> p (k s)"),
                                ps[:, 0:2, :].rearrange("p a n -> p (a n)")[:, 0:768],
                                c_hi[:, t % 2].rearrange("p k s -> p (k s)").bitcast(F32), ALU.subtract
                                ).then_inc(u_clo, 1)

            low(n + 2)
            low(n + 3)
            heads = lambda a: a[:, 0:2, :].rearrange("p t (h d) -> p (t h) d", d=MD)
            dve.wait_ge(t_square, NTOK + 1)
            mean_squares([(heads(T), 0, 8, MD)])
            low(n + 4)
            rooted()
            do(v.tensor_tensor(heads(S), heads(S), rr[:, 0:8].unsqueeze(2).to_broadcast([P, 8, MD]), ALU.mult))
            v.tensor_tensor(heads(T), heads(S), g_mk.unsqueeze(1).to_broadcast([P, 8, MD]), ALU.mult
                            ).then_inc(t_ready, 1)
            low(n + 5)
            low(n + 6)
            dve.wait_ge(up_hi, 1)
            v.tensor_tensor(uq_lo[:], uq_raw[:], uq_hi[:].bitcast(F32), ALU.subtract).then_inc(up_lo, 1)
            low(n + 7)
            up_in(0)
            dve.wait_ge(up_hi, 2)
            v.tensor_tensor(ukv_lo[:], ukv_raw[:], ukv_hi[:].bitcast(F32), ALU.subtract).then_inc(up_lo, 1)
            dve.wait_ge(mem_free, 4)
            dve.wait_ge(t_stored, 16 * (NTOK + 1))
            v.tensor_copy(T[:, 0:2, :], S[:, 0:2, :]).then_inc(t_ready, 1)

            tables(g_qr)

            def up_squares(t):
                rope, nope = u_fin[:, t % 2, 0:256], u_fin[:, t % 2, 256:1280]
                dve.wait_ge(u_sq, t + 1)
                wait(dve, u_rr, t)
                steps.did(v.tensor_reduce(ss[:, 0:8], nope.rearrange("p (h d) -> p h d", d=BN), X, ALU.add))
                steps.did(v.tensor_reduce(ss[:, 8:12], rope.rearrange("p (h d) -> p h d", d=BR), X, ALU.add))
                steps.settle()
                steps.did(v.tensor_scalar(ss[:, 0:8], ss[:, 0:8], 1.0 / BN, EPS, ALU.mult, ALU.add))
                steps.settle()
                v.tensor_scalar(ss[:, 8:12], ss[:, 8:12], 1.0 / BR, EPS, ALU.mult, ALU.add).then_inc(u_ms, 1)

            def up_norm(t):
                nope = lambda a: a[:, t % 2, 256:1280].rearrange("p (h d) -> p h d", d=BN)
                rope = lambda a: a[:, t % 2, 0:256].rearrange("p (h d) -> p h d", d=BR)
                dve.wait_ge(u_rr, t + 1)
                steps.did(v.tensor_tensor(rope(u_out), rope(u_out), rr[:, 8:12].unsqueeze(2).to_broadcast([P, 4, BR]),
                                          ALU.mult))
                steps.did(v.tensor_tensor(nope(u_fin), nope(u_out), rr[:, 0:8].unsqueeze(2).to_broadcast([P, 8, BN]),
                                          ALU.mult))
                steps.settle()
                x1, x2 = rope(u_out)[:, :, 0:32], rope(u_out)[:, :, 32:64]
                d1, d2 = rope(u_fin)[:, :, 0:32], rope(u_fin)[:, :, 32:64]
                table = lambda i: tab[:, i, t, :].unsqueeze(1).to_broadcast([P, BH, 32])
                steps.did(v.tensor_tensor(d1, x1, table(0), ALU.mult))
                steps.did(v.tensor_tensor(u_tmp[:, 0], x2, table(1), ALU.mult))
                steps.did(v.tensor_tensor(d2, x2, table(2), ALU.mult))
                steps.did(v.tensor_tensor(u_tmp[:, 1], x1, table(3), ALU.mult))
                steps.settle()
                steps.did(v.tensor_tensor(d1, d1, u_tmp[:, 0], ALU.subtract))
                v.tensor_tensor(d2, d2, u_tmp[:, 1], ALU.add).then_inc(u_done, 1)

            def up_keep(t):
                dve.wait_ge(u_kn, t + 1)
                v.tensor_scalar(knT[:, :, t * P:(t + 1) * P], ps[:, 7, :].rearrange("p (h s) -> p h s", h=BH),
                                g_kn, None, ALU.mult).then_inc(u_kn_kept, 1)

            do(v.tensor_scalar(sinks[:], sinks[:], 1.0 / SCALE_A, None, ALU.mult))

            def maximum(at_, c, par, first=False):
                dve.wait_ge(at_.scored, c + 1)
                if at_ is A:
                    ins = a_maxima(par, first)
                elif at_ is B:
                    ins = b_max(c)
                else:
                    ins = m_maxima(par)
                ins.then_inc(at_.max, 1)

            def normalise(at_, c, par):
                dve.wait_ge(at_.exp, c + 1)
                ins = a_normal(par) if at_ is A else b_normal(c) if at_ is B else m_normal(par)
                ins.then_inc(at_.p, 1)

            def gate(at_, c, par, pair):
                dve.wait_ge(at_.pv, c + 1)
                dve.wait_ge(at_.gates_loaded, pair * 16 + 16)
                if at_ is B:
                    h, t = BSTEPS[c]
                    to, out = mixed[:, AJ + h, t * P:(t + 1) * P], ps[:, 1, 0:P]
                elif at_ is A:
                    to, out = mixed[:, 0:AJ, bass.ds(c * CHUNK, CHUNK)], ps[:, 1, :].rearrange("p (j s) -> p j s", j=AJ)
                else:
                    to, out = mixed[:, AJ + BH:KT, bass.ds(c * P, P)], ps[:, 1, :].rearrange("p (j s) -> p j s", j=MH)
                v.tensor_tensor(to, out, to, ALU.mult).then_inc(at_.gated, 1)

            def tiles_of(at_, n, before=None, after=None, beside=None):
                def body(i):
                    for par in range(2):
                        c = i * 2 + par
                        normalise(at_, c, par)
                        if below(c + 2, n):
                            maximum(at_, c + 2, par)
                        elif after:
                            maximum(after, c + 2 - n, par)
                        if isinstance(c, int) and c == 0:
                            if before:
                                gate(*before)
                        else:
                            gate(at_, c - 1, 1 - par, i if par else i - 1)
                        if beside:
                            beside(c)
                return body

            def a_maxima(par, first=False):
                sc = ps[:, 2 + 2 * par:4 + 2 * par, :].rearrange("p a (g k) -> p (a g) k", k=P)
                if first:
                    do(v.memset(sc[:, :, CHUNK:P], -BIG))
                do(v.tensor_reduce(st[:, par, 0, :], sc, X, ALU.max))
                do(v.tensor_tensor(st[:, par, 0, :], st[:, par, 0, :], sinks[:], ALU.max))
                steps.did(v.tensor_tensor(st[:, par, 4, :], sinks[:], st[:, par, 0, :], ALU.subtract))
                return v.tensor_scalar(st[:, par, 1, :], st[:, par, 0, :], -SCALE_A, None, ALU.mult)

            def a_normal(par):
                do(v.tensor_tensor(st[:, par, 2, :], st[:, par, 2, :], st[:, par, 4, :], ALU.add))
                do(v.reciprocal(st[:, par, 3, :], st[:, par, 2, :]))
                return v.tensor_tensor(a_p[:, par], a_p[:, par], st[:, par, 3, :].unsqueeze(2).to_broadcast([P, 8, P]),
                                       ALU.mult)

            def b_max(s):
                h, t = BSTEPS[s]
                width, par = (t + 1) * P, s % 2
                sc = ps[:, 2 + 2 * par:4 + 2 * par, :].rearrange("p a n -> p (a n)")
                do(v.memset(sc[0:CHUNK, width - CHUNK:width], -BIG))
                do(v.tensor_reduce(st[:, par, 0, 0:1], sc[:, 0:width], X, ALU.max))
                return v.tensor_scalar(st[:, par, 1, 0:1], st[:, par, 0, 0:1], -SCALE_B, None, ALU.mult)

            def b_normal(s):
                h, t = BSTEPS[s]
                width, par = (t + 1) * P, s % 2
                do(v.reciprocal(st[:, par, 3, 0:1], st[:, par, 2, 0:1]))
                return v.tensor_scalar(b_p[:, par, 0:width], b_p[:, par, 0:width], st[:, par, 3, 0:1], None, ALU.mult)

            def m_maxima(par):
                sc = ps[:, 2 + 2 * par:4 + 2 * par, :].rearrange("p a (g k) -> p (a g) k", k=NMEM)
                do(v.tensor_reduce(st[:, par, 0, 0:MH], sc, X, ALU.max))
                return v.tensor_scalar(st[:, par, 1, 0:MH], st[:, par, 0, 0:MH], -SCALE_M, None, ALU.mult)

            def m_normal(par):
                do(v.reciprocal(st[:, par, 3, 0:MH], st[:, par, 2, 0:MH]))
                return v.tensor_tensor(c_p[:, par], c_p[:, par], st[:, par, 3, 0:MH].unsqueeze(2)
                                       .to_broadcast([P, MH, NMEM]), ALU.mult)

            for step in range(TT + 3):
                if 0 <= step - 1 < TT:
                    up_squares(step - 1)
                if step == TT + 2:
                    maximum(A, 0, 0, first=True)
                    maximum(A, 1, 1)
                if step >= 3:
                    up_keep(step - 3)
                if step + 1 < TT:
                    up_in(step + 1)
                if step == 0:
                    dve.wait_ge(w_used, CH_OUT)
                    for g in range(AKV):
                        rows = slice(64 - 64 * g, 128 - 64 * g)
                        v.memset(a_kT[rows, g, :], 0.0).then_inc(zeroed, 1)
                if 0 <= step - 1 < TT:
                    up_norm(step - 1)

            pipelined(dve, NCHUNK // 2, tiles_of(A, NCHUNK, after=B), [steps])

            for s in range(len(BSTEPS)):
                normalise(B, s, s % 2)
                k = s + 2 - len(BSTEPS)
                if k < 0:
                    maximum(B, s + 2, s % 2)
                else:
                    maximum(M, k, k)
                if s == 0:
                    gate(A, NCHUNK - 1, 1, NCHUNK // 2 - 1)
                else:
                    gate(B, s - 1, (s - 1) % 2, BSTEPS[s - 1][0])

            def low_mixed(k):
                dve.wait_ge(h_hi_ready, KT + k + 1)
                v.tensor_tensor(h_lo[:, k, :], mixed[:, k, :], h_hi[:, k, :].bitcast(F32), ALU.subtract
                                ).then_inc(h_lo_ready, 1)

            def ahead(c):
                if isinstance(c, int) and c >= TT - 3:
                    if c == TT - 3:
                        low(CH_OUT)
                    else:
                        low_mixed(c - TT + 2)

            last_b = (B, len(BSTEPS) - 1, 1, BH - 1)
            pipelined(dve, TT // 2, tiles_of(M, TT, before=last_b, beside=ahead), [steps])
            gate(M, TT - 1, 1, TT // 2 - 1)

            def add_residual(og):
                buf = (S, T)[og % 2]
                dve.wait_ge(res_loaded[og % 2], 16 * (og // 2 + 1))
                for t in range(TT):
                    if t < TT - 1:
                        dve.wait_ge(acc_done, (TT - 1) * (NTOK + og) + t + 1)
                    else:
                        dve.wait_ge(w_used, CH_OUT + CPG * (og + 1))
                    v.tensor_tensor(buf[:, t, :], ps[:, t, :], buf[:, t, :], ALU.add).then_inc(acc_free, 1)

            for c in range(1, CPG):
                for k in (2 * c, 2 * c + 1):
                    low_mixed(k)
                low(CH_OUT + c)
            for n in range(CH_OUT + CPG, NCH):
                low(n)
                if (n - CH_OUT) % CPG == 0:
                    add_residual((n - CH_OUT) // CPG - 1)
            add_residual(OUT_GROUPS - 1)

        @block.tensor
        def _(pe):
            mm = nc.tensor.matmul

            def three(out, a_hi, a_lo, b_hi, b_lo, start, stop):
                mm(out, a_hi, b_hi, start=start, stop=False)
                mm(out, a_hi, b_lo, start=False, stop=False)
                return mm(out, a_lo, b_hi, start=False, stop=stop)

            def token_group(g, n0, tok_parts=None, gates=False, slot0=0):
                for c in range(CPG):
                    slot, n = (slot0 + c) % SPLIT, n0 + c
                    pe.wait_ge(lo_ready, n + 1)
                    for kk in range(2):
                        k = 2 * c + kk
                        if tok_parts is not None:
                            pe.wait_ge(h_lo_ready, tok_parts + k + 1)
                        for b in range(8):
                            if k == 0:
                                wait(pe, acc_free, g * 8 + (b - 7))
                            w = slice(kk * HALF, (kk + 1) * HALF)
                            if gates:
                                ct, half = b // 2, b % 2
                                col = slice(kk * HALF + ct * P, kk * HALF + (ct + 1) * P)
                                tok = slice(half * HALF, (half + 1) * HALF)
                                ins = three(ps[:, b, :], w_hi[:, slot, col], w_lo[:, slot, col],
                                            h_hi[:, k, tok], h_lo[:, k, tok], k == 0, k == KT - 1)
                            else:
                                tok = slice(b * P, (b + 1) * P)
                                ins = three(ps[:, b, :], h_hi[:, k, tok], h_lo[:, k, tok],
                                            w_hi[:, slot, w], w_lo[:, slot, w], k == 0, k == KT - 1)
                            if k == KT - 1 and b < 7:
                                ins.then_inc(acc_done, 1)
                    ins.then_inc(w_used, 1)

            token_group(0, 0, tok_parts=0)
            with pe.Fori(1, G_GATE0) as g:
                token_group(g, g * CPG)
            with pe.Fori(G_GATE0, NTOK) as g:
                token_group(g, g * CPG, gates=True)

            pe.wait_ge(lo_ready, CH_KR + 1)
            slot = CH_KR % SPLIT
            pe.wait_ge(acc_free, 8 * (NTOK - 1) + 2)
            for k in range(KT):
                w = slice(k * BR, (k + 1) * BR)
                for half in range(2):
                    tok = slice(half * HALF, (half + 1) * HALF)
                    ins = three(ps[0:BR, half, :], w_hi[:, slot, w], w_lo[:, slot, w], h_hi[:, k, tok], h_lo[:, k, tok],
                                k == 0, k == KT - 1)
                if k in (KT // 4 - 1, KT // 2 - 1):
                    ins.then_inc(h_quarter_used, 1)
            ins.then_inc(w_used, 1)
            turn = nc.tensor.transpose

            def up_in(t):
                pe.wait_ge(u_loaded[t % 2], 32 * (t // 2 + 1))
                wait(pe, u_clo, t)
                for k in range(6):
                    ins = turn(ps[:, k // 4, k % 4 * P:(k % 4 + 1) * P], u_in[:, t % 2, k * P:(k + 1) * P], ident[:])
                ins.then_inc(u_turned, 1)

            for m in range(2):
                for c in range(CPG):
                    n = CH_MEM + CPG * m + c
                    pe.wait_ge(lo_ready, n + 1)
                    for kk in range(2):
                        k = 2 * c + kk
                        if m == 0:
                            pe.wait_ge(m_lo_ready, k + 1)
                        for t in range(2):
                            if k == 0:
                                pe.wait_ge(acc_free, 8 * NTOK)
                                wait(pe, kr_nat, m)
                            tok, w = slice(t * P, (t + 1) * P), slice(kk * HALF, (kk + 1) * HALF)
                            ins = three(ps[:, MEM_BANKS[m][t], :], m_hi[:, k, tok], m_lo[:, k, tok], w_hi[:, n % SPLIT, w],
                                        w_lo[:, n % SPLIT, w], k == 0, k == KT - 1)
                            if k == KT - 1 and t == 0:
                                ins.then_inc(mem_done, 1)
                    ins.then_inc(w_used, 1)
                    if (m, c) == (0, 1):
                        pe.wait_ge(pool_consts, 1)
                        pe.wait_ge(kr_raw, 1)
                        for t in range(TT):
                            ins = turn(ps[:, 2, t * BR:(t + 1) * BR], kr_a[:, t * P:(t + 1) * P], ident[0:BR, 0:BR])
                        ins.then_inc(kr_back, 1)
                    if (m, c) == (1, 6):
                        up_in(0)
                    if (m, c) == (1, 3):
                        pe.wait_ge(kr_norm, 1)
                        for t in range(TT):
                            ins = turn(ps[:, 3 + t // 4, t % 4 * P:(t % 4 + 1) * P],
                                       kr_d[:, t].rearrange("p a d -> p (a d)"), ident[:])
                        ins.then_inc(kr_turned, 1)

            def up(t):
                hi, lo = c_hi[:, t % 2], c_lo[:, t % 2]
                pe.wait_ge(u_clo, t + 1)
                if t == 0:
                    pe.wait_ge(kr_kept, 2)
                    pe.wait_ge(up_lo, 2)
                    pe.wait_ge(mem_free, 4)
                wait(pe, u_q_out, t)
                wait(pe, u_qr_kept, t - 2)
                for k in range(4):
                    for out, a, b in ((ps[:, 3, :], 0, 512), (ps[:, 2, 256:512], 512, 768)):
                        ins = three(out, hi[:, k, :], lo[:, k, :], uq_hi[:, k, a:b], uq_lo[:, k, a:b], k == 0, k == 3)
                ins.then_inc(u_up_q, 1)
                wait(pe, u_kv_out, 2 * t)
                for k in range(2):
                    for bank, a, b in ((4, 0, 512), (5, 512, 1024)):
                        ins = three(ps[:, bank, :], hi[:, 4 + k, :], lo[:, 4 + k, :], ukv_hi[:, k, a:b],
                                    ukv_lo[:, k, a:b], k == 0, k == 1)
                ins.then_inc(u_up, 1)

            def up_back(t):
                rotary_bank = 2 if t < TT - 1 else 1
                fin = u_fin[:, t % 2]
                pe.wait_ge(u_done, t + 1)
                wait(pe, u_qr_kept, t)
                wait(pe, u_q_out, min(t + 3, TT))
                for h in range(2):
                    ins = turn(ps[:, rotary_bank, h * P:(h + 1) * P], fin[:, h * P:(h + 1) * P], ident[:])
                ins.then_inc(u_qr, 1)
                wait(pe, u_qn_kept, t)
                for h in range(BH):
                    ins = turn(ps[:, 6, h * P:(h + 1) * P], fin[:, 256 + h * P:256 + (h + 1) * P], ident[:])
                ins.then_inc(u_qn, 1)
                wait(pe, u_kn_kept, t)
                for h in range(BH):
                    ins = turn(ps[:, 7, h * P:(h + 1) * P], fin[:, 768 + h * P:768 + (h + 1) * P], ident[:])
                ins.then_inc(u_kn, 1)

            def turn_q(at_, par):
                q, n = (a_q, CHUNK) if at_ is A else (c_q, P)
                for j in range(HALF // n):
                    ins = turn(ps[:, 0, j * n:(j + 1) * n], q[:, par, j * P:(j + 1) * P], ident[0:n, 0:n])
                ins.then_inc(at_.turned, 1)

            def queries_ready(at_, c, par, pair):
                pe.wait_ge(at_.q_loaded[par], pair * 16 + 16)
                wait(pe, at_.qT, c)

            def scores_ready(at_, c):
                if at_ is not B:
                    pe.wait_ge(at_.qT, c + 1)
                wait(pe, at_.exp, c - 1)

            def score(at_, c, par):
                bank = 2 + 2 * par
                if at_ is A:
                    row = max(c - 1, 0) if isinstance(c, int) else c - 1
                    for jp in range(AJ // 2):
                        ins = mm(ps[:, bank + jp // 2, jp % 2 * 2 * P:(jp % 2 + 1) * 2 * P]
                                 .rearrange("p (g k) -> p g k", g=AKV),
                                 a_qT[:, par, 2 * jp:2 * jp + 2, :].rearrange("p j s -> p (j s)"),
                                 a_kT[:, :, bass.ds(row * CHUNK, P)], start=True, stop=True)
                elif at_ is B:
                    h, t = BSTEPS[c]
                    q, width = slice(t * P, (t + 1) * P), (t + 1) * P
                    for a in range(0, width, HALF):
                        b = min(width, a + HALF)
                        out = ps[:, bank + a // HALF, 0:b - a]
                        mm(out, qnT[:, h, q], knT[:, h, a:b], start=True, stop=False)
                        ins = mm(out, qrT[:, h // 2, q], krT[:, h % 2, a:b], start=False, stop=True)
                else:
                    for h in range(MH):
                        ins = mm(ps[:, bank + h // 2, h % 2 * NMEM:(h % 2 + 1) * NMEM], c_qT[:, par, h, :], kmT[:, h, :],
                                 start=True, stop=True)
                ins.then_inc(at_.scored, 1)

            def turn_p(at_, c, par):
                pe.wait_ge(at_.p, c + 1)
                wait(pe, at_.pT, c)
                to = lambda k: ps[:, 6 + k // 4, k % 4 * P:(k % 4 + 1) * P]
                if at_ is A:
                    for g in range(AKV):
                        for jp in range(AJ // 2):
                            ins = turn(to(4 * g + jp), a_p[:, par, 2 * jp + g, :], ident[:])
                elif at_ is B:
                    for k in range(BSTEPS[c][1] + 1):
                        ins = turn(to(k), b_p[:, par, k * P:(k + 1) * P], ident[:])
                else:
                    for kb in range(2):
                        for h in range(MH):
                            ins = turn(to(4 * kb + h), c_p[:, par, h, kb * P:(kb + 1) * P], ident[:])
                ins.then_inc(at_.p_turned, 1)

            def value(at_, c, par, pair):
                pe.wait_ge(at_.pT, c + 1)
                wait(pe, at_.gated, c)
                if at_ is A:
                    pe.wait_ge(a_v_loaded[par], pair * 16 + 16)
                    for g in range(AKV):
                        ins = mm(ps[64 * g:64 * g + 64, 1, :], a_v[:, par, 64 * g:64 * g + 64],
                                 a_pT[:, par, g * HALF:(g + 1) * HALF], start=True, stop=True)
                elif at_ is B:
                    h, t = BSTEPS[c]
                    for k in range(t + 1):
                        ins = mm(ps[:, 1, 0:P], vB[:, k, h * BV:(h + 1) * BV], b_pT[:, par, k * P:(k + 1) * P],
                                 start=(k == 0), stop=(k == t))
                else:
                    for h in range(MH):
                        for kb in range(2):
                            k = kb * HALF + h * P
                            ins = mm(ps[:, 1, h * P:(h + 1) * P], vM[:, kb, h * MD:(h + 1) * MD], c_pT[:, par, k:k + P],
                                     start=(kb == 0), stop=(kb == 1))
                ins.then_inc(at_.pv, 1)

            def begin(at_, last, n_last, k):
                if k >= 1:
                    pe.wait_ge(last.exp, n_last - 2 + k)
                    scores_ready(at_, k - 1)
                    score(at_, k - 1, k - 1)
                if at_ is not B:
                    queries_ready(at_, k, k % 2, k // 2)
                    turn_q(at_, k % 2)

            def tiles_of(at_, n, before=None, after=None):
                def body(i):
                    for par in range(2):
                        c = i * 2 + par
                        if below(c + 2, n):
                            scores_ready(at_, c + 2)
                            if below(c + 3, n):
                                queries_ready(at_, c + 3, 1 - par, i + 1 + par)
                            score(at_, c + 2, par)
                            if below(c + 3, n):
                                turn_q(at_, 1 - par)
                        elif after:
                            begin(after, at_, n, c + 3 - n)
                        if isinstance(c, int) and c == 0:
                            if before:
                                value(*before)
                        else:
                            if isinstance(c, int) and c == 1 and before:
                                pe.wait_ge(before[0].gated, before[1] + 1)
                            value(at_, c - 1, 1 - par, i if par else i - 1)
                        turn_p(at_, c, par)
                return body

            for step in range(TT + 3):
                if 1 <= step < TT:
                    up_in(step)
                if 0 <= step - 1 < TT:
                    up(step - 1)
                if step == TT + 2:
                    pe.wait_ge(km_kept, 1)
                    pe.wait_ge(u_q_out, TT)
                    pe.wait_ge(u_kv_out, 2 * TT)
                    pe.wait_ge(u_qr_kept, TT - 1)
                    for c in range(2):
                        queries_ready(A, c, c, 0)
                        turn_q(A, c)
                        scores_ready(A, c)
                        score(A, c, c)
                if step >= 3:
                    up_back(step - 3)
                if step == TT:
                    pe.wait_ge(kn_loaded, 16)
                    pe.wait_ge(u_clo, TT)
                    for t in range(TT):
                        ins = turn(ps[:, t // 4, t % 4 * P:(t % 4 + 1) * P], a_kn[:, t, :], ident[:])
                    ins.then_inc(kn_turned, 1)
                if step == TT + 1:
                    pe.wait_ge(km_loaded, 16)
                    pe.wait_ge(kn_kept, 2)
                    for h in range(MH):
                        for t in range(2):
                            k = 2 * h + t
                            ins = turn(ps[:, k // 4, k % 4 * P:(k % 4 + 1) * P], c_km[:, t, h * P:(h + 1) * P], ident[:])
                    ins.then_inc(km_turned, 1)

            pe.wait_ge(u_qn_kept, TT)
            pe.wait_ge(u_kn_kept, TT)
            queries_ready(A, 2, 0, 1)
            turn_q(A, 0)
            pipelined(pe, NCHUNK // 2, tiles_of(A, NCHUNK, after=B))

            for s in range(len(BSTEPS)):
                if s + 2 < len(BSTEPS):
                    scores_ready(B, s + 2)
                    score(B, s + 2, s % 2)
                k = s + 3 - len(BSTEPS)
                if k >= 0:
                    if k == 0:
                        pe.wait_ge(vm_loaded, 16)
                    begin(M, B, len(BSTEPS), k)
                if s == 0:
                    value(A, NCHUNK - 1, 1, NCHUNK // 2 - 1)
                else:
                    if s == 1:
                        pe.wait_ge(A.gated, NCHUNK)
                    value(B, s - 1, (s - 1) % 2, None)
                turn_p(B, s, s % 2)

            last_b = (B, len(BSTEPS) - 1, 1, None)
            pipelined(pe, TT // 2, tiles_of(M, TT, before=last_b))
            value(M, TT - 1, 1, TT // 2 - 1)

            pe.wait_ge(M.gated, TT)
            token_group(NTOK, CH_OUT, tok_parts=KT, slot0=CH_OUT % SPLIT)
            with pe.Fori(1, OUT_GROUPS) as og:
                token_group(og + NTOK, og * CPG + CH_OUT, slot0=CH_OUT % SPLIT)


def kernel(x, mem, positions, g_in, w_in, a_g_q, a_g_k, a_sinks, b_g_cq, b_w_q_up, b_g_ckv, b_w_kv_up, b_g_q_nope,
           b_g_q_rope, b_g_k_nope, b_g_k_rope, m_g_mem, m_w_kv, m_g_q, m_g_k, w_o):
    import concourse.bacc as bacc
    from concourse.bass_utils import run_bass_kernel_spmd

    f = lambda a: np.ascontiguousarray(np.asarray(a))
    tiles = lambda a: a.reshape(-1, P, a.shape[-1])
    x0, mem0 = f(x)[0], f(mem)[0]
    w = f(w_in)[0]
    cuts = np.cumsum([AH * AD, AKV * AD, AKV * AD, AH * AD, BQR, BKVR, BR, BH * BV, MH * MD, MH * MD])
    aq, ak, av, ag, cq, ckv, kr, bg, mq, mg = np.split(w, cuts[:-1], axis=1)
    paired = lambda a: a.reshape(a.shape[0], AKV, AJ, AD).transpose(0, 2, 1, 3).reshape(a.shape[0], -1)
    wo = f(w_o)[0]
    wo = np.concatenate([paired(wo[:AH * AD].T).T, wo[AH * AD:]], 0)

    def chunks(a):
        a = a.reshape(CPG, 2, P, -1, HALF)
        return a.transpose(3, 0, 2, 1, 4).reshape(-1, P, 2 * HALF)

    front = np.concatenate([ak, av, ckv, cq, paired(aq), mq, paired(ag), bg, mg], 1)
    stream = np.concatenate([
        chunks(front),
        kr.reshape(KT, P, BR).transpose(1, 0, 2).reshape(1, P, KT * BR),
        chunks(f(m_w_kv)[0]),
        chunks(wo),
    ], 0)
    assert stream.shape[0] == NCH
    q_up = f(b_w_q_up)[0].reshape(BQR, BH, BN + BR)
    q_up = np.concatenate([q_up[:, :, :BN].reshape(BQR, -1), q_up[:, :, BN:].reshape(BQR, -1)], 1)
    kv_up = f(b_w_kv_up)[0].reshape(BKVR, BH, BN + BV)
    kv_up = np.concatenate([kv_up[:, :, :BN].reshape(BKVR, -1), kv_up[:, :, BN:].reshape(BKVR, -1)], 1)
    arrays = {
        "w": stream, "xT": tiles(x0.T), "memT": tiles(mem0.T), "x": x0,
        "w_q_up": tiles(q_up), "w_kv_up": tiles(kv_up),
        "positions": f(positions)[0].reshape(TT, P).T.astype(np.int32),
        "sinks": f(a_sinks)[0].reshape(AKV, AJ // 2, 2).transpose(2, 1, 0).reshape(2, AJ),
        "cols": np.concatenate([f(g_in)[0].reshape(KT, P).T, f(m_g_mem)[0].reshape(KT, P).T, f(b_g_q_nope).T,
                                f(b_g_k_nope).T], 1),
        "rows": np.concatenate([f(a_g_q), f(a_g_k), f(b_g_cq), f(b_g_ckv), f(b_g_q_rope), f(b_g_k_rope), f(m_g_q),
                                f(m_g_k), (10000.0 ** (-np.arange(0, AD, 2, dtype=np.float64) / AD)
                                           ).astype(np.float32)[None]], 1),
    }
    nc = bacc.Bacc("TRN2", target_bir_lowering=False, num_devices=1)
    sent, io = {}, {}
    for name, a in arrays.items():
        a = np.ascontiguousarray(a)
        sent[f"in_{name}"] = a
        io[name] = nc.dram_tensor(f"in_{name}", a.shape, mybir.dt.from_np(a.dtype), kind="ExternalInput").ap()
    io["y"] = nc.dram_tensor("out_y", (SEQ, D), F32, kind="ExternalOutput").ap()
    layer(nc, io)
    r = run_bass_kernel_spmd(nc, [sent], core_ids=[0])
    return r.results[0]["out_y"].reshape(1, SEQ, D)
```
